# Optimizing a Trainium2 kernel written in Bass

```python
import math
import jax, jax.numpy as jnp
from jax import lax
import numpy as np

D_MODEL = 1024
BATCH = 1
SEQ = 1024
DEPTH = 1

D_MIX = D_MODEL
S5_WIDTH = D_MIX // 2
S5_GROUP = 16
S5_GROUPS = S5_WIDTH // S5_GROUP
S5_STATE = 64
S5_MAX_RE = -1e-4
DN_HEADS = 4
DN_HEAD_DIM = 128
DN_WIDTH = DN_HEADS * DN_HEAD_DIM
DN_CONV = 5
DN_CHUNK = 64
IN_COLS = S5_WIDTH + 4 * DN_WIDTH + 4 * DN_HEADS
N_EXPERT_GROUPS = 4
EXPERTS_PER_GROUP = 8
N_EXPERTS = N_EXPERT_GROUPS * EXPERTS_PER_GROUP
TOP_K = 2
D_EXPERT = 512
MOE_BLOCK = 128
NORM_EPS = 1e-6

kernel_name = 'hybrid_s5_gdn_hier_moe_encoder'

def _rmsnorm(x, w):
    xf = x.astype(jnp.float32)
    return xf * lax.rsqrt(jnp.mean(xf * xf, axis=-1, keepdims=True) + NORM_EPS) * w.astype(jnp.float32)

def _l2norm(x):
    return x * lax.rsqrt(jnp.sum(x * x, axis=-1, keepdims=True) + NORM_EPS)

def _ssm_combine(left, right):
    a_l, b_l = left
    a_r, b_r = right
    return a_r * a_l, a_r * b_l + b_r

def _s5_scan(u, lam_re, lam_im, log_dt, b_re, b_im, c_re, c_im, reverse):
    f32 = jnp.float32
    lam = lax.complex(jnp.minimum(lam_re.astype(f32), S5_MAX_RE), lam_im.astype(f32))
    dt = jnp.exp(log_dt.astype(f32))[:, None]
    lam_bar = jnp.exp(lam * dt)
    b_bar = ((lam_bar - 1.0) / lam)[:, :, None] * lax.complex(b_re.astype(f32), b_im.astype(f32))
    bu = jnp.einsum('blgp,gnp->blgn', u.astype(jnp.complex64), b_bar)
    a = jnp.broadcast_to(lam_bar, bu.shape)
    _, state = lax.associative_scan(_ssm_combine, (a, bu), reverse=reverse, axis=1)
    c = lax.complex(c_re.astype(f32), c_im.astype(f32))
    return jnp.real(jnp.einsum('blgn,gpn->blgp', state, c))

def _s5_mixer(u, lam_re, lam_im, log_dt, b_re, b_im, c_re, c_im, d, w_glu, b_glu):
    bsz, seq, _ = u.shape
    u = u.astype(jnp.float32)
    ug = u.reshape(bsz, seq, S5_GROUPS, S5_GROUP)
    y_f = _s5_scan(ug, lam_re[0], lam_im[0], log_dt[0], b_re[0], b_im[0], c_re[0], c_im[0], False)
    y_b = _s5_scan(ug, lam_re[1], lam_im[1], log_dt[1], b_re[1], b_im[1], c_re[1], c_im[1], True)
    y = (y_f + y_b).reshape(bsz, seq, S5_WIDTH) + d * u
    y = jax.nn.gelu(y, approximate=False)
    return y * jax.nn.sigmoid(y @ w_glu + b_glu)

def _centred_dwconv(x, w):
    ch = x.shape[-1]
    pad = DN_CONV // 2
    return lax.conv_general_dilated(x, w[:, None, :], window_strides=(1,), padding=((pad, pad),),
                                    dimension_numbers=('NWC', 'WIO', 'NWC'), feature_group_count=ch)

def _gated_delta_chunked(q, k, v, g, beta):
    bsz, nh, seq, dk = q.shape
    dv = v.shape[-1]
    n_chunks = seq // DN_CHUNK
    q, k, v = [t.reshape(bsz, nh, n_chunks, DN_CHUNK, -1) for t in (q, k, v)]
    g = jnp.cumsum(g.reshape(bsz, nh, n_chunks, DN_CHUNK), axis=-1)
    beta = beta.reshape(bsz, nh, n_chunks, DN_CHUNK)
    tril = jnp.tril(jnp.ones((DN_CHUNK, DN_CHUNK), bool))
    strict = jnp.tril(jnp.ones((DN_CHUNK, DN_CHUNK), bool), -1)
    diff = g[..., :, None] - g[..., None, :]
    decay = jnp.where(tril, jnp.exp(jnp.where(tril, diff, 0.0)), 0.0)
    kb = k * beta[..., None]
    a_mat = jnp.where(strict, jnp.einsum('bhnid,bhnjd->bhnij', kb, k) * decay, 0.0)
    sys = jnp.eye(DN_CHUNK, dtype=q.dtype) + a_mat
    rhs = jnp.concatenate([v * beta[..., None], kb * jnp.exp(g)[..., None]], axis=-1)
    sol = lax.linalg.triangular_solve(sys, rhs, left_side=True, lower=True, unit_diagonal=True)
    u_c, w_c = sol[..., :dv], sol[..., dv:]
    attn = jnp.where(tril, jnp.einsum('bhnid,bhnjd->bhnij', q, k) * decay, 0.0)
    g_last = g[..., -1]
    k_dec = k * jnp.exp(g_last[..., None] - g)[..., None]
    q_dec = q * jnp.exp(g)[..., None]

    def step(state, inp):
        q_i, k_i, u_i, w_i, attn_i, gl_i = inp
        v_new = u_i - jnp.einsum('bhck,bhkv->bhcv', w_i, state)
        o_i = jnp.einsum('bhck,bhkv->bhcv', q_i, state) + jnp.einsum('bhij,bhjv->bhiv', attn_i, v_new)
        state = state * jnp.exp(gl_i)[..., None, None] + jnp.einsum('bhck,bhcv->bhkv', k_i, v_new)
        return state, o_i

    xs = tuple(jnp.moveaxis(t, 2, 0) for t in (q_dec, k_dec, u_c, w_c, attn, g_last))
    s0 = jnp.zeros((bsz, nh, dk, dv), q.dtype)
    _, o = lax.scan(step, s0, xs)
    return jnp.moveaxis(o, 0, 2).reshape(bsz, nh, seq, dv)

def _gdn_mixer(qkv, z, a_raw, b_raw, conv_w, a_log, dt_bias, norm_w):
    f32 = jnp.float32
    bsz, seq, _ = qkv.shape
    qkv = jax.nn.silu(_centred_dwconv(qkv.astype(f32), conv_w.astype(f32)))
    q, k, v = jnp.split(qkv, 3, axis=-1)

    def heads(t):
        return t.reshape(bsz, seq, DN_HEADS, DN_HEAD_DIM).transpose(0, 2, 1, 3)

    q = _l2norm(heads(q)) * DN_HEAD_DIM ** -0.5
    k = _l2norm(heads(k))
    v = heads(v)
    g = -jnp.exp(a_log.astype(f32)) * jax.nn.softplus(a_raw.astype(f32) + dt_bias.astype(f32))
    beta = jax.nn.sigmoid(b_raw.astype(f32))
    g = g.transpose(0, 2, 3, 1)
    beta = beta.transpose(0, 2, 3, 1)

    def flip(t):
        return jnp.flip(t, axis=2)

    o_f = _gated_delta_chunked(q, k, v, g[:, 0], beta[:, 0])
    o_b = flip(_gated_delta_chunked(flip(q), flip(k), flip(v), flip(g[:, 1]), flip(beta[:, 1])))
    o = (o_f + o_b).transpose(0, 2, 1, 3)
    zh = z.astype(f32).reshape(bsz, seq, DN_HEADS, DN_HEAD_DIM)
    o = o * lax.rsqrt(jnp.mean(o * o, axis=-1, keepdims=True) + NORM_EPS) * norm_w.astype(f32) * jax.nn.silu(zh)
    return o.reshape(bsz, seq, DN_WIDTH)

def _hier_moe(h, w_rg, b_rg, w_re, b_re, w_gate, w_up, w_down):
    n_tok, d = h.shape
    g_logits = h @ w_rg + b_rg
    g_prob = jax.nn.softmax(g_logits.astype(jnp.float32), axis=-1)
    _, g_sel = lax.top_k(g_logits, 1)
    p_group = jnp.take_along_axis(g_prob, g_sel, axis=-1)
    e_logits_all = jnp.einsum('td,gde->tge', h, w_re) + b_re
    e_logits = jnp.take_along_axis(e_logits_all, g_sel[:, :, None], axis=1)[:, 0]
    top_val, top_idx = lax.top_k(e_logits, TOP_K)
    gate = jax.nn.softmax(top_val.astype(jnp.float32), axis=-1) * p_group
    expert_idx = (g_sel * EXPERTS_PER_GROUP + top_idx).astype(jnp.int32)

    n_assign = n_tok * TOP_K
    n_blocks = -(-n_assign // MOE_BLOCK) + N_EXPERTS
    n_slots = n_blocks * MOE_BLOCK
    flat_e = expert_idx.reshape(-1)
    flat_tok = jnp.repeat(jnp.arange(n_tok, dtype=jnp.int32), TOP_K)
    flat_w = gate.reshape(-1)
    order = jnp.argsort(flat_e)
    e_sorted, tok_sorted, w_sorted = flat_e[order], flat_tok[order], flat_w[order]
    counts = jnp.bincount(flat_e, length=N_EXPERTS)
    padded = ((counts + MOE_BLOCK - 1) // MOE_BLOCK) * MOE_BLOCK
    pad_end = jnp.cumsum(padded)
    pad_start = pad_end - padded
    start = jnp.cumsum(counts) - counts
    dest = pad_start[e_sorted] + (jnp.arange(n_assign, dtype=jnp.int32) - start[e_sorted])
    slot_tok = jnp.zeros((n_slots,), jnp.int32).at[dest].set(tok_sorted)
    slot_w = jnp.zeros((n_slots,), jnp.float32).at[dest].set(w_sorted)
    block_start = jnp.arange(n_blocks, dtype=jnp.int32) * MOE_BLOCK
    block_expert = jnp.minimum(jnp.searchsorted(pad_end, block_start, side='right'), N_EXPERTS - 1)
    x_blocks = h[slot_tok].reshape(n_blocks, MOE_BLOCK, d)

    def expert_block(args):
        xb, e = args
        hid = jax.nn.silu(xb @ w_gate[e]) * (xb @ w_up[e])
        return hid @ w_down[e]

    y = lax.map(expert_block, (x_blocks, block_expert)).reshape(n_slots, d)
    return jnp.zeros((n_tok, d), y.dtype).at[slot_tok].add(y * slot_w[:, None])

def setup_inputs(seed: int = 0) -> dict:
    key = jax.random.key(seed)
    ks = jax.random.split(key, 32)
    f32 = jnp.float32

    def nrm(k, shape, s):
        return jax.random.normal(k, shape, f32) * s

    st = (DEPTH, 2, S5_GROUPS, S5_STATE)
    dt_gdn = jnp.exp(jax.random.uniform(ks[15], (DEPTH, 2, DN_HEADS), f32, math.log(1e-3), math.log(1e-1)))
    return {
        'x': nrm(ks[0], (BATCH, SEQ, D_MODEL), 1.0),
        'norm_mix': 1.0 + nrm(ks[1], (DEPTH, D_MODEL), 0.02),
        'w_in': nrm(ks[2], (DEPTH, D_MODEL, IN_COLS), D_MODEL ** -0.5),
        's5_lam_re': -0.5 + nrm(ks[3], st, 0.01),
        's5_lam_im': math.pi * jnp.arange(S5_STATE, dtype=f32) + nrm(ks[4], st, 0.01),
        's5_log_dt': jax.random.uniform(ks[5], (DEPTH, 2, S5_GROUPS), f32, math.log(1e-3), math.log(1e-1)),
        's5_b_re': nrm(ks[6], (DEPTH, 2, S5_GROUPS, S5_STATE, S5_GROUP), (2 * S5_GROUP) ** -0.5),
        's5_b_im': nrm(ks[7], (DEPTH, 2, S5_GROUPS, S5_STATE, S5_GROUP), (2 * S5_GROUP) ** -0.5),
        's5_c_re': nrm(ks[8], (DEPTH, 2, S5_GROUPS, S5_GROUP, S5_STATE), S5_STATE ** -0.5),
        's5_c_im': nrm(ks[9], (DEPTH, 2, S5_GROUPS, S5_GROUP, S5_STATE), S5_STATE ** -0.5),
        's5_d': nrm(ks[10], (DEPTH, S5_WIDTH), 1.0),
        's5_w_glu': nrm(ks[11], (DEPTH, S5_WIDTH, S5_WIDTH), S5_WIDTH ** -0.5),
        's5_b_glu': nrm(ks[12], (DEPTH, S5_WIDTH), 0.01),
        'gdn_conv_w': nrm(ks[13], (DEPTH, DN_CONV, 3 * DN_WIDTH), DN_CONV ** -0.5),
        'gdn_a_log': jnp.log(jax.random.uniform(ks[14], (DEPTH, 2, DN_HEADS), f32, 1.0, 16.0)),
        'gdn_dt_bias': dt_gdn + jnp.log(-jnp.expm1(-dt_gdn)),
        'gdn_norm_w': 1.0 + nrm(ks[16], (DEPTH, DN_HEAD_DIM), 0.02),
        'w_out': nrm(ks[17], (DEPTH, D_MIX, D_MODEL), D_MIX ** -0.5),
        'norm_ffn': 1.0 + nrm(ks[18], (DEPTH, D_MODEL), 0.02),
        'router_w_group': nrm(ks[19], (DEPTH, D_MODEL, N_EXPERT_GROUPS), D_MODEL ** -0.5),
        'router_b_group': nrm(ks[20], (DEPTH, N_EXPERT_GROUPS), 0.01),
        'router_w_expert': nrm(ks[21], (DEPTH, N_EXPERT_GROUPS, D_MODEL, EXPERTS_PER_GROUP), D_MODEL ** -0.5),
        'router_b_expert': nrm(ks[22], (DEPTH, N_EXPERT_GROUPS, EXPERTS_PER_GROUP), 0.01),
        'expert_w_gate': nrm(ks[23], (DEPTH, N_EXPERTS, D_MODEL, D_EXPERT), D_MODEL ** -0.5),
        'expert_w_up': nrm(ks[24], (DEPTH, N_EXPERTS, D_MODEL, D_EXPERT), D_MODEL ** -0.5),
        'expert_w_down': nrm(ks[25], (DEPTH, N_EXPERTS, D_EXPERT, D_MODEL), D_EXPERT ** -0.5),
        'norm_final': 1.0 + nrm(ks[26], (D_MODEL,), 0.02),
    }

def reference(x, norm_mix, w_in, s5_lam_re, s5_lam_im, s5_log_dt, s5_b_re, s5_b_im, s5_c_re, s5_c_im,
              s5_d, s5_w_glu, s5_b_glu, gdn_conv_w, gdn_a_log, gdn_dt_bias, gdn_norm_w, w_out, norm_ffn,
              router_w_group, router_b_group, router_w_expert, router_b_expert,
              expert_w_gate, expert_w_up, expert_w_down, norm_final):
    x = x.astype(jnp.float32)
    bsz, seq, d = x.shape
    cuts = [S5_WIDTH, S5_WIDTH + 3 * DN_WIDTH, S5_WIDTH + 4 * DN_WIDTH, S5_WIDTH + 4 * DN_WIDTH + 2 * DN_HEADS]
    for i in range(DEPTH):
        h = _rmsnorm(x, norm_mix[i])
        proj = h @ w_in[i]
        u_s5, qkv, z, a_raw, b_raw = jnp.split(proj, cuts, axis=-1)
        y_s5 = _s5_mixer(u_s5, s5_lam_re[i], s5_lam_im[i], s5_log_dt[i], s5_b_re[i], s5_b_im[i],
                         s5_c_re[i], s5_c_im[i], s5_d[i], s5_w_glu[i], s5_b_glu[i])
        y_dn = _gdn_mixer(qkv, z, a_raw.reshape(bsz, seq, 2, DN_HEADS), b_raw.reshape(bsz, seq, 2, DN_HEADS),
                          gdn_conv_w[i], gdn_a_log[i], gdn_dt_bias[i], gdn_norm_w[i])
        x = x + jnp.concatenate([y_s5, y_dn], axis=-1) @ w_out[i]
        h = _rmsnorm(x, norm_ffn[i]).reshape(bsz * seq, d)
        y = _hier_moe(h, router_w_group[i], router_b_group[i], router_w_expert[i], router_b_expert[i],
                      expert_w_gate[i], expert_w_up[i], expert_w_down[i])
        x = x + y.reshape(bsz, seq, d)
    return _rmsnorm(x, norm_final)


_drawn_inputs = setup_inputs


def setup_inputs(seed=0):
    import zlib

    import numpy as np

    out = dict(_drawn_inputs(seed))
    spreads = {}
    factors = {'s5_lam_re': 200.0,
     's5_b_glu': 50.311,
     'gdn_norm_w': 2.944,
     'router_b_group': 21.38,
     'router_b_expert': 12.147,
     'norm_final': 22.061,
     's5_lam_im': 38.912,
     's5_log_dt': 36.544,
     's5_b_re': 49.784,
     's5_b_im': 49.912,
     's5_c_re': 46.064,
     's5_c_im': 50.976,
     'norm_ffn': 3.438}
    for name, (base, spread) in spreads.items():
        noise = np.random.default_rng([zlib.crc32(name.encode()), seed]).standard_normal(out[name].shape)
        drawn = base * np.exp(spread * noise) if base else spread * noise
        out[name] = __import__('jax').numpy.asarray(drawn.astype(out[name].dtype))
    for name, factor in factors.items():
        out[name] = (out[name] * factor).astype(out[name].dtype)
    return out
```

```python
from contextlib import ExitStack
import math

import concourse.bass as bass
from concourse import mybir

F32 = mybir.dt.float32
I32 = mybir.dt.int32
U32 = mybir.dt.uint32
ALU = mybir.AluOpType
ACT = mybir.ActivationFunctionType
AX = mybir.AxisListType

P = 128
D = 1024
L = 1024
KT = D // P
TT = L // P
H = 4
DH = 128
DW = H * DH
S5W = 512
NG = 32
GC = 16
NS = 64
T5 = 8
NC5 = L // T5
NP5 = NG // 2
IN_COLS = 2576
EPS = 1e-6
NEXP = 32
NGRP = 4
EPG = 8
DE = 512
MAXB = L * 2 // P + NEXP - 1
TWO_PI = 2.0 * math.pi
MAGIC = 1.5 * 2.0 ** 23
BIG = 1.0e30


class Steps:

    def __init__(self, eng, sem):
        self.eng, self.sem, self.n = eng, sem, 0

    def __call__(self, ins):
        self.n += 1
        ins.then_inc(self.sem, 1)
        return self.n

    def done(self, n=None):
        self.eng.wait_ge(self.sem, self.n if n is None else n)


class Core:

    def __init__(self, nc, stack):
        self.nc, self.stack, self.sems = nc, stack, []
        stack.callback(self.release)

    def sb(self, name, shape, dt=F32, side="left"):
        return self.stack.enter_context(self.nc.sbuf_tensor(name, shape, dt, side=side))

    def ps(self, name, shape, dt=F32):
        return self.stack.enter_context(self.nc.psum_tensor(name, shape, dt))

    def sem(self, name):
        self.sems.append(self.nc.alloc_semaphore(name))
        return self.sems[-1]

    def release(self):
        if self.sems:
            self.nc.clear_and_free_semaphores(self.sems)
            self.nc.all_engine_barrier()


def constants(nc, core):
    c = {}
    c["ident"] = core.sb("ident", [P, P])
    c["ones"] = core.sb("ones", [P, P])
    c["upto"] = [core.sb("upto_f", [P, P]), core.sb("upto_b", [P, P])]
    c["level"] = [core.sb("level_f", [P, 7, P]), core.sb("level_b", [P, 7, P])]
    made = core.sem("const_made")
    with nc.Block() as block:
        @block.gpsimd
        def _(pool):
            step = Steps(pool, made)
            step(pool.memset(c["ones"][:], 1.0))
            step.done()
            one = c["ones"][:]
            step(pool.affine_select(out=c["ident"][:], in_=one, compare_op=ALU.is_equal, fill=0.0, base=0,
                                    pattern=[[1, P]], channel_multiplier=-1))
            step(pool.affine_select(out=c["upto"][0][:], in_=one, compare_op=ALU.is_ge, fill=0.0, base=0,
                                    pattern=[[1, P]], channel_multiplier=-1))
            step(pool.affine_select(out=c["upto"][1][:], in_=one, compare_op=ALU.is_ge, fill=0.0, base=0,
                                    pattern=[[-1, P]], channel_multiplier=1))
            for lv in range(7):
                s, n = 2 ** lv, P // 2 ** (lv + 1)
                for d in range(2):
                    v = c["level"][d][:, lv, :].rearrange("p (m a s) -> p m a s", m=n, a=2)
                    step(pool.memset(c["level"][d][:, lv, :], 0.0))
                    step.done()
                    half = v[:, :, d, :]
                    ones = one.rearrange("p (m a s) -> p m a s", m=n, a=2)[:, :, 0, :]
                    lo = s if d == 0 else 0
                    step(pool.affine_select(out=half, in_=ones, compare_op=ALU.is_ge, fill=0.0, base=-lo,
                                            pattern=[[-2 * s, n], [0, s]], channel_multiplier=1))
                    step.done()
                    step(pool.affine_select(out=half, in_=half, compare_op=ALU.is_ge, fill=0.0, base=lo + s - 1,
                                            pattern=[[2 * s, n], [0, s]], channel_multiplier=-1))
                    step.done()
    return c


def in_projection(nc, core, c, a, out):
    kv, zs, uT, qT, kT = (out[n] for n in ("kv", "zs", "uT", "qT", "kT"))
    hT = core.sb("hT", [P, KT, L])
    wblk = core.sb("wblk", [P, 2, KT, 512])
    wab = core.sb("wab", [P, KT, 16])
    work = core.sb("conv_work", [P, 2 * (L + 4) + 2 * L])
    convin = work[:, 0:2 * (L + 4)].rearrange("p (a n) -> p a n", a=2)
    acc = work[:, 2 * (L + 4):].rearrange("p (a n) -> p a n", a=2)
    uS = work[:, 0:NG * T5 * GC].rearrange("p (g n) -> p g n", g=NG)
    act_t = core.sb("conv_silu", [P, L])
    sq = core.sb("square", [P, D])
    xs = kv[:].rearrange("p (t a) n -> p t (a n)", a=2)
    q_rows = uT[:].rearrange("p (t a) n -> p t (a n)", a=4)
    rows = [q_rows, kv[:, 0:TT], kv[:, TT:2 * TT]]
    ss = core.sb("x_ss", [P, TT])
    ms = core.sb("x_ms", [P, TT])
    rs = core.sb("x_rs", [P, TT])
    nss = core.sb("qk_ss", [P, 2, H, TT])
    nrt = core.sb("qk_rt", [P, 2, H, TT])
    nrs = core.sb("qk_rs", [P, 2, H, TT])
    normw = core.sb("norm_mix_w", [P, KT])
    cw = core.sb("conv_w", [P, 5, 12])
    mm_ps = core.ps("proj_ps", [P, 2, 2, 512])
    tr_ps = core.ps("turn_ps", [P, 2, 2, 512])

    x_ld = [core.sem(f"x_ld{i}") for i in range(2)]
    par_ld = core.sem("par_ld")
    w_ld = [core.sem("w_ld0"), core.sem("w_ld1")]
    x_sq, x_ms, x_rt, x_h, x_tr, x_ev = (core.sem("x_" + n) for n in ("sq", "ms", "rt", "h", "tr", "ev"))
    dv = core.sem("proj_dve_step")
    pj = core.sem("projected")
    pj_ev = core.sem("projected_out")
    cv = core.sem("convolved")
    sl = core.sem("silu_done")
    tr = core.sem("tile_turned")
    tr_ev = core.sem("rows_out")
    sqd = core.sem("squared")
    red = core.sem("squares_summed")
    qk_ss, qk_rt = core.sem("qk_ss_done"), core.sem("qk_rt_done")
    nrm = core.sem("rows_normalised")
    qk_tr, qk_ev = core.sem("qk_turned"), core.sem("qk_out")
    x_rows = a["x"].rearrange("b (t p) d -> p (b t) d", p=P)
    w_in = a["w_in"][0].rearrange("(k p) n -> p k n", p=P)
    starts = [512, 1024, 1536, 0, 2048]
    NJ = 12

    with nc.Block() as block:
        @block.sync
        def _(sp):
            for i in range(2):
                sp.dma_start(xs[:, 4 * i:4 * i + 4], x_rows[:, 4 * i:4 * i + 4]).then_inc(x_ld[i], 16)
            with nc.allow_non_contiguous_dma(reason="small parameters"):
                sp.dma_start(normw[:], a["norm_mix"][0].rearrange("(k p) -> p k", p=P)).then_inc(par_ld, 16)
                for j in range(5):
                    sp.dma_start(cw[:, j, :], a["gdn_conv_w"][0, j].rearrange("(t p) -> p t", p=P)
                                 ).then_inc(par_ld, 16)
                sp.dma_start(wab[:], w_in[:, :, 2560:2576]).then_inc(par_ld, 16)
            for n in range(5):
                if n >= 2:
                    sp.wait_ge(pj, 4 * (n - 1))
                sp.dma_start(wblk[:, n % 2], w_in[:, :, starts[n]:starts[n] + 512]).then_inc(w_ld[n % 2], 16)

        @block.scalar
        def _(act):
            def silu(j):
                act.wait_ge(cv, j + 1)
                if j >= 1:
                    act.wait_ge(tr, j)
                act.activation(act_t[:], acc[:, j % 2, :], ACT.Silu).then_inc(sl, 1)

            def square(j):
                if j < 8:
                    act.wait_ge(tr_ev, j + 1)
                    if j >= 1:
                        act.wait_ge(red, j)
                    act.activation(sq[:].rearrange("p (t n) -> p t n", n=P),
                                   rows[j // 4][:, :, (j % 4) * P:(j % 4 + 1) * P], ACT.Square).then_inc(sqd, 1)

            for t in range(TT):
                act.wait_ge(x_ld[t // 4], 16)
                if t:
                    act.wait_ge(x_sq, t)
                act.activation(sq[:], xs[:, t, :], ACT.Square, accum_out=ss[:, t:t + 1]).then_inc(x_sq, 1)
            act.wait_ge(x_ms, 1)
            act.activation(rs[:], ms[:], ACT.Sqrt).then_inc(x_rt, 1)
            act.wait_ge(par_ld, 16 * 7)
            for n in range(2 * KT):
                half, k = n // KT, n % KT
                act.wait_ge(x_tr, n + 1)
                act.activation(hT[:, k, half * 512:half * 512 + 512], tr_ps[:, n % 2, 0, :], ACT.Copy,
                               scale=normw[:, k:k + 1]).then_inc(x_ev, 1)
            for j in range(NJ):
                act.wait_ge(pj, j + 1)
                if j < 2:
                    act.wait_ge(dv, 2)
                else:
                    act.wait_ge(cv, j - 1)
                act.activation(convin[:, j % 2, 2:2 + L], mm_ps[:, j % 2].rearrange("p a n -> p (a n)"),
                               ACT.Copy).then_inc(pj_ev, 1)
                if j >= 1:
                    silu(j - 1)
                if j >= 3:
                    square(j - 3)
            silu(NJ - 1)
            act.wait_ge(qk_ss, 1)
            act.activation(nrt[:], nss[:], ACT.Sqrt).then_inc(qk_rt, 1)
            act.wait_ge(sl, NJ)
            for t in range(T5):
                act.wait_ge(pj, NJ + t + 1)
                act.activation(uS[:, :, t * GC:(t + 1) * GC],
                               mm_ps[:, t % 2, 0, :].rearrange("p (g q) -> p g q", q=GC), ACT.Copy
                               ).then_inc(pj_ev, 1)
            for t in range(TT):
                act.wait_ge(pj, NJ + T5 + t + 1)
                act.activation(zs[:, t, :], mm_ps[:, t % 2, 0, :], ACT.Silu).then_inc(pj_ev, 1)
            act.wait_ge(pj, NJ + T5 + TT + 1)
            act.activation(out["ab"][:].rearrange("p t n -> p (t n)"), mm_ps[:, 0, 0, 0:TT * 16], ACT.Copy
                           ).then_inc(pj_ev, 1)
            for n in range(2 * TT):
                act.wait_ge(qk_tr, n + 1)
                dst = (qT, kT)[n % 2]
                act.activation(dst[:, :, (n // 2) * P:(n // 2 + 1) * P],
                               tr_ps[:, n % 2, 0, :].rearrange("p (h n) -> p h n", h=H), ACT.Copy
                               ).then_inc(qk_ev, 1)
            for m in range(NG // 4):
                n = 2 * TT + m
                act.wait_ge(qk_tr, n + 1)
                act.activation(uT[:, 4 * m:4 * m + 4, :],
                               tr_ps[:, n % 2, 0, :].rearrange("p (g n) -> p g n", g=4), ACT.Copy
                               ).then_inc(qk_ev, 1)

        @block.tensor
        def _(pe):
            for n in range(2 * KT):
                half, k = n // KT, n % KT
                pe.wait_ge(x_h, 4 * half + 4)
                if n >= 2:
                    pe.wait_ge(x_ev, n - 1)
                for t in range(4):
                    mm = pe.transpose(tr_ps[:, n % 2, 0, t * P:(t + 1) * P],
                                      xs[:, 4 * half + t, k * P:(k + 1) * P], c["ident"][:])
                mm.then_inc(x_tr, 1)
            pe.wait_ge(x_ev, 2 * KT)

            def turn(j):
                pe.wait_ge(sl, j + 1)
                if j >= 2:
                    pe.wait_ge(tr_ev, j - 1)
                for t in range(TT):
                    mm = pe.transpose(tr_ps[:, j % 2, t // 4, (t % 4) * P:(t % 4 + 1) * P],
                                      act_t[:, t * P:(t + 1) * P], c["ident"][:])
                mm.then_inc(tr, 1)

            for j in range(NJ):
                blk = j // 4
                if j % 4 == 0:
                    pe.wait_ge(w_ld[blk % 2], 16 * (blk // 2 + 1))
                if j >= 2:
                    pe.wait_ge(pj_ev, j - 1)
                for half in range(2):
                    for k in range(KT):
                        mm = pe.matmul(mm_ps[:, j % 2, half, :], wblk[:, blk % 2, k, (j % 4) * P:(j % 4 + 1) * P],
                                       hT[:, k, half * 512:half * 512 + 512], start=k == 0, stop=k == KT - 1)
                mm.then_inc(pj, 1)
                if j >= 1:
                    turn(j - 1)
            pe.wait_ge(w_ld[1], 32)
            for t in range(T5):
                pe.wait_ge(pj_ev, NJ + t - 1)
                for k in range(KT):
                    mm = pe.matmul(mm_ps[:, t % 2, 0, :], hT[:, k, t:L:T5], wblk[:, 1, k, :],
                                   start=k == 0, stop=k == KT - 1)
                mm.then_inc(pj, 1)
                if t == 0:
                    turn(NJ - 1)
            pe.wait_ge(w_ld[0], 48)
            for t in range(TT):
                pe.wait_ge(pj_ev, NJ + T5 + t - 1)
                for k in range(KT):
                    mm = pe.matmul(mm_ps[:, t % 2, 0, :], hT[:, k, t * P:(t + 1) * P], wblk[:, 0, k, :],
                                   start=k == 0, stop=k == KT - 1)
                mm.then_inc(pj, 1)
            pe.wait_ge(par_ld, 16 * 7)
            pe.wait_ge(pj_ev, NJ + T5 + TT)
            for t in range(TT):
                for k in range(KT):
                    mm = pe.matmul(mm_ps[:, 0, 0, t * 16:t * 16 + 16], hT[:, k, t * P:(t + 1) * P], wab[:, k, :],
                                   start=k == 0, stop=k == KT - 1)
            mm.then_inc(pj, 1)
            pe.wait_ge(tr_ev, NJ)
            for n in range(2 * TT):
                pe.wait_ge(nrm, n + 1)
                if n >= 2:
                    pe.wait_ge(qk_ev, n - 1)
                for h in range(H):
                    mm = pe.transpose(tr_ps[:, n % 2, 0, h * P:(h + 1) * P],
                                      rows[n % 2][:, n // 2, h * P:(h + 1) * P], c["ident"][:])
                mm.then_inc(qk_tr, 1)
            for g in range(NG):
                n = 2 * TT + g // 4
                if g % 4 == 0:
                    pe.wait_ge(qk_ev, n - 1)
                mm = pe.transpose(tr_ps[:, n % 2, 0, (g % 4) * P:(g % 4 + 1) * P], uS[:, g, :], c["ident"][:])
                if g % 4 == 3:
                    mm.then_inc(qk_tr, 1)

        @block.vector
        def _(dve):
            step = Steps(dve, dv)
            step(dve.memset(convin[:, :, 0:2], 0.0))
            step(dve.memset(convin[:, :, L + 2:L + 4], 0.0))
            dve.wait_ge(x_sq, TT)
            dve.tensor_scalar(ms[:], ss[:], 1.0 / D, EPS, ALU.mult, ALU.add).then_inc(x_ms, 1)
            dve.wait_ge(x_rt, 1)
            step(dve.reciprocal(ms[:], rs[:]))
            step.done()
            for t in range(TT):
                dve.tensor_scalar(xs[:, t, :], xs[:, t, :], ms[:, t:t + 1], None, ALU.mult).then_inc(x_h, 1)

            def rows_out(j):
                dve.wait_ge(tr, j + 1)
                if j == 0:
                    dve.wait_ge(x_tr, 2 * KT)
                dve.tensor_copy(rows[j // 4][:, :, (j % 4) * P:(j % 4 + 1) * P],
                                tr_ps[:, j % 2].rearrange("p a (t n) -> p (a t) n", n=P)).then_inc(tr_ev, 1)

            def sum_squares(j):
                if 0 <= j < 8:
                    dve.wait_ge(sqd, j + 1)
                    dve.tensor_reduce(nss[:, j // 4, j % 4, :], sq[:].rearrange("p (t n) -> p t n", n=P),
                                      AX.X, ALU.add).then_inc(red, 1)

            for j in range(NJ):
                dve.wait_ge(pj_ev, j + 1)
                if j >= 2:
                    dve.wait_ge(sl, j - 1)
                src = convin[:, j % 2, :]
                step(dve.tensor_scalar(acc[:, j % 2, :], src[:, 0:L], cw[:, 0, j:j + 1], None, ALU.mult))
                for tap in range(1, 5):
                    step.done()
                    ins = dve.scalar_tensor_tensor(out=acc[:, j % 2, :], in0=src[:, tap:tap + L],
                                                   scalar=cw[:, tap, j:j + 1], in1=acc[:, j % 2, :],
                                                   op0=ALU.mult, op1=ALU.add)
                    if tap < 4:
                        step(ins)
                ins.then_inc(cv, 1)
                if j >= 2:
                    rows_out(j - 2)
                    sum_squares(j - 3)
            rows_out(NJ - 2)
            dve.wait_ge(red, 8)
            dve.tensor_scalar(nss[:], nss[:], EPS, None, ALU.add).then_inc(qk_ss, 1)
            rows_out(NJ - 1)
            dve.wait_ge(qk_rt, 1)
            step(dve.reciprocal(nrs[:], nrt[:]))
            step.done()
            step(dve.tensor_scalar(nrs[:, 0], nrs[:, 0], DH ** -0.5, None, ALU.mult))
            step.done()
            dve.wait_ge(tr_ev, NJ)
            for n in range(2 * TT):
                t = n // 2
                view = rows[n % 2][:, t, :].rearrange("p (h d) -> p h d", h=H)
                scale = nrs[:, n % 2, :, t:t + 1].broadcast_to([P, H, DH])
                dve.tensor_tensor(view, view, scale, ALU.mult).then_inc(nrm, 1)


def persistent(low, core):
    return {
        "uT": low.sb("uT", [P, NG, NC5]),
        "qT": low.sb("qT", [P, H, L]),
        "kT": core.sb("kT", [P, H, L]),
        "kv": core.sb("kv_rows", [P, 2 * TT, DW]),
        "zs": core.sb("silu_z", [P, TT, DW]),
        "ab": core.sb("ab", [P, TT, 16]),
    }


def fill_expert_rows(sp, c, y_dram, filled):
    n = L * 2 // P
    rows = y_dram[n * P:, :].rearrange("(b p) (r c) -> p b r c", p=P, c=P)
    for b in range(rows.shape[1]):
        ones = c["ones"][:].rearrange("p (r c) -> p r c", r=1).broadcast_to([P, D // P, P])
        sp.dma_start(rows[:, b], ones).then_inc(filled, 16)


def gates(nc, core, c, a, out, tb, y_dram, filled):
    par = core.sb("gate_par", [P, 2, 8])
    t1 = core.sb("gate_t1", [P, TT, 8])
    t2 = core.sb("gate_t2", [P, TT, 8])
    t3 = core.sb("gate_t3", [P, TT, 8])
    g_ps = core.ps("gate_ps", [P, 2, 512])
    ld, v, s, m, mv = (core.sem("gate_" + n) for n in ("ld", "dve", "act", "pe", "out"))
    xa, xb = out["ab"][:, :, 0:8], out["ab"][:, :, 8:16]

    with nc.Block() as block:
        @block.sync
        def _(sp):
            for i, name in enumerate(("gdn_dt_bias", "gdn_a_log")):
                sp.dma_start(par[:, i, :], a[name].rearrange("o d h -> o (d h)").partition_broadcast(P)
                             ).then_inc(ld, 16)
            fill_expert_rows(sp, c, y_dram, filled)

        @block.vector
        def _(dve):
            step = Steps(dve, v)
            dve.wait_ge(ld, 32)
            bias = par[:, 0:1, :].broadcast_to([P, TT, 8])
            step(dve.tensor_tensor(t1[:], xa, bias, ALU.add))
            dve.wait_ge(s, 4)
            step(dve.tensor_scalar(t1[:], t1[:], 0.0, None, ALU.max))
            step.done()
            step(dve.tensor_tensor(t1[:], t1[:], t2[:], ALU.add))
            step.done()
            step(dve.scalar_tensor_tensor(out=tb["g"][:], in0=t1[:], scalar=-1.0,
                                          in1=par[:, 1:2, :].broadcast_to([P, TT, 8]),
                                          op0=ALU.mult, op1=ALU.mult))
            dve.wait_ge(m, 1)
            step(dve.tensor_copy(tb["G"][:, :, 0:4], g_ps[:, 0, 0:32].rearrange("p (t h) -> p t h", h=4)))
            step(dve.tensor_copy(tb["G"][:, :, 4:8], g_ps[:, 0, 32:64].rearrange("p (t h) -> p t h", h=4)))
            step(dve.tensor_copy(t2[:], g_ps[:, 0, 64:128].rearrange("p (t h) -> p t h", h=8)))
            step.done()
            step(dve.tensor_tensor(t3[:], t2[:], tb["G"][:], ALU.subtract))
            dve.wait_ge(s, 6)
            step(dve.tensor_tensor(tb["betaG"][:], tb["beta"][:], tb["eG"][:], ALU.mult))

        @block.scalar
        def _(act):
            act.wait_ge(v, 1)
            act.activation(t2[:], t1[:], ACT.Abs).then_inc(s, 1)
            act.wait_ge(s, 1)
            act.activation(t2[:], t2[:], ACT.Exp, scale=-1.0).then_inc(s, 1)
            act.wait_ge(s, 2)
            act.activation(t2[:], t2[:], ACT.Ln, bias=1.0).then_inc(s, 1)
            act.activation(par[:, 1, :], par[:, 1, :], ACT.Exp).then_inc(s, 1)
            act.activation(tb["beta"][:], xb, ACT.Sigmoid).then_inc(s, 1)
            act.wait_ge(v, 8)
            act.activation(tb["eG"][:], tb["G"][:], ACT.Exp).then_inc(s, 1)
            act.activation(tb["eTot"][:], t2[:], ACT.Exp)
            act.activation(tb["kdec"][:], t3[:], ACT.Exp).then_inc(s, 1)

        @block.tensor
        def _(pe):
            pe.wait_ge(v, 4)
            for d in range(2):
                pe.matmul(g_ps[:, 0, 32 * d:32 * d + 32], c["upto"][d][:], tb["g"][:, :, 4 * d:4 * d + 4],
                          start=True, stop=True)
            pe.matmul(g_ps[:, 0, 64:128], c["ones"][:], tb["g"][:].rearrange("p t h -> p (t h)"),
                      start=True, stop=True).then_inc(m, 1)


def gate_tables(core):
    return {n: core.sb("tab_" + n, [P, TT, 8]) for n in ("g", "G", "beta", "eG", "eTot", "kdec", "betaG")}


def delta_schedule():
    for t in range(TT + 1):
        steps = []
        if t < TT:
            steps += [("decay", 0), ("scores", 0), ("start", 0)]
            for lv in range(1, 7):
                steps += [("z", lv), ("d", lv)] + ([("turn", lv)] if lv < 6 else [])
            steps += [("solve", 0)]
        if t >= 1:
            a, b = (4, 7) if t < TT else (0, 0)
            steps.insert(a, ("read_state", -1))
            steps.insert(b + 1, ("new_state", -1))
        for name, lv in steps:
            for d in range(2):
                yield name, lv, (t - 1 if lv < 0 else t), d


def delta_net(nc, core, c, a, out, tb, o_sum):
    qT, kT, kv = out["qT"], out["kT"], out["kv"]

    def buf(name, n=1):
        return [core.sb(f"{name}{d}", [P, n, H, P]) for d in range(2)]

    e_b, ab_b, as_b, t_b, tt_b, z_b = buf("decay"), buf("amat"), buf("alev", 6), buf("T"), buf("TT"), buf("zc")
    at_b, u_b, w_b, kbg_b, kd_b = buf("attn", 2), buf("u"), buf("wT"), buf("kbg"), buf("kdec")
    vn_b, tmp_b, s_b, sd_b = buf("vnew"), buf("otmp"), buf("state"), buf("state_dec")
    X = [core.ps(f"bank_x{d}", [P, H, P]) for d in range(2)]
    Y = [core.ps(f"bank_y{d}", [P, H, P]) for d in range(2)]
    V = [core.ps(f"bank_v{d}", [P, H, P]) for d in range(2)]
    O = [core.ps(f"bank_o{d}", [P, H, P]) for d in range(2)]
    names = ("gsum kk kq diff absd decay masked betad amat attn alev t_first tt_first tt z zc dd turned t "
             "u_mm w_mm u w vb kbg kd ws qs vnew o_part av kv o o_added s_dec state tmp0").split()
    S = {n: [core.sem(f"dn_{n}{d}") for d in range(2)] for n in names}

    def chunk(t, d):
        return t if d == 0 else TT - 1 - t

    def cols(t, d):
        ch = chunk(t, d)
        return slice(ch * P, ch * P + P)

    def per_head(table, t, d):
        return table[:, chunk(t, d), 4 * d:4 * d + 4].rearrange("p (h o) -> p h o", o=1).broadcast_to([P, H, P])

    def rows(which, t, d):
        return kv[:, which * TT + chunk(t, d), :].rearrange("p (h n) -> p h n", h=H)

    def over_heads(m):
        return m.rearrange("p (o n) -> p o n", o=1).broadcast_to([P, H, P])

    with nc.Block() as block:
        @block.tensor
        def _(pe):
            def wait(name, d, n):
                if n > 0:
                    pe.wait_ge(S[name][d], n)

            def heads(dst, lhs, rhs):
                for h in range(H):
                    mm = pe.matmul(dst[:, h, :], lhs(h), rhs(h), start=True, stop=True)
                return mm

            for name, lv, t, d in delta_schedule():
                cs = cols(t, d)
                if name == "decay":
                    wait("u", d, t)
                    heads(X[d], lambda h: tb["g"][:, chunk(t, d), 4 * d + h:4 * d + h + 1].broadcast_to([P, P]),
                          lambda h: c["upto"][d][:]).then_inc(S["gsum"][d], 1)
                    wait("w", d, t)
                    heads(Y[d], lambda h: kT[:, h, cs], lambda h: kT[:, h, cs]).then_inc(S["kk"][d], 1)
                elif name == "scores":
                    wait("diff", d, t + 1)
                    heads(X[d], lambda h: kT[:, h, cs], lambda h: qT[:, h, cs]).then_inc(S["kq"][d], 1)
                elif name == "start":
                    wait("t_first", d, t + 1)
                    wait("amat", d, t + 1)
                    for h in range(H):
                        mm = pe.transpose(Y[d][:, h, :], t_b[d][:, 0, h, :], c["ident"][:])
                    mm.then_inc(S["tt_first"][d], 1)
                elif name == "z":
                    wait("alev", d, 6 * t + lv)
                    wait("tt", d, 7 * t + lv)
                    if lv == 1:
                        wait("attn", d, t + 1)
                    else:
                        wait("t", d, 5 * t + lv - 1)
                    heads(X[d], lambda h: as_b[d][:, lv - 1, h, :], lambda h: tt_b[d][:, 0, h, :]
                          ).then_inc(S["z"][d], 1)
                elif name == "d":
                    wait("zc", d, 6 * t + lv)
                    heads(Y[d], lambda h: t_b[d][:, 0, h, :], lambda h: z_b[d][:, 0, h, :]
                          ).then_inc(S["dd"][d], 1)
                elif name == "turn":
                    wait("tt", d, 7 * t + lv + 1)
                    for h in range(H):
                        mm = pe.transpose(X[d][:, h, :], tt_b[d][:, 0, h, :], c["ident"][:])
                    mm.then_inc(S["turned"][d], 1)
                elif name == "solve":
                    wait("tt", d, 7 * t + 7)
                    wait("vb", d, t + 1)
                    heads(X[d], lambda h: tt_b[d][:, 0, h, :], lambda h: e_b[d][:, 0, h, :]
                          ).then_inc(S["u_mm"][d], 1)
                    wait("kbg", d, t + 1)
                    heads(Y[d], lambda h: kbg_b[d][:, 0, h, :], lambda h: tt_b[d][:, 0, h, :]
                          ).then_inc(S["w_mm"][d], 1)
                elif name == "read_state":
                    wait("w", d, t + 1)
                    wait("state", d, t + 1)
                    wait("o", d, t)
                    heads(V[d], lambda h: w_b[d][:, 0, h, :], lambda h: s_b[d][:, 0, h, :]).then_inc(S["ws"][d], 1)
                    heads(O[d], lambda h: qT[:, h, cs], lambda h: s_b[d][:, 0, h, :]).then_inc(S["qs"][d], 1)
                elif name == "new_state":
                    wait("vnew", d, t + 1)
                    wait("attn", d, t + 1)
                    heads(V[d], lambda h: at_b[d][:, t % 2, h, :], lambda h: vn_b[d][:, 0, h, :]
                          ).then_inc(S["av"][d], 1)
                    wait("o_part", d, t + 1)
                    wait("kd", d, t + 1)
                    heads(O[d], lambda h: kd_b[d][:, 0, h, :], lambda h: vn_b[d][:, 0, h, :]
                          ).then_inc(S["kv"][d], 1)

        @block.vector
        def _(dve):
            def wait(name, d, n):
                if n > 0:
                    dve.wait_ge(S[name][d], n)

            for d in range(2):
                dve.memset(s_b[d][:], 0.0).then_inc(S["state"][d], 1)
            for name, lv, t, d in delta_schedule():
                ch = chunk(t, d)
                if name == "decay":
                    wait("gsum", d, t + 1)
                    wait("u_mm", d, t)
                    dve.tensor_tensor(e_b[d][:, 0], per_head(tb["G"], t, d), X[d][:], ALU.subtract
                                      ).then_inc(S["diff"][d], 1)
                elif name == "scores":
                    wait("kk", d, t + 1)
                    wait("betad", d, t + 1)
                    dve.tensor_tensor(ab_b[d][:, 0], Y[d][:], ab_b[d][:, 0], ALU.mult).then_inc(S["amat"][d], 1)
                    wait("kq", d, t + 1)
                    wait("masked", d, t + 1)
                    dve.tensor_tensor(at_b[d][:, t % 2], X[d][:], at_b[d][:, t % 2], ALU.mult
                                      ).then_inc(S["attn"][d], 1)
                elif name == "start":
                    wait("tt_first", d, t + 1)
                    dve.tensor_copy(tt_b[d][:, 0], Y[d][:]).then_inc(S["tt"][d], 1)
                elif name == "d":
                    wait("dd", d, 6 * t + lv)
                    wait("tt", d, 7 * t + lv)
                    dve.tensor_tensor(tt_b[d][:, 0], tt_b[d][:, 0], Y[d][:], ALU.subtract).then_inc(S["tt"][d], 1)
                elif name == "read_state":
                    wait("ws", d, t + 1)
                    wait("u", d, t + 1)
                    dve.tensor_tensor(vn_b[d][:, 0], u_b[d][:, 0], V[d][:], ALU.subtract).then_inc(S["vnew"][d], 1)
                    wait("qs", d, t + 1)
                    wait("o", d, t)
                    wait("o_added", d, t - 4)
                    dve.tensor_tensor(tmp_b[d][:, 0], O[d][:], per_head(tb["eG"], t, d), ALU.mult
                                      ).then_inc(S["o_part"][d], 1)
                elif name == "new_state":
                    wait("av", d, t + 1)
                    wait("o_part", d, t + 1)
                    dst = o_sum[:, ch, :].rearrange("p (h n) -> p h n", h=H) if t < TT // 2 else tmp_b[d][:, 0]
                    dve.tensor_tensor(dst, tmp_b[d][:, 0], V[d][:], ALU.add).then_inc(S["o"][d], 1)
                    wait("kv", d, t + 1)
                    wait("s_dec", d, t + 1)
                    dve.tensor_tensor(s_b[d][:, 0], sd_b[d][:, 0], O[d][:], ALU.add).then_inc(S["state"][d], 1)

        @block.scalar
        def _(act):
            def wait(name, d, n):
                if n > 0:
                    act.wait_ge(S[name][d], n)

            for name, lv, t, d in delta_schedule():
                if name == "decay":
                    wait("diff", d, t + 1)
                    act.activation(e_b[d][:, 0], e_b[d][:, 0], ACT.Abs).then_inc(S["absd"][d], 1)
                    wait("absd", d, t + 1)
                    act.activation(e_b[d][:, 0], e_b[d][:, 0], ACT.Exp, scale=-1.0).then_inc(S["decay"][d], 1)
                elif name == "z":
                    wait("z", d, 6 * t + lv)
                    act.activation(z_b[d][:, 0], X[d][:], ACT.Copy).then_inc(S["zc"][d], 1)
                elif name == "turn":
                    wait("turned", d, 5 * t + lv)
                    act.activation(t_b[d][:, 0], X[d][:], ACT.Copy).then_inc(S["t"][d], 1)
                elif name == "solve":
                    wait("u_mm", d, t + 1)
                    wait("vnew", d, t)
                    act.activation(u_b[d][:, 0], X[d][:], ACT.Copy).then_inc(S["u"][d], 1)
                    wait("w_mm", d, t + 1)
                    act.activation(w_b[d][:, 0], Y[d][:], ACT.Copy).then_inc(S["w"][d], 1)

        @block.gpsimd
        def _(pool):
            def wait(name, d, n):
                if n > 0:
                    pool.wait_ge(S[name][d], n)

            for name, lv, t, d in delta_schedule():
                ch = chunk(t, d)
                if name == "decay":
                    wait("decay", d, t + 1)
                    wait("av", d, t - 1)
                    pool.tensor_tensor(at_b[d][:, t % 2], e_b[d][:, 0], over_heads(c["upto"][d][:]), ALU.mult
                                       ).then_inc(S["masked"][d], 1)
                    wait("alev", d, 6 * t)
                    pool.tensor_tensor(ab_b[d][:, 0], e_b[d][:, 0], per_head(tb["beta"], t, d), ALU.mult
                                       ).then_inc(S["betad"][d], 1)
                elif name == "scores":
                    wait("amat", d, t + 1)
                    wait("dd", d, 6 * t)
                    pool.tensor_tensor(t_b[d][:, 0], ab_b[d][:, 0], over_heads(c["level"][d][:, 0, :]), ALU.mult
                                       ).then_inc(S["tmp0"][d], 1)
                    wait("tmp0", d, t + 1)
                    pool.tensor_tensor(t_b[d][:, 0], over_heads(c["ident"][:]), t_b[d][:, 0], ALU.subtract
                                       ).then_inc(S["t_first"][d], 1)
                    for lv in range(1, 7):
                        wait("z", d, 6 * t)
                        pool.tensor_tensor(as_b[d][:, lv - 1], ab_b[d][:, 0], over_heads(c["level"][d][:, lv, :]),
                                           ALU.mult).then_inc(S["alev"][d], 1)
                    wait("betad", d, t + 1)
                    pool.tensor_tensor(e_b[d][:, 0], rows(1, t, d), per_head(tb["beta"], t, d), ALU.mult
                                       ).then_inc(S["vb"][d], 1)
                    wait("w_mm", d, t)
                    pool.tensor_tensor(kbg_b[d][:, 0], rows(0, t, d), per_head(tb["betaG"], t, d), ALU.mult
                                       ).then_inc(S["kbg"][d], 1)
                elif name == "read_state":
                    wait("kv", d, t)
                    pool.tensor_tensor(kd_b[d][:, 0], rows(0, t, d), per_head(tb["kdec"], t, d), ALU.mult
                                       ).then_inc(S["kd"][d], 1)
                    wait("state", d, t + 1)
                    pool.tensor_tensor(sd_b[d][:, 0], s_b[d][:, 0], per_head(tb["eTot"], t, d), ALU.mult
                                       ).then_inc(S["s_dec"][d], 1)
                elif name == "new_state" and t >= TT // 2:
                    wait("o", d, t + 1)
                    wait("o", 1 - d, TT - t)
                    acc = o_sum[:, ch, :].rearrange("p (h n) -> p h n", h=H)
                    pool.tensor_tensor(acc, acc, tmp_b[d][:, 0], ALU.add).then_inc(S["o_added"][d], 1)


def s5_tables(core):
    return {
        "E": core.sb("s5_E", [P, 2 * NP5, 2, P]),
        "G": core.sb("s5_G", [P, 2, 2 * NP5, T5 + 1, GC]),
        "M": core.sb("s5_M", [P, NG, P]),
        "cos": core.sb("s5_cos", [P, 2 * NP5, NC5]),
        "sin": core.sb("s5_sin", [P, 2 * NP5, NC5]),
        "rho": core.sb("s5_rho", [P, 2 * NP5]),
    }


def s5_parameters(nc, core, c, a, tb):
    DJ = 2 * NP5
    raw = core.sb("s5_raw", [DJ, 3, P])
    ldt = core.sb("s5_ldt", [DJ, 2])
    lam = core.sb("s5_lam", [P, 3, DJ])
    BC = core.sb("s5_BC_in", [P, 2 * DJ * 2 * GC])
    B = BC[:, 0:2 * DJ * GC].rearrange("p (i j q) -> p i j q", i=2, j=DJ)
    Cn = BC[:, 2 * DJ * GC:].rearrange("p (i n) -> p i n", i=8)
    BD = BC[:].rearrange("p (i j q) -> p i j q", i=2, j=DJ)
    Bb = core.sb("s5_Bbar", [P, 2, DJ, GC])
    C = core.sb("s5_C", [P, 2, DJ, GC])
    s = core.sb("s5_small", [P, 20, DJ])
    pw = core.sb("s5_powers", [P, 2, T5 + 1, DJ])
    scr = core.sb("s5_scratch", [P, 6144])
    Dc = core.sb("s5_dcol", [2 * GC, NP5])
    dm = core.sb("s5_dmask", [2 * GC, GC])
    ramp = core.sb("s5_ramp", [P, NC5])
    ps = core.ps("s5_ps", [P, 4, 512])
    ld, v, g, acts, m, ev, mv, kd = (core.sem("s5p_" + n) for n in
                                     ("ld", "dve", "pool", "act", "pe", "out", "kcopy", "kmove"))
    (RE, IM, LD, DTC, AR, TH, TN, EM, EE, SN, SH, DR, DI, MM, T1, T2, QR, QI, TAU, HALF) = range(20)
    made = {n: core.sem("s5p_made_" + n) for n in ("ar", "theta", "turns", "E", "BD")}
    E, G = tb["E"], tb["G"]
    KKn = 2 * T5 - 1
    mv2 = core.sem("s5p_kbank_out")

    def EB(ri):
        return scr[:, 2048 * ri:2048 * ri + 2048].rearrange("p (j n) -> p j n", j=NP5)

    KK = scr[0:2 * GC, 0:NP5 * KKn * GC].rearrange("p (j k q) -> p j k q", j=NP5, k=KKn)

    with nc.Block() as block:
        @block.sync
        def _(sp):
            for i, n in enumerate(("s5_lam_re", "s5_lam_im")):
                sp.dma_start(raw[:, i, :], a[n][0].rearrange("d (j a) n -> (d j) (a n)", a=2)).then_inc(ld, 16)
            with nc.allow_non_contiguous_dma(reason="small parameters"):
                sp.dma_start(ldt[:], a["s5_log_dt"][0].rearrange("d (j a) -> (d j) a", a=2)).then_inc(ld, 16)
                sp.dma_start(Dc[:], a["s5_d"][0].rearrange("(j r) -> r j", r=2 * GC)).then_inc(ld, 16)
                for i, n in enumerate(("s5_b_re", "s5_b_im")):
                    sp.dma_start(B[:, i], a[n][0].rearrange("d (j a) n q -> (a n) (d j) q", a=2)).then_inc(ld, 16)
                for i, n in enumerate(("s5_c_re", "s5_c_im")):
                    for d in range(2):
                        for half in range(2):
                            src = a[n][0, d].rearrange("(h j a) p n -> h j p a n", h=2, a=2)[half]
                            for j in range(8):
                                sp.dma_start(Cn[j * GC:(j + 1) * GC, 4 * i + 2 * d + half, :]
                                             .rearrange("p (a n) -> p a n", a=2), src[j]).then_inc(ld, 16)

            sp.wait_ge(mv, 1)
            with nc.allow_non_contiguous_dma(reason="rows of 512 bytes"):
                for t in range(T5):
                    for h in range(2):
                        sp.dma_start(
                            tb["M"][t * GC:(t + 1) * GC].rearrange("p (j a) n -> p j a n", a=2)[:, :, h, :],
                            KK[h * GC:(h + 1) * GC, :, T5 - 1 - t:2 * T5 - 1 - t, :].rearrange("p j k q -> p j (k q)")
                        ).then_inc(kd, 16)
            sp.wait_ge(kd, 16 * 2 * T5)

        @block.gpsimd
        def _(pool):
            pool.iota(ramp[:], [[1, NC5]], base=0, channel_multiplier=0,
                      allow_small_or_imprecise_dtypes=True).then_inc(g, 1)
            pool.wait_ge(made["turns"], 1)
            pool.wait_ge(m, 3)
            pool.memset(BD[:], 0.0).then_inc(g, 1)

        @block.scalar
        def _(act):
            act.wait_ge(m, 1)
            act.activation(lam[:].rearrange("p i n -> p (i n)"), ps[:, 0, 0:3 * DJ], ACT.Copy).then_inc(acts, 1)
            act.wait_ge(acts, 1)
            act.activation(s[:, DTC], lam[:, 2], ACT.Exp).then_inc(acts, 1)
            act.wait_ge(made["ar"], 1)
            act.activation(s[:, TN], s[:, AR], ACT.Tanh, scale=0.5).then_inc(acts, 1)
            act.wait_ge(made["theta"], 1)
            act.activation(s[:, SN], s[:, TH], ACT.Sin).then_inc(acts, 1)
            act.activation(s[:, SH], s[:, TH], ACT.Sin, scale=0.5).then_inc(acts, 1)
            for i in range(8):
                act.wait_ge(m, 2 + i // 4)
                ri, d, half = i // 4, (i // 2) % 2, i % 2
                dj = NP5 * d + 8 * half
                act.activation(C[:, ri, dj:dj + 8, :], ps[:, 1 + i // 4, (i % 4) * P:(i % 4 + 1) * P]
                               .rearrange("p (j q) -> p j q", q=GC), ACT.Copy).then_inc(ev, 1)
            act.wait_ge(made["turns"], 1)
            act.activation(tb["cos"][:], tb["sin"][:], ACT.Abs).then_inc(acts, 1)
            act.wait_ge(acts, 6)
            act.activation(tb["sin"][:], tb["sin"][:], ACT.Sin, scale=6.283185).then_inc(acts, 1)
            act.activation(tb["cos"][:], tb["cos"][:], ACT.Sin, scale=-6.283185, bias=s[:, HALF, 0:1]
                           ).then_inc(acts, 1)
            for n in range(16):
                act.wait_ge(m, 3 + n + 1)
                act.activation(E[:, 2 * n:2 * n + 2].rearrange("p j r n -> p (j r n)"), ps[:, n % 2, :], ACT.Copy
                               ).then_inc(ev, 1)

        @block.tensor
        def _(pe):
            pe.wait_ge(ld, 16 * 70)
            pe.wait_ge(v, 1)
            for i in range(3):
                mm = pe.transpose(ps[:, 0, i * DJ:(i + 1) * DJ], raw[:, i, :], c["ident"][0:DJ, 0:DJ])
            mm.then_inc(m, 1)
            for i in range(8):
                mm = pe.transpose(ps[:, 1 + i // 4, (i % 4) * P:(i % 4 + 1) * P], Cn[:, i, :], c["ident"][:])
                if i % 4 == 3:
                    mm.then_inc(m, 1)
            for n in range(16):
                d = n // 8
                pe.wait_ge(made["E"], d + 1)
                pe.wait_ge(ev, 8 + n - 1 if n >= 2 else 8)
                for x in range(4):
                    j, ri = (2 * n + x // 2) % NP5, x % 2
                    mm = pe.transpose(ps[:, n % 2, x * P:(x + 1) * P], EB(ri)[:, j, :], c["ident"][:])
                mm.then_inc(m, 1)
            pe.wait_ge(made["BD"], 1)
            for d in (1, 0):
                for q in range(4):
                    bank = 2 + q % 2
                    n = (1 - d) * 4 + q
                    if n >= 2:
                        pe.wait_ge(mv2, n - 1)
                    for x in range(4):
                        dj = NP5 * d + 4 * q + x
                        for ri in range(2):
                            mm = pe.matmul(ps[0:2 * GC, bank, x * P:(x + 1) * P], BD[:, ri, dj, :],
                                           G[:, ri, dj, d:d + T5, :].rearrange("p k q -> p (k q)"),
                                           start=ri == 0, stop=ri == 1)
                    mm.then_inc(m, 1)

        @block.vector
        def _(dve):
            step = Steps(dve, v)
            TTo, STT = dve.tensor_tensor, dve.scalar_tensor_tensor

            def ew(dst, x, y, op, mark=None, n=1):
                step.done()
                if mark is None:
                    step(TTo(dst, x, y, op))
                else:
                    TTo(dst, x, y, op).then_inc(made[mark], 1)
                    dve.wait_ge(made[mark], n)

            dve.wait_ge(ld, 16 * 70)
            step(dve.tensor_copy(raw[:, 2, :].rearrange("p (a n) -> p a n", a=2),
                                 ldt[:].rearrange("p (a o) -> p a o", o=1).broadcast_to([DJ, 2, NS])))
            dve.wait_ge(acts, 2)
            step(dve.tensor_scalar(s[:, RE], lam[:, 0], -1e-4, None, ALU.min))
            ew(s[:, AR], s[:, RE], s[:, DTC], ALU.mult, "ar")
            step(TTo(s[:, TH], lam[:, 1], s[:, DTC], ALU.mult))
            step.done()
            step(dve.tensor_scalar(s[:, T1], s[:, TH], 1.0 / TWO_PI, MAGIC, ALU.mult, ALU.add))
            step.done()
            step(dve.tensor_scalar(s[:, T1], s[:, T1], MAGIC, None, ALU.subtract))
            step.done()
            step(STT(out=s[:, TH], in0=s[:, T1], scalar=-6.28125, in1=s[:, TH], op0=ALU.mult, op1=ALU.add))
            step.done()
            step(STT(out=s[:, TH], in0=s[:, T1], scalar=-(TWO_PI - 6.28125), in1=s[:, TH],
                     op0=ALU.mult, op1=ALU.add))
            step.done()
            dve.tensor_scalar(s[:, TH], s[:, TH], 3.141592, -3.141592, ALU.min, ALU.max).then_inc(made["theta"], 1)
            dve.wait_ge(made["theta"], 1)
            step(dve.tensor_scalar(s[:, TAU], s[:, TH], T5 / TWO_PI, None, ALU.mult))
            step.done()
            step(dve.tensor_scalar(s[:, T1], s[:, TAU], MAGIC, MAGIC, ALU.add, ALU.subtract))
            ew(s[:, TAU], s[:, TAU], s[:, T1], ALU.subtract)
            dve.wait_ge(acts, 3)
            step.done()
            step(dve.tensor_scalar(s[:, T1], s[:, TN], -1.0, 1.0, ALU.mult, ALU.add))
            step.done()
            step(dve.reciprocal(s[:, T2], s[:, T1]))
            step.done()
            step(STT(out=s[:, EM], in0=s[:, TN], scalar=2.0, in1=s[:, T2], op0=ALU.mult, op1=ALU.mult))
            step.done()
            step(dve.tensor_scalar(s[:, EE], s[:, EM], 1.0, None, ALU.add))
            dve.wait_ge(acts, 5)
            step.done()
            step(STT(out=s[:, T1], in0=s[:, SH], scalar=-2.0, in1=s[:, SH], op0=ALU.mult, op1=ALU.mult))
            step.done()
            step(dve.tensor_scalar(s[:, T2], s[:, T1], 1.0, None, ALU.add))
            ew(s[:, T2], s[:, T2], s[:, EM], ALU.mult)
            ew(s[:, DR], s[:, T2], s[:, T1], ALU.add)
            ew(s[:, DI], s[:, EE], s[:, SN], ALU.mult)
            ew(s[:, T1], s[:, RE], s[:, RE], ALU.mult)
            ew(s[:, T2], lam[:, 1], lam[:, 1], ALU.mult)
            ew(s[:, MM], s[:, T1], s[:, T2], ALU.add)
            step.done()
            step(dve.reciprocal(s[:, MM], s[:, MM]))
            ew(s[:, T1], s[:, DR], s[:, RE], ALU.mult)
            ew(s[:, T2], s[:, DI], lam[:, 1], ALU.mult)
            ew(s[:, T1], s[:, T1], s[:, T2], ALU.add)
            ew(s[:, QR], s[:, T1], s[:, MM], ALU.mult)
            ew(s[:, T1], s[:, DI], s[:, RE], ALU.mult)
            ew(s[:, T2], s[:, DR], lam[:, 1], ALU.mult)
            ew(s[:, T1], s[:, T1], s[:, T2], ALU.subtract)
            ew(s[:, QI], s[:, T1], s[:, MM], ALU.mult)
            ew(tb["rho"][:], s[:, EE], s[:, EE], ALU.mult)
            ew(tb["rho"][:], tb["rho"][:], tb["rho"][:], ALU.mult)
            ew(tb["rho"][:], tb["rho"][:], tb["rho"][:], ALU.mult)
            step(dve.memset(pw[:, 0, 0, :], 1.0))
            step(dve.memset(pw[:, 1, 0, :], 0.0))
            step(dve.memset(s[:, HALF, :], math.pi / 2))
            step(dve.tensor_scalar(pw[:, 0, 1, :], s[:, DR], 1.0, None, ALU.add))
            step(dve.tensor_copy(pw[:, 1, 1, :], s[:, DI]))
            tmp = scr[:, 0:4 * DJ].rearrange("p (k n) -> p k n", k=4)
            for w in (1, 2, 4):
                xr = pw[:, 0, w:w + 1, :].broadcast_to([P, w, DJ])
                xi = pw[:, 1, w:w + 1, :].broadcast_to([P, w, DJ])
                yr, yi = pw[:, 0, 1:w + 1, :], pw[:, 1, 1:w + 1, :]
                zr, zi = pw[:, 0, w + 1:2 * w + 1, :], pw[:, 1, w + 1:2 * w + 1, :]
                ew(zr, xr, yr, ALU.mult)
                ew(tmp[:, 0:w], xi, yi, ALU.mult)
                ew(zr, zr, tmp[:, 0:w], ALU.subtract)
                ew(zi, xr, yi, ALU.mult)
                ew(tmp[:, 0:w], xi, yr, ALU.mult)
                ew(zi, zi, tmp[:, 0:w], ALU.add)

            def spread(x, n):
                return x.rearrange("p (j o) -> p j o", o=1).broadcast_to([P, x.shape[1], n])

            qr, qi = spread(s[:, QR], GC), spread(s[:, QI], GC)
            t16 = scr[:, 0:DJ * GC].rearrange("p (j q) -> p j q", j=DJ)
            ew(Bb[:, 0], qr, B[:, 0], ALU.mult)
            ew(t16, qi, B[:, 1], ALU.mult)
            ew(Bb[:, 0], Bb[:, 0], t16, ALU.subtract)
            ew(Bb[:, 1], qr, B[:, 1], ALU.mult)
            ew(t16, qi, B[:, 0], ALU.mult)
            ew(Bb[:, 1], Bb[:, 1], t16, ALU.add)
            dve.wait_ge(g, 1)
            tau = spread(s[:, TAU], NC5)
            rmp = ramp[:].rearrange("p (o n) -> p o n", o=1).broadcast_to([P, DJ, NC5])
            ew(tb["sin"][:], tau, rmp, ALU.mult)
            step.done()
            step(dve.tensor_scalar(tb["cos"][:], tb["sin"][:], MAGIC, MAGIC, ALU.add, ALU.subtract))
            ew(tb["sin"][:], tb["sin"][:], tb["cos"][:], ALU.subtract, "turns")

            def power(d, ri, lo, n, reverse):
                x = pw[:, ri, lo:lo + n, NP5 * d:NP5 * d + NP5]
                if reverse:
                    x = x[:, ::-1, :]
                return x.rearrange("p k (j o) -> p j k o", o=1).broadcast_to([P, NP5, n, GC])

            def along(x, n):
                return x.rearrange("p j (o q) -> p j o q", o=1).broadcast_to([P, NP5, n, GC])

            dve.wait_ge(ev, 8)
            tg = scr[:, 0:NP5 * 9 * GC].rearrange("p (j k q) -> p j k q", j=NP5, k=9)
            for d in range(2):
                dj = slice(NP5 * d, NP5 * d + NP5)
                pr, pi = power(d, 0, 0, 9, d == 1), power(d, 1, 0, 9, d == 1)
                cr, ci = along(C[:, 0, dj, :], 9), along(C[:, 1, dj, :], 9)
                gr, gn = G[:, 0, dj], G[:, 1, dj]
                ew(gr, cr, pr, ALU.mult)
                ew(tg, ci, pi, ALU.mult)
                ew(gr, gr, tg, ALU.subtract)
                ew(gn, cr, pi, ALU.mult)
                ew(tg, ci, pr, ALU.mult)
                step.done()
                for j in range(0, NP5):
                    ins = STT(out=gn[:, j].rearrange("p k q -> p (k q)"), in0=gn[:, j].rearrange("p k q -> p (k q)"),
                              scalar=-1.0, in1=tg[:, j].rearrange("p k q -> p (k q)"), op0=ALU.mult,
                              op1=ALU.subtract)
                    step(ins)
            te = scr[:, 4096:6144].rearrange("p (j k q) -> p j k q", j=NP5, k=T5)
            for d in range(2):
                dj = slice(NP5 * d, NP5 * d + NP5)
                pr, pi = power(d, 0, 0, T5, d == 0), power(d, 1, 0, T5, d == 0)
                br, bi = along(Bb[:, 0, dj, :], T5), along(Bb[:, 1, dj, :], T5)
                er = EB(0).rearrange("p j (k q) -> p j k q", k=T5)
                ei = EB(1).rearrange("p j (k q) -> p j k q", k=T5)
                step.done()
                if d:
                    dve.wait_ge(m, 3 + 8)
                ew(er, pr, br, ALU.mult)
                ew(te, pi, bi, ALU.mult)
                ew(er, er, te, ALU.subtract)
                ew(ei, pr, bi, ALU.mult)
                ew(te, pi, br, ALU.mult)
                ew(ei, ei, te, ALU.add, "E", d + 1)
            dve.wait_ge(g, 2)
            for h in range(2):
                rows = slice(NS * h, NS * h + NS)
                step(dve.tensor_copy(BD[rows, :, :, h * GC:(h + 1) * GC], Bb[rows]))
            ew(dm[:], c["ident"][0:2 * GC, 0:GC], c["ident"][0:2 * GC, GC:2 * GC], ALU.add, "BD")
            dve.wait_ge(m, 3 + 16)
            for d in (1, 0):
                for q in range(4):
                    n = (1 - d) * 4 + q
                    dve.wait_ge(m, 3 + 16 + n + 1)
                    kp = ps[0:2 * GC, 2 + q % 2, :].rearrange("p (j k q) -> p j k q", j=4, k=T5)
                    if d == 1:
                        dve.tensor_copy(KK[:, 4 * q:4 * q + 4, 0:T5, :], kp).then_inc(mv2, 1)
                    else:
                        dve.wait_ge(mv2, 4 + q)
                        step(dve.tensor_copy(KK[:, 4 * q:4 * q + 4, T5:KKn, :], kp[:, :, 1:T5, :]))
                        mid = KK[:, 4 * q:4 * q + 4, T5 - 1, :]
                        dve.tensor_tensor(mid, mid, kp[:, :, 0, :], ALU.add).then_inc(mv2, 1)
            dve.wait_ge(mv2, 8)
            t7 = BD[0:2 * GC, 0, 0:NP5, 0:GC]
            dve.wait_ge(m, 3 + 16 + 8)
            step(TTo(t7, Dc[:].rearrange("p (j o) -> p j o", o=1).broadcast_to([2 * GC, NP5, GC]),
                     dm[:].rearrange("p (o q) -> p o q", o=1).broadcast_to([2 * GC, NP5, GC]), ALU.mult))
            step.done()
            mid = KK[:, :, T5 - 1, :]
            dve.tensor_tensor(mid, mid, t7, ALU.add).then_inc(mv, 1)


def s5_mixer(nc, core, c, a, uT, tb, yT):
    E, G, M = tb["E"], tb["G"], tb["M"]
    rot = core.sb("s5_rotp", [P, 2, 2, 2, NC5])
    z = core.sb("s5_z", [P, 2, 2, 2, NC5])
    zs = core.sb("s5_zs", [P, 2, 2, NC5])
    back = core.sb("s5_back", [P, 2, 2, 2, NC5])
    st = core.sb("s5_state", [P, 2, 2, 2, NC5])
    ys = core.sb("s5_y", [P, T5, S5W])
    bg = core.sb("s5_bglu", [P, 4])
    free = E[:].rearrange("p j r n -> p (j r n)")
    yg = free[:, 0:4 * L].rearrange("p (k n) -> p k n", k=4)
    sg = free[:, 4 * L:6 * L].rearrange("p (k n) -> p k n", k=2)
    wg = free[:, 6 * L:8 * L].rearrange("p (k n) -> p k n", k=4)
    vps = core.ps("s5_v", [P, 2, 2, 2, NC5])
    tps = core.ps("s5_tps", [P, 4, 512])
    yps = tps[:].rearrange("p (b h) (j n) -> p b h j n", b=2, j=4)
    names = "ld vmm rot z scan back state ymm yout turned gelu glu gate out zero".split()
    S = {n: core.sem("s5m_" + n) for n in names}
    cosv = tb["cos"][:].rearrange("p (d j) n -> p d j n", d=2)
    sinv = tb["sin"][:].rearrange("p (d j) n -> p d j n", d=2)

    def table(x, j):
        return x[:, :, j:j + 1, :].broadcast_to([P, 2, 2, NC5])

    with nc.Block() as block:
        @block.sync
        def _(sp):
            with nc.allow_non_contiguous_dma(reason="small parameters"):
                sp.dma_start(bg[:], a["s5_b_glu"][0].rearrange("(k p) -> p k", p=P)).then_inc(S["ld"], 16)
            sp.wait_ge(S["vmm"], NP5)
            sp.dma_start(wg[:], a["s5_w_glu"][0].rearrange("(k p) n -> p k n", p=P)).then_inc(S["ld"], 16)

        @block.tensor
        def _(pe):
            def inputs(j):
                if j >= 2:
                    pe.wait_ge(S["rot"], 2 * (j - 1))
                for d in range(2):
                    for ri in range(2):
                        for h in range(2):
                            u = uT[:, 2 * j + h, :]
                            rows = slice(NS * h, NS * h + NS)
                            mm = pe.matmul(vps[rows, j % 2, d, ri, :], E[:, NP5 * d + j, ri, rows],
                                           u if d == 0 else u[:, ::-1], start=True, stop=True)
                mm.then_inc(S["vmm"], 1)

            def outputs(j):
                if j % 4 == 0 and j >= 8:
                    pe.wait_ge(S["yout"], 2 * (j // 4 - 1))
                pe.wait_ge(S["state"], 4 * (j + 1))
                for h in range(2):
                    g = 2 * j + h
                    dst = yps[:, (j // 4) % 2, h, j % 4, :]
                    rows = slice(NS * h, NS * h + NS)
                    pe.matmul(dst, uT[:, g, :], M[:, g, :], start=True, stop=False)
                    for d in range(2):
                        for ri in range(2):
                            mm = pe.matmul(dst, st[rows, j % 2, d, ri, :],
                                           G[rows, ri, NP5 * d + j, 1 - d:1 - d + T5, :]
                                           .rearrange("p k q -> p (k q)"),
                                           start=False, stop=d == 1 and ri == 1)
                mm.then_inc(S["ymm"], 1)

            inputs(0)
            inputs(1)
            for j in range(NP5):
                outputs(j)
                if j + 2 < NP5:
                    inputs(j + 2)
            pe.wait_ge(S["yout"], NP5 // 2)
            for k in range(4):
                for half in range(2):
                    n = 2 * k + half
                    if n >= 4:
                        pe.wait_ge(S["gelu"], n - 3)
                    for t in range(4):
                        mm = pe.transpose(tps[:, n % 4, t * P:(t + 1) * P],
                                          ys[:, 4 * half + t, k * P:(k + 1) * P], c["ident"][:])
                    mm.then_inc(S["turned"], 1)
            pe.wait_ge(S["gelu"], 8)
            pe.wait_ge(S["ld"], 32)
            for m in range(4):
                if m >= 2:
                    pe.wait_ge(S["gate"], m - 1)
                for half in range(2):
                    for k in range(4):
                        mm = pe.matmul(tps[:, 2 * (m % 2) + half, :], wg[:, k, m * P:(m + 1) * P],
                                       yg[:, k, half * 512:half * 512 + 512], start=k == 0, stop=k == 3)
                mm.then_inc(S["glu"], 1)

        @block.vector
        def _(dve):
            for slot in range(2):
                for ri in range(2):
                    dve.memset(st[:, slot, 0, ri, 0:1], 0.0).then_inc(S["out"], 1)
                    dve.memset(st[:, slot, 1, ri, NC5 - 1:NC5], 0.0).then_inc(S["out"], 1)
            for j in range(NP5):
                b = j % 2
                dve.wait_ge(S["vmm"], j + 1)
                if j:
                    dve.wait_ge(S["z"], 2 * j)
                dve.tensor_tensor(rot[:, 0], vps[:, b], table(cosv, j), ALU.mult).then_inc(S["rot"], 1)
                dve.tensor_tensor(rot[:, 1], vps[:, b], table(sinv, j), ALU.mult).then_inc(S["rot"], 1)
                dve.wait_ge(S["rot"], 2 * (j + 1))
                if j >= 2:
                    dve.wait_ge(S["scan"], 4 * (j - 1))
                dve.tensor_tensor(z[:, b, :, 0], rot[:, 0, :, 0], rot[:, 1, :, 1], ALU.add).then_inc(S["z"], 1)
                dve.tensor_tensor(z[:, b, :, 1], rot[:, 0, :, 1], rot[:, 1, :, 0], ALU.subtract
                                  ).then_inc(S["z"], 1)
                dve.wait_ge(S["z"], 2 * (j + 1))
                if j:
                    dve.wait_ge(S["back"], 2 * j)
                for d in range(2):
                    rho = tb["rho"][:, NP5 * d + j:NP5 * d + j + 1].broadcast_to([P, NC5])
                    for ri in range(2):
                        dve.tensor_tensor_scan(zs[:, d, ri], rho, z[:, b, d, ri], 0.0, ALU.mult, ALU.add
                                               ).then_inc(S["scan"], 1)
            for m in range(4):
                dve.wait_ge(S["gate"], m + 1)
                dve.tensor_tensor(yT[:, m, :], yg[:, m, :], sg[:, m % 2, :], ALU.mult).then_inc(S["out"], 1)

        @block.gpsimd
        def _(pool):
            n = NC5 - 1
            for j in range(NP5):
                b = j % 2
                pool.wait_ge(S["scan"], 4 * (j + 1))
                if j:
                    pool.wait_ge(S["state"], 4 * j)
                pool.tensor_tensor(back[:, 0], zs[:], table(cosv, j), ALU.mult).then_inc(S["back"], 1)
                pool.tensor_tensor(back[:, 1], zs[:], table(sinv, j), ALU.mult).then_inc(S["back"], 1)
                pool.wait_ge(S["back"], 2 * (j + 1))
                if j == 0:
                    pool.wait_ge(S["out"], 8)
                elif j >= 2:
                    pool.wait_ge(S["ymm"], j - 1)
                pool.tensor_tensor(st[:, b, 0, 0, 1:], back[:, 0, 0, 0, 0:n], back[:, 1, 0, 1, 0:n],
                                   ALU.subtract).then_inc(S["state"], 1)
                pool.tensor_tensor(st[:, b, 0, 1, 1:], back[:, 0, 0, 1, 0:n], back[:, 1, 0, 0, 0:n],
                                   ALU.add).then_inc(S["state"], 1)
                pool.tensor_tensor(st[:, b, 1, 0, 0:n][:, ::-1], back[:, 0, 1, 0, 0:n], back[:, 1, 1, 1, 0:n],
                                   ALU.subtract).then_inc(S["state"], 1)
                pool.tensor_tensor(st[:, b, 1, 1, 0:n][:, ::-1], back[:, 0, 1, 1, 0:n], back[:, 1, 1, 0, 0:n],
                                   ALU.add).then_inc(S["state"], 1)

        @block.scalar
        def _(act):
            yv = ys[:].rearrange("p t (j h q) -> p h j t q", j=NP5, h=2)
            for n in range(NP5 // 4):
                act.wait_ge(S["ymm"], 4 * (n + 1))
                for h in range(2):
                    act.activation(yv[:, h, 4 * n:4 * n + 4], yps[:, n % 2, h].rearrange("p j (t q) -> p j t q", t=T5),
                                   ACT.Copy).then_inc(S["yout"], 1)
            for k in range(4):
                for half in range(2):
                    n = 2 * k + half
                    act.wait_ge(S["turned"], n + 1)
                    act.activation(yg[:, k, :].rearrange("p (n t) -> p t n", t=T5)[:, 4 * half:4 * half + 4, :],
                                   tps[:, n % 4].rearrange("p (t n) -> p t n", t=4), ACT.Gelu
                                   ).then_inc(S["gelu"], 1)
            act.wait_ge(S["ld"], 32)
            for m in range(4):
                act.wait_ge(S["glu"], m + 1)
                if m >= 2:
                    act.wait_ge(S["out"], 8 + m - 1)
                act.activation(sg[:, m % 2, :], tps[:, 2 * (m % 2):2 * (m % 2) + 2, :].rearrange("p a n -> p (a n)"),
                               ACT.Sigmoid, bias=bg[:, m:m + 1]).then_inc(S["gate"], 1)


def gated_norm(nc, core, c, a, o_sum, zs, ydn):
    sq = core.sb("gn_sq", [P, 2, DW])
    ss = core.sb("gn_ss", [P, TT, H])
    rt = core.sb("gn_rt", [P, TT, H])
    rs = core.sb("gn_rs", [P, TT, H])
    nw = core.sb("gn_w", [P, 1])
    ps = core.ps("gn_ps", [P, 2, 512])
    ld, sqd, red, rtd, rsd, nrm, turned, out, part = (core.sem("gn_" + n) for n in
                                                      "ld sq red rt rs nrm turned out part".split())

    def heads(x):
        return x.rearrange("p (h n) -> p h n", h=H)

    with nc.Block() as block:
        @block.sync
        def _(sp):
            with nc.allow_non_contiguous_dma(reason="small parameters"):
                sp.dma_start(nw[:], a["gdn_norm_w"].rearrange("o n -> n o")).then_inc(ld, 16)

        @block.scalar
        def _(act):
            for t in range(TT):
                if t >= 2:
                    act.wait_ge(red, t - 1)
                act.activation(sq[:, t % 2, :], o_sum[:, t, :], ACT.Square).then_inc(sqd, 1)
            act.wait_ge(rsd, 1)
            act.activation(rt[:], ss[:], ACT.Sqrt).then_inc(rtd, 1)
            act.wait_ge(ld, 16)
            for t in range(TT):
                act.wait_ge(turned, t + 1)
                act.activation(ydn[:, :, t * P:(t + 1) * P], ps[:, t % 2, :].rearrange("p (h n) -> p h n", h=H),
                               ACT.Copy, scale=nw[:, 0:1]).then_inc(out, 1)

        @block.vector
        def _(dve):
            for t in range(TT):
                dve.wait_ge(sqd, t + 1)
                dve.tensor_reduce(ss[:, t, :], heads(sq[:, t % 2, :]), AX.X, ALU.add).then_inc(red, 1)
            dve.wait_ge(red, TT)
            dve.tensor_scalar(ss[:], ss[:], 1.0 / DH, EPS, ALU.mult, ALU.add).then_inc(rsd, 1)
            dve.wait_ge(rtd, 1)
            dve.reciprocal(rs[:], rt[:]).then_inc(rsd, 1)
            dve.wait_ge(rsd, 2)
            for t in range(TT):
                scale = rs[:, t, :].rearrange("p (h o) -> p h o", o=1).broadcast_to([P, H, DH])
                dve.tensor_tensor(heads(o_sum[:, t, :]), heads(o_sum[:, t, :]), scale, ALU.mult
                                  ).then_inc(part, 1)
                dve.wait_ge(part, t + 1)
                dve.tensor_tensor(o_sum[:, t, :], o_sum[:, t, :], zs[:, t, :], ALU.mult).then_inc(nrm, 1)

        @block.tensor
        def _(pe):
            for t in range(TT):
                pe.wait_ge(nrm, t + 1)
                if t >= 2:
                    pe.wait_ge(out, t - 1)
                for h in range(H):
                    mm = pe.transpose(ps[:, t % 2, h * P:(h + 1) * P], o_sum[:, t, h * DH:(h + 1) * DH],
                                      c["ident"][:])
                mm.then_inc(turned, 1)


def out_projection(nc, core, c, a, ys5, ydn, x1, logits, h_dram, filled):
    NR = NGRP + NEXP
    wo = core.sb("w_out_sb", [P, KT, D])
    nf = core.sb("norm_ffn_row", [P, D])
    h2 = core.sb("h_row", [P, 2, D])
    hT = core.sb("h_turned", [P, 2, KT, P])
    sq = core.sb("op_sq", [P, D])
    ss = core.sb("op_ss", [P, TT])
    ms = core.sb("op_ms", [P, TT])
    rt = core.sb("op_rt", [P, TT])
    rs = core.sb("op_rs", [P, TT])
    wr = core.sb("w_router", [P, KT, NR])
    br = core.sb("b_router", [P, NR])
    mm_ps = core.ps("op_ps", [P, 2, 2, 512])
    tr_ps = core.ps("op_turn", [P, 2, 512])
    lg_ps = core.ps("op_logits", [P, 2, 512])
    names = "x w par mm x1 sq ms rt rs h turned hT lg store0 store1".split()
    S = {n: core.sem("op_" + n) for n in names}
    store = [S["store0"], S["store1"]]

    with nc.Block() as block:
        @block.sync
        def _(sp):
            sp.dma_start(wo[:], a["w_out"][0].rearrange("(k p) n -> p k n", p=P)).then_inc(S["w"], 16)
            sp.dma_start(x1[:], a["x"].rearrange("b (t p) d -> p (b t) d", p=P)).then_inc(S["x"], 16)
            sp.dma_start(nf[:], a["norm_ffn"].partition_broadcast(P)).then_inc(S["par"], 16)
            with nc.allow_non_contiguous_dma(reason="small parameters"):
                sp.dma_start(wr[:, :, 0:NGRP], a["router_w_group"][0].rearrange("(k p) n -> p k n", p=P)
                             ).then_inc(S["par"], 16)
                for g in range(NGRP):
                    sp.dma_start(wr[:, :, NGRP + EPG * g:NGRP + EPG * (g + 1)],
                                 a["router_w_expert"][0, g].rearrange("(k p) n -> p k n", p=P)
                                 ).then_inc(S["par"], 16)
                sp.dma_start(br[:, 0:NGRP], a["router_b_group"].partition_broadcast(P)).then_inc(S["par"], 16)
                sp.dma_start(br[:, NGRP:], a["router_b_expert"].rearrange("o g e -> o (g e)")
                             .partition_broadcast(P)).then_inc(S["par"], 16)
            for t in range(TT):
                sp.wait_ge(S["h"], t + 1)
                sp.dma_start(h_dram[t * P:(t + 1) * P, :], h2[:, t % 2, :]).then_inc(store[t % 2], 16)
            sp.wait_ge(filled, 16 * (MAXB + 1 - L * 2 // P))
            for s in range(2):
                sp.wait_ge(store[s], 16 * TT // 2)

        @block.tensor
        def _(pe):
            def project(t):
                if t >= 2:
                    pe.wait_ge(S["x1"], t - 1)
                for half in range(2):
                    for k in range(KT):
                        y = ys5[:, k] if k < 4 else ydn[:, k - 4]
                        mm = pe.matmul(mm_ps[:, t % 2, half, :], y[:, t * P:(t + 1) * P],
                                       wo[:, k, half * 512:half * 512 + 512], start=k == 0, stop=k == KT - 1)
                mm.then_inc(S["mm"], 1)

            def route(t):
                pe.wait_ge(S["h"], t + 1)
                for half in range(2):
                    n = 2 * t + half
                    if n >= 2:
                        pe.wait_ge(S["hT"], n - 1)
                    for k in range(4):
                        mm = pe.transpose(tr_ps[:, half, k * P:(k + 1) * P],
                                          h2[:, t % 2, (4 * half + k) * P:(4 * half + k + 1) * P], c["ident"][:])
                    mm.then_inc(S["turned"], 1)

            def logit(t):
                pe.wait_ge(S["hT"], 2 * t + 2)
                for k in range(KT):
                    mm = pe.matmul(lg_ps[:, 0, t * NR:(t + 1) * NR], hT[:, t % 2, k, :], wr[:, k, :],
                                   start=k == 0, stop=k == KT - 1)
                mm.then_inc(S["lg"], 1)

            pe.wait_ge(S["w"], 16)
            pe.wait_ge(S["par"], 16 * 8)
            for t in range(TT + 2):
                if t < TT:
                    project(t)
                if 1 <= t <= TT:
                    route(t - 1)
                if t >= 2:
                    logit(t - 2)

        @block.vector
        def _(dve):
            dve.wait_ge(S["x"], 16)
            dve.wait_ge(S["par"], 16 * 8)
            for t in range(TT):
                dve.wait_ge(S["mm"], t + 1)
                dve.tensor_tensor(x1[:, t, :], x1[:, t, :], mm_ps[:, t % 2].rearrange("p a n -> p (a n)"), ALU.add
                                  ).then_inc(S["x1"], 1)
                dve.wait_ge(S["sq"], t + 1)
                dve.tensor_scalar(ms[:, t:t + 1], ss[:, t:t + 1], 1.0 / D, EPS, ALU.mult, ALU.add
                                  ).then_inc(S["ms"], 1)
                dve.wait_ge(S["rt"], t + 1)
                dve.reciprocal(rs[:, t:t + 1], rt[:, t:t + 1]).then_inc(S["rs"], 1)
                dve.wait_ge(S["rs"], t + 1)
                if t >= 2:
                    dve.wait_ge(store[t % 2], 16 * (t // 2))
                    dve.wait_ge(S["turned"], 2 * (t - 1))
                dve.scalar_tensor_tensor(out=h2[:, t % 2, :], in0=x1[:, t, :], scalar=rs[:, t:t + 1], in1=nf[:],
                                         op0=ALU.mult, op1=ALU.mult).then_inc(S["h"], 1)
            dve.wait_ge(S["lg"], TT)
            dve.tensor_tensor(logits[:], lg_ps[:, 0, 0:TT * NR].rearrange("p (t n) -> p t n", n=NR),
                              br[:].rearrange("p (o n) -> p o n", o=1).broadcast_to([P, TT, NR]), ALU.add
                              ).then_inc(S["x1"], 1)

        @block.scalar
        def _(act):
            def turned(t):
                for half in range(2):
                    n = 2 * t + half
                    act.wait_ge(S["turned"], n + 1)
                    if t >= 2:
                        act.wait_ge(S["lg"], t - 1)
                    act.activation(hT[:, t % 2, 4 * half:4 * half + 4, :],
                                   tr_ps[:, half, :].rearrange("p (k n) -> p k n", k=4), ACT.Copy
                                   ).then_inc(S["hT"], 1)

            for t in range(TT):
                act.wait_ge(S["x1"], t + 1)
                if t:
                    act.wait_ge(S["sq"], t)
                act.activation(sq[:], x1[:, t, :], ACT.Square, accum_out=ss[:, t:t + 1]).then_inc(S["sq"], 1)
                act.wait_ge(S["ms"], t + 1)
                act.activation(rt[:, t:t + 1], ms[:, t:t + 1], ACT.Sqrt).then_inc(S["rt"], 1)
                if t >= 1:
                    turned(t - 1)
            turned(TT - 1)


def router_tables(core):
    return {
        "slot_tok": core.sb("slot_token", [P, MAXB + 3], I32),
        "block": core.sb("block_expert", [P, MAXB + 1], I32),
        "count": core.sb("block_count", [P, 1], I32),
        "dest": core.sb("dest_slot", [P, 2, TT], I32),
        "gate": core.sb("gate", [P, 2, TT]),
    }


def router(nc, core, c, logits, rt):
    NB = MAXB + 1
    strict = core.sb("r_strict", [P, P])
    iota = core.sb("r_iota", [P, P])
    tokid = core.sb("r_tokid", [P, TT])
    ge = core.sb("r_group", [P, TT, NGRP])
    one_g = core.sb("r_one_group", [P, TT, NGRP])
    em = core.sb("r_masked", [P, TT, NEXP])
    t32 = core.sb("r_t32", [P, TT, NEXP])
    one = core.sb("r_one", [P, 2, TT, NEXP])
    both = core.sb("r_both", [P, TT, NEXP])
    pos = core.sb("r_pos", [P, TT, NEXP])
    off = core.sb("r_off", [P, TT + 1, NEXP])
    blocks = core.sb("r_blocks", [P, 3, NEXP])
    cmp8 = core.sb("r_cmp8", [P, NEXP, TT])
    cmpb = core.sb("r_cmpb", [P, NB, NEXP])
    col = core.sb("r_cols", [P, 8, TT])
    dest = core.sb("r_dest", [P, 2, TT])
    blk = core.sb("r_blk", [P, 2, TT])
    slot = core.sb("r_slot", [P, 2, TT])
    hit_s = core.sb("r_hit_slot", [P, 2 * TT, P])
    hit_b = core.sb("r_hit_block", [P, 2 * TT, NB])
    ebf = core.sb("r_ebf", [P, NB])
    ps = core.ps("r_ps", [P, 3, 512])
    pg, v, s, m, hit = (core.sem("r_" + n) for n in "pool dve act pe hit".split())
    s_ready = [core.sem("r_ready_" + n) for n in ("groups", "gap", "experts")]
    GMAX, GSUM, M1, M2, W, TMP = range(6)

    def last(x, n):
        return x.rearrange("p (t o) -> p t o", o=1).broadcast_to([P, x.shape[1], n])

    def tiles(x, n=TT):
        return x.rearrange("p (o e) -> p o e", o=1).broadcast_to([P, n, x.shape[1]])

    with nc.Block() as block:
        @block.gpsimd
        def _(pool):
            step = Steps(pool, pg)
            step(pool.iota(iota[:], [[1, P]], base=0, channel_multiplier=0, allow_small_or_imprecise_dtypes=True))
            step(pool.iota(tokid[:], [[P, TT]], base=0, channel_multiplier=1, allow_small_or_imprecise_dtypes=True))
            step(pool.affine_select(out=strict[:], in_=c["ones"][:], compare_op=ALU.is_gt, fill=0.0, base=0,
                                    pattern=[[1, P]], channel_multiplier=-1))
            step(pool.memset(rt["slot_tok"][:], 0))

        @block.scalar
        def _(act):
            act.wait_ge(s_ready[0], 1)
            act.activation(ge[:], ge[:], ACT.Exp).then_inc(s, 1)
            act.wait_ge(s_ready[1], 1)
            act.activation(col[:, TMP], col[:, TMP], ACT.Exp).then_inc(s, 1)

        @block.tensor
        def _(pe):
            pe.wait_ge(s_ready[2], 1)
            pe.wait_ge(pg, 3)
            flat = both[:].rearrange("p t e -> p (t e)")
            pe.matmul(ps[:, 0, 0:TT * NEXP], strict[:], flat, start=True, stop=True)
            pe.matmul(ps[:, 1, 0:TT * NEXP], c["ones"][:], flat, start=True, stop=True).then_inc(m, 1)
            for n in range(2 * TT):
                pe.wait_ge(hit, 2 * (n + 1))
                mm = pe.matmul(ps[:, 2, 0:NB], hit_s[:, n, :], hit_b[:, n, :], start=n == 0, stop=n == 2 * TT - 1)
            mm.then_inc(m, 1)

        @block.vector
        def _(dve):
            step = Steps(dve, v)
            TTo = dve.tensor_tensor

            def seq(ins_of, mark=None):
                step.done()
                ins = ins_of()
                if mark is None:
                    step(ins)
                else:
                    ins.then_inc(mark, 1)
                    dve.wait_ge(mark, 1)

            dve.wait_ge(pg, 4)
            lg, le = logits[:, :, 0:NGRP], logits[:, :, NGRP:]
            step(dve.tensor_reduce(col[:, GMAX], lg, AX.X, ALU.max))
            seq(lambda: TTo(ge[:], lg, last(col[:, GMAX], NGRP), ALU.subtract))

            def first_max(dst, x, n, mx, tmp):
                seq(lambda: TTo(tmp, x, last(mx, n), ALU.is_equal))
                seq(lambda: dve.tensor_scalar(tmp, tmp, -BIG, BIG, ALU.mult, ALU.add))
                seq(lambda: TTo(tmp, tmp, tiles(iota[:, 0:n]), ALU.add))
                seq(lambda: dve.tensor_reduce(col[:, W], tmp, AX.X, ALU.min))
                seq(lambda: TTo(dst, last(col[:, W], n), tiles(iota[:, 0:n]), ALU.is_equal))

            first_max(one_g[:], lg, NGRP, col[:, GMAX], t32[:, :, 0:NGRP])
            step.done()
            dve.tensor_copy(t32[:, :, 0:NGRP], one_g[:]).then_inc(s_ready[0], 1)
            dve.wait_ge(s_ready[0], 1)
            g4 = one_g[:].rearrange("p t (g o) -> p t g o", o=1).broadcast_to([P, TT, NGRP, EPG])
            e4 = em[:].rearrange("p t (g e) -> p t g e", g=NGRP)
            t4 = t32[:].rearrange("p t (g e) -> p t g e", g=NGRP)
            l4 = le.rearrange("p t (g e) -> p t g e", g=NGRP)
            seq(lambda: TTo(e4, l4, g4, ALU.mult))
            seq(lambda: dve.tensor_copy(t4, g4))
            seq(lambda: dve.tensor_scalar(t32[:], t32[:], BIG, -BIG, ALU.mult, ALU.add))
            seq(lambda: TTo(em[:], em[:], t32[:], ALU.add))
            seq(lambda: dve.tensor_reduce(col[:, M1], em[:], AX.X, ALU.max))
            first_max(one[:, 0], em[:], NEXP, col[:, M1], t32[:])
            seq(lambda: dve.tensor_scalar(t32[:], one[:, 0], -3.0 * BIG, None, ALU.mult))
            seq(lambda: TTo(em[:], em[:], t32[:], ALU.add))
            seq(lambda: dve.tensor_reduce(col[:, M2], em[:], AX.X, ALU.max))
            first_max(one[:, 1], em[:], NEXP, col[:, M2], t32[:])
            seq(lambda: TTo(both[:], one[:, 0], one[:, 1], ALU.add), s_ready[2])
            seq(lambda: TTo(col[:, TMP], col[:, M2], col[:, M1], ALU.subtract), s_ready[1])
            dve.wait_ge(s, 2)
            seq(lambda: dve.tensor_reduce(col[:, GSUM], ge[:], AX.X, ALU.add))
            seq(lambda: dve.tensor_scalar(col[:, W], col[:, TMP], 1.0, None, ALU.add))
            seq(lambda: TTo(col[:, W], col[:, W], col[:, GSUM], ALU.mult))
            seq(lambda: dve.reciprocal(rt["gate"][:, 0], col[:, W]))
            seq(lambda: TTo(rt["gate"][:, 1], rt["gate"][:, 0], col[:, TMP], ALU.mult))
            dve.wait_ge(m, 1)
            tot = ps[:, 1, 0:TT * NEXP].rearrange("p (t e) -> p t e", t=TT)
            seq(lambda: dve.memset(off[:, 0, :], 0.0))
            for t in range(TT):
                seq(lambda: TTo(off[:, t + 1, :], off[:, t, :], tot[:, t, :], ALU.add))
            cnt = off[:, TT, :]
            seq(lambda: dve.tensor_scalar(ebf[:, 0:TT], iota[:, 0:TT], float(P), None, ALU.mult))
            seq(lambda: TTo(cmp8[:], last(cnt, TT), tiles(ebf[:, 0:TT], NEXP), ALU.is_gt))
            seq(lambda: dve.tensor_reduce(blocks[:, 0], cmp8[:], AX.X, ALU.add))
            seq(lambda: dve.tensor_tensor_scan(blocks[:, 1], c["ones"][:, 0:NEXP], blocks[:, 0], 0.0,
                                               ALU.mult, ALU.add))
            seq(lambda: TTo(blocks[:, 2], blocks[:, 1], blocks[:, 0], ALU.subtract))
            seq(lambda: dve.tensor_scalar(blocks[:, 2], blocks[:, 2], float(P), None, ALU.mult))
            seq(lambda: TTo(pos[:], off[:, 0:TT, :], ps[:, 0, 0:TT * NEXP].rearrange("p (t e) -> p t e", t=TT),
                            ALU.add))
            seq(lambda: TTo(pos[:], pos[:], tiles(blocks[:, 2]), ALU.add))
            for k in range(2):
                seq(lambda: TTo(t32[:], pos[:], one[:, k], ALU.mult))
                seq(lambda: dve.tensor_reduce(dest[:, k], t32[:], AX.X, ALU.add))
            seq(lambda: dve.tensor_copy(rt["dest"][:], dest[:]))
            seq(lambda: dve.tensor_scalar(blk[:], dest[:], 1.0 / P, -(P - 1) / (2.0 * P), ALU.mult, ALU.add))
            seq(lambda: dve.tensor_scalar(blk[:], blk[:], MAGIC, MAGIC, ALU.add, ALU.subtract))
            seq(lambda: dve.scalar_tensor_tensor(out=slot[:], in0=blk[:], scalar=-float(P), in1=dest[:],
                                                 op0=ALU.mult, op1=ALU.add))
            step.done()
            for n in range(2 * TT):
                k, t = n // TT, n % TT
                dve.tensor_scalar(hit_s[:, n, :], iota[:], slot[:, k, t:t + 1], tokid[:, t:t + 1],
                                  ALU.is_equal, ALU.mult).then_inc(hit, 1)
                dve.tensor_scalar(hit_b[:, n, :], iota[:, 0:NB], blk[:, k, t:t + 1], None,
                                  ALU.is_equal).then_inc(hit, 1)
            step(TTo(cmpb[:], tiles(blocks[:, 1], NB), last(iota[:, 0:NB], NEXP), ALU.is_le))
            seq(lambda: dve.tensor_reduce(ebf[:], cmpb[:], AX.X, ALU.add))
            seq(lambda: dve.tensor_scalar(ebf[:], ebf[:], float(NEXP - 1), None, ALU.min))
            seq(lambda: dve.tensor_copy(rt["block"][:], ebf[:]))
            seq(lambda: dve.tensor_copy(rt["count"][:], blocks[:, 1, NEXP - 1:NEXP]))
            dve.wait_ge(m, 2)
            seq(lambda: dve.tensor_copy(rt["slot_tok"][:, 0:NB], ps[:, 2, 0:NB]))


def experts(nc, core, c, a, rt, h_dram, y_dram):
    KD = DE // P
    wg = core.sb("w_gate", [P, 2, KT, DE])
    wu = core.sb("w_up", [P, 2, KT, DE])
    wd = core.sb("w_down", [P, 2, KD, D])
    idx = core.sb("gather_idx", [P, 2], I32)
    xg = core.sb("gathered", [P, 2, D])
    xT = core.sb("gathered_T", [P, 2, KT, P])
    sg = core.sb("silu_gate", [P, DE])
    hid = core.sb("hidden", [P, DE])
    hT = core.sb("hidden_T", [P, KD, P])
    y = core.sb("expert_out", [P, 2, D])
    g_ps = core.ps("gate_mm", [P, 512])
    u_ps = core.ps("up_mm", [P, 512])
    x_ps = core.ps("x_turned", [P, 2, 512])
    h_ps = core.ps("h_turned_ps", [P, 512])
    y_ps = core.ps("down_mm", [P, 2, 512])
    names = "gate_mm up_mm x_turned xT silu hid h_turned hT down_mm y_out idx turn".split()
    S = {n: core.sem("ex_" + n) for n in names}
    ld = {n: [core.sem(f"ex_ld_{n}{s}") for s in range(2)] for n in "gud"}
    gathered = [core.sem(f"ex_gathered{s}") for s in range(2)]
    stored = [core.sem(f"ex_stored{s}") for s in range(2)]
    w_gate = a["expert_w_gate"].rearrange("o e (p k) n -> p (o e) k n", k=KT)
    w_up = a["expert_w_up"].rearrange("o e (p k) n -> p (o e) k n", k=KT)
    w_down = a["expert_w_down"].rearrange("o e (p k) n -> p (o e) k n", k=KD)
    y_blocks = y_dram.rearrange("(b p) d -> b p d", p=P)
    PAIRS = (MAXB + 1) // 2

    with nc.Block() as block:
        @block.sync
        def _(sp):
            count = sp.value_load(rt["count"][0:1, 0:1], min_val=16, max_val=MAXB)
            with sp.Fori(0, PAIRS) as i:
                for s in range(2):
                    b = i * 2 + s
                    with sp.If(b < count):
                        e = sp.value_load(rt["block"][0:1, bass.ds(b, 1)], min_val=0, max_val=NEXP - 1)
                        sp.wait_ge(S["up_mm"], b + 1)
                        sp.dma_start(wg[:, s], w_gate[:, bass.ds(e, 1)].rearrange("p o k n -> p (o k) n")
                                     ).then_inc(ld["g"][s], 16)
                        sp.dma_start(wu[:, s], w_up[:, bass.ds(e, 1)].rearrange("p o k n -> p (o k) n")
                                     ).then_inc(ld["u"][s], 16)
                        sp.wait_ge(S["down_mm"], b + 1)
                        sp.dma_start(wd[:, s], w_down[:, bass.ds(e, 1)].rearrange("p o k n -> p (o k) n")
                                     ).then_inc(ld["d"][s], 16)

        @block.gpsimd
        def _(pool):
            count = pool.value_load(rt["count"][0:1, 0:1], min_val=16, max_val=MAXB)

            def gather(s, b, wait_idx):
                pool.tensor_copy(idx[:, s:s + 1], rt["slot_tok"][:, bass.ds(b, 1)]).then_inc(S["idx"], 1)
                pool.wait_ge(S["idx"], wait_idx)
                pool.sem_inc(S["turn"], 1)
                pool.indirect_dma_start(out=xg[:, s, :], out_offset=None, in_=h_dram,
                                        in_offset=bass.IndirectOffsetOnAxis(ap=idx[:, s:s + 1], axis=0)
                                        ).then_inc(gathered[s], 16)

            gather(0, 0, 1)
            with pool.Fori(0, PAIRS) as i:
                for s in range(2):
                    b = i * 2 + s
                    with pool.If(b < count):
                        pool.wait_ge(S["x_turned"], b + 1)
                        gather(1 - s, b + 1, b + 2)
            pool.wait_ge(gathered[0], 16 * (count // 2 + 1))
            pool.wait_ge(gathered[1], 16 * ((count + 1) // 2))
            pool.sem_inc(S["turn"], 1)

        @block.tensor
        def _(pe):
            count = pe.value_load(rt["count"][0:1, 0:1], min_val=16, max_val=MAXB)
            pe.sem_inc(S["up_mm"], 2)
            pe.sem_inc(S["down_mm"], 2)

            def turn_rows(s):
                for k in range(KT):
                    mm = pe.transpose(x_ps[:, k // 4, (k % 4) * P:(k % 4 + 1) * P], xg[:, s, k:D:KT],
                                      c["ident"][:])
                mm.then_inc(S["x_turned"], 1)

            pe.wait_ge(gathered[0], 16)
            turn_rows(0)
            with pe.Fori(0, PAIRS) as i:
                for s in range(2):
                    b = i * 2 + s
                    with pe.If(b < count):
                        pe.wait_ge(ld["g"][s], i * 16 + 16)
                        pe.wait_ge(S["xT"], b + 1)
                        pe.wait_ge(S["silu"], b + 1)
                        for k in range(KT):
                            mm = pe.matmul(g_ps[:], xT[:, s, k, :], wg[:, s, k, :], start=k == 0, stop=k == KT - 1)
                        mm.then_inc(S["gate_mm"], 1)
                        pe.wait_ge(ld["u"][s], i * 16 + 16)
                        pe.wait_ge(S["hid"], b + 1)
                        for k in range(KT):
                            mm = pe.matmul(u_ps[:], xT[:, s, k, :], wu[:, s, k, :], start=k == 0, stop=k == KT - 1)
                        mm.then_inc(S["up_mm"], 1)
                        pe.wait_ge(gathered[1 - s], i * 16 + 16 * (s + 1))
                        turn_rows(1 - s)
                        pe.wait_ge(S["hid"], b + 2)
                        for k in range(KD):
                            mm = pe.transpose(h_ps[:, k * P:(k + 1) * P], hid[:, k:DE:KD], c["ident"][:])
                        mm.then_inc(S["h_turned"], 1)
                        pe.wait_ge(ld["d"][s], i * 16 + 16)
                        pe.wait_ge(S["hT"], b + 1)
                        pe.wait_ge(S["y_out"], b * 2 + 2)
                        for half in range(2):
                            for k in range(KD):
                                mm = pe.matmul(y_ps[:, half, :], hT[:, k, :], wd[:, s, k, half * 512:half * 512 + 512],
                                               start=k == 0, stop=k == KD - 1)
                        mm.then_inc(S["down_mm"], 1)

        @block.scalar
        def _(act):
            count = act.value_load(rt["count"][0:1, 0:1], min_val=16, max_val=MAXB)
            act.sem_inc(S["silu"], 1)
            act.sem_inc(S["y_out"], 2)
            for s in range(2):
                act.sem_inc(stored[s], 16)

            def rows_out(s):
                act.activation(xT[:, s].rearrange("p k n -> p (k n)"), x_ps[:].rearrange("p a n -> p (a n)"),
                               ACT.Copy).then_inc(S["xT"], 1)

            act.wait_ge(S["x_turned"], 1)
            rows_out(0)
            with act.Fori(0, PAIRS) as i:
                for s in range(2):
                    b = i * 2 + s
                    with act.If(b < count):
                        act.wait_ge(S["gate_mm"], b + 1)
                        act.wait_ge(S["hid"], b + 1)
                        act.activation(sg[:], g_ps[:], ACT.Silu).then_inc(S["silu"], 1)
                        act.wait_ge(S["x_turned"], b + 2)
                        rows_out(1 - s)
                        act.wait_ge(S["down_mm"], b + 3)
                        act.wait_ge(stored[s], i * 16 + 16)
                        act.activation(y[:, s, 0:512], y_ps[:, 0, :], ACT.Copy).then_inc(S["y_out"], 1)
                        act.wait_ge(S["y_out"], b * 2 + 4)
                        act.dma_start(y_blocks[bass.ds(b, 1)].rearrange("o p d -> p (o d)"), y[:, s, :]
                                      ).then_inc(stored[s], 16)
            act.wait_ge(stored[0], 16 * ((count + 1) // 2) + 16)
            act.wait_ge(stored[1], 16 * (count // 2) + 16)
            act.activation(sg[:, 0:1], c["ones"][:, 0:1], ACT.Copy)

        @block.vector
        def _(dve):
            count = dve.value_load(rt["count"][0:1, 0:1], min_val=16, max_val=MAXB)
            dve.sem_inc(S["hid"], 1)
            with dve.Fori(0, PAIRS) as i:
                for s in range(2):
                    b = i * 2 + s
                    with dve.If(b < count):
                        dve.wait_ge(S["up_mm"], b + 3)
                        dve.wait_ge(S["silu"], b + 2)
                        dve.tensor_tensor(hid[:], sg[:], u_ps[:], ALU.mult).then_inc(S["hid"], 1)
                        dve.wait_ge(S["h_turned"], b + 1)
                        dve.tensor_copy(hT[:].rearrange("p k n -> p (k n)"), h_ps[:]).then_inc(S["hT"], 1)
                        dve.wait_ge(S["down_mm"], b + 3)
                        dve.wait_ge(stored[s], i * 16 + 16)
                        dve.tensor_copy(y[:, s, 512:], y_ps[:, 1, :]).then_inc(S["y_out"], 1)


def combine(nc, core, c, a, x1, rt, y_dram, out):
    rows = core.sb("expert_rows", [P, 4, 2, D])
    res = core.sb("result", [P, 2, D])
    sq = core.sb("cb_sq", [P, D])
    nf = core.sb("norm_final_row", [P, D])
    st = core.sb("cb_stats", [P, 4, TT])
    par = core.sem("cb_par")
    got = [[core.sem(f"cb_got{s}{k}") for k in range(2)] for s in range(4)]
    stored = [core.sem(f"cb_stored{s}") for s in range(2)]
    add, sqd, msd, rtd, rsd, res_s = (core.sem("cb_" + n) for n in "add sq ms rt rs res".split())
    out_rows = out.rearrange("b (t p) d -> p (b t) d", p=P)

    with nc.Block() as block:
        @block.gpsimd
        def _(pool):
            for t in range(TT):
                if t >= 4:
                    pool.wait_ge(add, 2 * (t - 3))
                for k in range(2):
                    pool.indirect_dma_start(out=rows[:, t % 4, k, :], out_offset=None, in_=y_dram,
                                            in_offset=bass.IndirectOffsetOnAxis(ap=rt["dest"][:, k, t:t + 1], axis=0)
                                            ).then_inc(got[t % 4][k], 16)

        @block.sync
        def _(sp):
            sp.dma_start(nf[:], a["norm_final"].rearrange("(o n) -> o n", o=1).partition_broadcast(P)
                         ).then_inc(par, 16)
            for t in range(TT):
                sp.wait_ge(res_s, t + 1)
                sp.dma_start(out_rows[:, t, :], res[:, t % 2, :]).then_inc(stored[t % 2], 16)
            for s in range(2):
                sp.wait_ge(stored[s], 16 * TT // 2)

        @block.vector
        def _(dve):
            def norm(t):
                dve.wait_ge(sqd, t + 1)
                dve.tensor_scalar(st[:, 1, t:t + 1], st[:, 0, t:t + 1], 1.0 / D, EPS, ALU.mult, ALU.add
                                  ).then_inc(msd, 1)
                dve.wait_ge(rtd, t + 1)
                dve.reciprocal(st[:, 3, t:t + 1], st[:, 2, t:t + 1]).then_inc(rsd, 1)
                dve.wait_ge(rsd, t + 1)
                if t >= 2:
                    dve.wait_ge(stored[t % 2], 16 * (t // 2))
                dve.scalar_tensor_tensor(out=res[:, t % 2, :], in0=x1[:, t, :], scalar=st[:, 3, t:t + 1],
                                         in1=nf[:], op0=ALU.mult, op1=ALU.mult).then_inc(res_s, 1)

            dve.wait_ge(par, 16)
            for t in range(TT):
                for k in range(2):
                    dve.wait_ge(got[t % 4][k], 16 * (t // 4 + 1))
                    if k:
                        dve.wait_ge(add, 2 * t + 1)
                    dve.scalar_tensor_tensor(out=x1[:, t, :], in0=rows[:, t % 4, k, :],
                                             scalar=rt["gate"][:, k, t:t + 1], in1=x1[:, t, :],
                                             op0=ALU.mult, op1=ALU.add).then_inc(add, 1)
                if t:
                    norm(t - 1)
            norm(TT - 1)

        @block.scalar
        def _(act):
            for t in range(TT):
                act.wait_ge(add, 2 * (t + 1))
                if t:
                    act.wait_ge(sqd, t)
                act.activation(sq[:], x1[:, t, :], ACT.Square, accum_out=st[:, 0, t:t + 1]).then_inc(sqd, 1)
                act.wait_ge(msd, t + 1)
                act.activation(st[:, 2, t:t + 1], st[:, 1, t:t + 1], ACT.Sqrt).then_inc(rtd, 1)


def hybrid_encoder(nc, a, out):
    h_dram = nc.dram_tensor("h_rows", [L, D], F32).ap()
    y_dram = nc.dram_tensor("expert_rows_dram", [(MAXB + 1) * P, D], F32).ap()
    with ExitStack() as whole:
        core = Core(nc, whole)
        c = constants(nc, core)
        filled = core.sem("expert_rows_filled")
        with ExitStack() as late:
            with ExitStack() as mixers:
                mc = Core(nc, mixers)
                with ExitStack() as st:
                    dc = Core(nc, st)
                    o = persistent(mc, dc)
                    with ExitStack() as s:
                        in_projection(nc, Core(nc, s), c, a, o)
                    o_sum = dc.sb("o_sum", [P, TT, DW])
                    tb = gate_tables(dc)
                    with ExitStack() as s:
                        gates(nc, Core(nc, s), c, a, o, tb, y_dram, filled)
                    with ExitStack() as s:
                        delta_net(nc, Core(nc, s), c, a, o, tb, o_sum)
                    ydn = o["qT"]
                    with ExitStack() as s:
                        gated_norm(nc, Core(nc, s), c, a, o_sum, o["zs"], ydn)
                ys5 = o["uT"][:].rearrange("p (k g) n -> p k (g n)", k=4)
                with ExitStack() as st:
                    s5t = s5_tables(Core(nc, st))
                    with ExitStack() as s:
                        s5_parameters(nc, Core(nc, s), c, a, s5t)
                    with ExitStack() as s:
                        s5_mixer(nc, Core(nc, s), c, a, o["uT"], s5t, ys5)
                lc = Core(nc, late)
                x1 = lc.sb("x1", [P, TT, D], side="right")
                logits = lc.sb("logits", [P, TT, NGRP + NEXP], side="right")
                with ExitStack() as s:
                    out_projection(nc, Core(nc, s), c, a, ys5, ydn, x1, logits, h_dram, filled)
            rt = router_tables(lc)
            with ExitStack() as s:
                router(nc, Core(nc, s), c, logits, rt)
            with ExitStack() as s:
                experts(nc, Core(nc, s), c, a, rt, h_dram, y_dram)
            with ExitStack() as s:
                combine(nc, Core(nc, s), c, a, x1, rt, y_dram, out)


_INS = ["x", "norm_mix", "w_in", "s5_lam_re", "s5_lam_im", "s5_log_dt", "s5_b_re", "s5_b_im", "s5_c_re", "s5_c_im",
        "s5_d", "s5_w_glu", "s5_b_glu", "gdn_conv_w", "gdn_a_log", "gdn_dt_bias", "gdn_norm_w", "w_out", "norm_ffn",
        "router_w_group", "router_b_group", "router_w_expert", "router_b_expert",
        "expert_w_gate", "expert_w_up", "expert_w_down", "norm_final"]


def kernel(**inputs):
    import numpy as np
    import concourse.bacc as bacc
    from concourse.bass_utils import run_bass_kernel_spmd

    nc = bacc.Bacc("TRN2", target_bir_lowering=False, num_devices=1)
    arrays, aps = {}, {}
    for name in _INS:
        arr = np.ascontiguousarray(inputs[name])
        arrays[f"in_{name}"] = arr
        aps[name] = nc.dram_tensor(f"in_{name}", arr.shape, mybir.dt.from_np(arr.dtype), kind="ExternalInput").ap()
    out = nc.dram_tensor("out", (1, L, D), F32, kind="ExternalOutput").ap()
    hybrid_encoder(nc, aps, out)
    r = run_bass_kernel_spmd(nc, [arrays], core_ids=[0])
    return r.results[0]["out"]
```

```python
from contextlib import ExitStack
import math

import concourse.bass as bass
from concourse import mybir

F32 = mybir.dt.float32
I32 = mybir.dt.int32
U32 = mybir.dt.uint32
ALU = mybir.AluOpType
ACT = mybir.ActivationFunctionType
AX = mybir.AxisListType

P = 128
D = 1024
L = 1024
KT = D // P
TT = L // P
H = 4
DH = 128
DW = H * DH
S5W = 512
NG = 32
GC = 16
NS = 64
T5 = 8
NC5 = L // T5
NP5 = NG // 2
IN_COLS = 2576
EPS = 1e-6
NEXP = 32
NGRP = 4
EPG = 8
DE = 512
MAXB = L * 2 // P + NEXP - 1
TWO_PI = 2.0 * math.pi
MAGIC = 1.5 * 2.0 ** 23
BIG = 1.0e30


class Steps:

    def __init__(self, eng, sem):
        self.eng, self.sem, self.n = eng, sem, 0

    def __call__(self, ins):
        self.n += 1
        ins.then_inc(self.sem, 1)
        return self.n

    def done(self, n=None):
        self.eng.wait_ge(self.sem, self.n if n is None else n)


class Core:

    def __init__(self, nc, stack):
        self.nc, self.stack, self.sems = nc, stack, []
        stack.callback(self.release)

    def sb(self, name, shape, dt=F32, side="left"):
        return self.stack.enter_context(self.nc.sbuf_tensor(name, shape, dt, side=side))

    def ps(self, name, shape, dt=F32):
        return self.stack.enter_context(self.nc.psum_tensor(name, shape, dt))

    def sem(self, name):
        self.sems.append(self.nc.alloc_semaphore(name))
        return self.sems[-1]

    def release(self):
        if self.sems:
            self.nc.clear_and_free_semaphores(self.sems)
            self.nc.all_engine_barrier()


def constants(core):
    c = {}
    c["ident"] = core.sb("ident", [P, P])
    c["ones"] = core.sb("ones", [P, P])
    c["upto"] = [core.sb("upto_f", [P, P]), core.sb("upto_b", [P, P])]
    c["level"] = [core.sb("level_f", [P, 7, P]), core.sb("level_b", [P, 7, P])]
    return c


def make_constants(pool, c, made):
    step = Steps(pool, made)
    step(pool.memset(c["ones"][:], 1.0))
    step.done()
    one = c["ones"][:]
    step(pool.affine_select(out=c["ident"][:], in_=one, compare_op=ALU.is_equal, fill=0.0, base=0,
                            pattern=[[1, P]], channel_multiplier=-1))
    step(pool.affine_select(out=c["upto"][0][:], in_=one, compare_op=ALU.is_ge, fill=0.0, base=0,
                            pattern=[[1, P]], channel_multiplier=-1))
    step(pool.affine_select(out=c["upto"][1][:], in_=one, compare_op=ALU.is_ge, fill=0.0, base=0,
                            pattern=[[-1, P]], channel_multiplier=1))
    for lv in range(7):
        s, n = 2 ** lv, P // 2 ** (lv + 1)
        for d in range(2):
            v = c["level"][d][:, lv, :].rearrange("p (m a s) -> p m a s", m=n, a=2)
            step(pool.memset(c["level"][d][:, lv, :], 0.0))
            step.done()
            half = v[:, :, d, :]
            ones = one.rearrange("p (m a s) -> p m a s", m=n, a=2)[:, :, 0, :]
            lo = s if d == 0 else 0
            step(pool.affine_select(out=half, in_=ones, compare_op=ALU.is_ge, fill=0.0, base=-lo,
                                    pattern=[[-2 * s, n], [0, s]], channel_multiplier=1))
            step.done()
            step(pool.affine_select(out=half, in_=half, compare_op=ALU.is_ge, fill=0.0, base=lo + s - 1,
                                    pattern=[[2 * s, n], [0, s]], channel_multiplier=-1))
            step.done()


def in_projection(nc, core, c, a, out, tb, y_dram, filled):
    kv, zs, uT, qT, kT = (out[n] for n in ("kv", "zs", "uT", "qT", "kT"))
    hT = core.sb("hT", [P, KT, L])
    wblk = core.sb("wblk", [P, 2, KT, 512])
    wab = core.sb("wab", [P, KT, 16])
    work = core.sb("conv_work", [P, 2 * (L + 4) + 2 * L])
    convin = work[:, 0:2 * (L + 4)].rearrange("p (a n) -> p a n", a=2)
    acc = work[:, 2 * (L + 4):].rearrange("p (a n) -> p a n", a=2)
    uS = work[:, 0:NG * T5 * GC].rearrange("p (g n) -> p g n", g=NG)
    act_t = core.sb("conv_silu", [P, L])
    sq = core.sb("square", [P, D])
    xs = kv[:].rearrange("p (t a) n -> p t (a n)", a=2)
    q_rows = uT[:].rearrange("p (t a) n -> p t (a n)", a=4)
    rows = [q_rows, kv[:, 0:TT], kv[:, TT:2 * TT]]
    ss = core.sb("x_ss", [P, TT])
    ms = core.sb("x_ms", [P, TT])
    rs = core.sb("x_rs", [P, TT])
    nss = core.sb("qk_ss", [P, 2, H, TT])
    nrt = core.sb("qk_rt", [P, 2, H, TT])
    nrs = core.sb("qk_rs", [P, 2, H, TT])
    normw = core.sb("norm_mix_w", [P, KT])
    cw = core.sb("conv_w", [P, 5, 12])
    mm_ps = core.ps("proj_ps", [P, 2, 2, 512])
    tr_ps = core.ps("turn_ps", [P, 2, 2, 512])

    made = core.sem("const_made")
    x_ld = [core.sem(f"x_ld{i}") for i in range(4)]
    par_ld = core.sem("par_ld")
    w_ld = [core.sem("w_ld0"), core.sem("w_ld1")]
    x_sq, x_ms, x_rt, x_h, x_tr, x_ev = (core.sem("x_" + n) for n in ("sq", "ms", "rt", "h", "tr", "ev"))
    dv = core.sem("proj_dve_step")
    pj = core.sem("projected")
    pj_ev = core.sem("projected_out")
    cv = core.sem("convolved")
    sl = core.sem("silu_done")
    tr = core.sem("tile_turned")
    tr_ev = core.sem("rows_out")
    sqd = core.sem("squared")
    red = core.sem("squares_summed")
    qk_ss, qk_rt = core.sem("qk_ss_done"), core.sem("qk_rt_done")
    nrm = core.sem("rows_normalised")
    qk_tr, qk_ev = core.sem("qk_turned"), core.sem("qk_out")
    x_rows = a["x"].rearrange("b (t p) d -> p (b t) d", p=P)
    w_in = a["w_in"][0].rearrange("(k p) n -> p k n", p=P)
    starts = [512, 1024, 1536, 0, 2048]
    NJ = 12
    AB = NJ + T5
    g = gates(core, c, a, out, tb, mm_ps[:, 0, 1, :])

    def turned_bank(n):
        return tr_ps[:, n // 2 % 2, n % 2, :]

    def turned_after(t):
        return range(4 * t, 4 * t + 4) if t < 4 else range(2 * TT + 2 * (t - 4), 2 * TT + 2 * (t - 4) + 2)

    with nc.Block() as block:
        @block.sync
        def _(sp):
            for i in range(4):
                sp.dma_start(xs[:, 2 * i:2 * i + 2], x_rows[:, 2 * i:2 * i + 2]).then_inc(x_ld[i], 16)
            with nc.allow_non_contiguous_dma(reason="small parameters"):
                sp.dma_start(normw[:], a["norm_mix"][0].rearrange("(k p) -> p k", p=P)).then_inc(par_ld, 16)
                for j in range(5):
                    sp.dma_start(cw[:, j, :], a["gdn_conv_w"][0, j].rearrange("(t p) -> p t", p=P)
                                 ).then_inc(par_ld, 16)
                sp.dma_start(wab[:], w_in[:, :, 2560:2576]).then_inc(par_ld, 16)
            for n in range(5):
                if n >= 2:
                    sp.wait_ge(pj, 4 * (n - 1))
                sp.dma_start(wblk[:, n % 2], w_in[:, :, starts[n]:starts[n] + 512]).then_inc(w_ld[n % 2], 16)
            g.sync(sp)
            sp.wait_ge(made, 1)
            fill_expert_rows(sp, c, y_dram, filled)

        @block.gpsimd
        def _(pool):
            make_constants(pool, c, made)

        @block.scalar
        def _(act):
            def silu(j):
                act.wait_ge(cv, j + 1)
                if j >= 1:
                    act.wait_ge(tr, j)
                act.activation(act_t[:], acc[:, j % 2, :], ACT.Silu).then_inc(sl, 1)

            def square(j):
                if j < 8:
                    act.wait_ge(tr_ev, j + 1)
                    if j >= 1:
                        act.wait_ge(red, j)
                    act.activation(sq[:].rearrange("p (t n) -> p t n", n=P),
                                   rows[j // 4][:, :, (j % 4) * P:(j % 4 + 1) * P], ACT.Square).then_inc(sqd, 1)

            def evacuate_x(half):
                for n in range(KT * half, KT * half + KT):
                    k = n % KT
                    act.wait_ge(x_tr, n + 1)
                    act.activation(hT[:, k, half * 512:half * 512 + 512], turned_bank(n), ACT.Copy,
                                   scale=normw[:, k:k + 1]).then_inc(x_ev, 1)

            for t in range(TT):
                act.wait_ge(x_ld[t // 2], 16)
                if t:
                    act.wait_ge(x_sq, t)
                act.activation(sq[:], xs[:, t, :], ACT.Square, accum_out=ss[:, t:t + 1]).then_inc(x_sq, 1)
                if t % 4 == 3:
                    act.wait_ge(x_ms, t // 4 + 1)
                    act.activation(rs[:, t - 3:t + 1], ms[:, t - 3:t + 1], ACT.Sqrt).then_inc(x_rt, 1)
            act.wait_ge(par_ld, 16 * 7)
            evacuate_x(0)
            evacuate_x(1)
            for j in range(NJ):
                if j >= 1:
                    silu(j - 1)
                if j >= 3:
                    square(j - 3)
                act.wait_ge(pj, j + 1)
                if j < 2:
                    act.wait_ge(dv, 2)
                else:
                    act.wait_ge(cv, j - 1)
                act.activation(convin[:, j % 2, 2:2 + L], mm_ps[:, j % 2].rearrange("p a n -> p (a n)"),
                               ACT.Copy).then_inc(pj_ev, 1)
            silu(NJ - 1)
            act.wait_ge(qk_ss, 1)
            act.activation(nrt[:], nss[:], ACT.Sqrt).then_inc(qk_rt, 1)
            act.wait_ge(sl, NJ)
            for t in range(T5):
                act.wait_ge(pj, NJ + t + 1)
                act.activation(uS[:, :, t * GC:(t + 1) * GC],
                               mm_ps[:, t % 2, 0, :].rearrange("p (g q) -> p g q", q=GC), ACT.Copy
                               ).then_inc(pj_ev, 1)
            act.wait_ge(pj, AB + 1)
            act.activation(out["ab"][:].rearrange("p t n -> p (t n)"), mm_ps[:, 0, 0, 0:TT * 16], ACT.Copy
                           ).then_inc(pj_ev, 1)
            act.wait_ge(pj_ev, AB + 1)
            g.softplus(act)
            for t in range(TT):
                act.wait_ge(pj, AB + 2 + t)
                act.activation(zs[:, t, :], mm_ps[:, (t + 1) % 2, 0, :], ACT.Silu).then_inc(pj_ev, 1)
                for n in turned_after(t):
                    act.wait_ge(qk_tr, n + 1)
                    if n < 2 * TT:
                        dst = (qT, kT)[n % 2]
                        act.activation(dst[:, :, (n // 2) * P:(n // 2 + 1) * P],
                                       turned_bank(n).rearrange("p (h n) -> p h n", h=H), ACT.Copy
                                       ).then_inc(qk_ev, 1)
                    else:
                        m = n - 2 * TT
                        act.activation(uT[:, 4 * m:4 * m + 4, :],
                                       turned_bank(n).rearrange("p (g n) -> p g n", g=4), ACT.Copy
                                       ).then_inc(qk_ev, 1)
                if t == 1:
                    g.factors(act)

        @block.tensor
        def _(pe):
            pe.wait_ge(made, 2)
            for n in range(2 * KT):
                half, k = n // KT, n % KT
                pe.wait_ge(x_h, 4 * half + 4)
                if n >= 4:
                    pe.wait_ge(x_ev, n - 3)
                for t in range(4):
                    mm = pe.transpose(turned_bank(n)[:, t * P:(t + 1) * P],
                                      xs[:, 4 * half + t, k * P:(k + 1) * P], c["ident"][:])
                mm.then_inc(x_tr, 1)
            pe.wait_ge(x_ev, 2 * KT)

            def turn(j):
                pe.wait_ge(sl, j + 1)
                if j >= 2:
                    pe.wait_ge(tr_ev, j - 1)
                for t in range(TT):
                    mm = pe.transpose(tr_ps[:, j % 2, t // 4, (t % 4) * P:(t % 4 + 1) * P],
                                      act_t[:, t * P:(t + 1) * P], c["ident"][:])
                mm.then_inc(tr, 1)

            for j in range(NJ):
                blk = j // 4
                if j % 4 == 0:
                    pe.wait_ge(w_ld[blk % 2], 16 * (blk // 2 + 1))
                if j >= 2:
                    pe.wait_ge(pj_ev, j - 1)
                for half in range(2):
                    for k in range(KT):
                        mm = pe.matmul(mm_ps[:, j % 2, half, :], wblk[:, blk % 2, k, (j % 4) * P:(j % 4 + 1) * P],
                                       hT[:, k, half * 512:half * 512 + 512], start=k == 0, stop=k == KT - 1)
                mm.then_inc(pj, 1)
                if j >= 1:
                    turn(j - 1)
            pe.wait_ge(w_ld[1], 32)
            for t in range(T5):
                pe.wait_ge(pj_ev, NJ + t - 1)
                for k in range(KT):
                    mm = pe.matmul(mm_ps[:, t % 2, 0, :], hT[:, k, t:L:T5], wblk[:, 1, k, :],
                                   start=k == 0, stop=k == KT - 1)
                mm.then_inc(pj, 1)
                if t == 0:
                    turn(NJ - 1)
            pe.wait_ge(par_ld, 16 * 7)
            pe.wait_ge(pj_ev, AB - 1)
            for t in range(TT):
                for k in range(KT):
                    mm = pe.matmul(mm_ps[:, 0, 0, t * 16:t * 16 + 16], hT[:, k, t * P:(t + 1) * P], wab[:, k, :],
                                   start=k == 0, stop=k == KT - 1)
            mm.then_inc(pj, 1)
            pe.wait_ge(w_ld[0], 48)
            for t in range(TT):
                pe.wait_ge(pj_ev, AB + t)
                for k in range(KT):
                    mm = pe.matmul(mm_ps[:, (t + 1) % 2, 0, :], hT[:, k, t * P:(t + 1) * P], wblk[:, 0, k, :],
                                   start=k == 0, stop=k == KT - 1)
                mm.then_inc(pj, 1)
                if t == 0:
                    pe.wait_ge(tr_ev, NJ)
                    pe.wait_ge(pj_ev, AB)
                if t == 1:
                    pe.wait_ge(made, 4)
                    g.sums(pe)
                for n in turned_after(t):
                    if n >= 4:
                        pe.wait_ge(qk_ev, n - 3)
                    if n < 2 * TT:
                        pe.wait_ge(nrm, n + 1)
                    for h in range(H):
                        src = rows[n % 2][:, n // 2, h * P:(h + 1) * P] if n < 2 * TT else uS[:, 4 * (n - 2 * TT) + h, :]
                        mm = pe.transpose(turned_bank(n)[:, h * P:(h + 1) * P], src, c["ident"][:])
                    mm.then_inc(qk_tr, 1)

        @block.vector
        def _(dve):
            step = Steps(dve, dv)
            step(dve.memset(convin[:, :, 0:2], 0.0))
            step(dve.memset(convin[:, :, L + 2:L + 4], 0.0))
            for half in range(2):
                ts = slice(4 * half, 4 * half + 4)
                dve.wait_ge(x_sq, 4 * half + 4)
                dve.tensor_scalar(ms[:, ts], ss[:, ts], 1.0 / D, EPS, ALU.mult, ALU.add).then_inc(x_ms, 1)
                dve.wait_ge(x_rt, half + 1)
                step(dve.reciprocal(ms[:, ts], rs[:, ts]))
                step.done()
                for t in range(4 * half, 4 * half + 4):
                    dve.tensor_scalar(xs[:, t, :], xs[:, t, :], ms[:, t:t + 1], None, ALU.mult).then_inc(x_h, 1)

            def rows_out(j):
                dve.wait_ge(tr, j + 1)
                if j == 0:
                    dve.wait_ge(x_tr, 2 * KT)
                dve.tensor_copy(rows[j // 4][:, :, (j % 4) * P:(j % 4 + 1) * P],
                                tr_ps[:, j % 2].rearrange("p a (t n) -> p (a t) n", n=P)).then_inc(tr_ev, 1)

            def sum_squares(j):
                if 0 <= j < 8:
                    dve.wait_ge(sqd, j + 1)
                    dve.tensor_reduce(nss[:, j // 4, j % 4, :], sq[:].rearrange("p (t n) -> p t n", n=P),
                                      AX.X, ALU.add).then_inc(red, 1)

            for j in range(NJ):
                dve.wait_ge(pj_ev, j + 1)
                if j >= 2:
                    dve.wait_ge(sl, j - 1)
                src = convin[:, j % 2, :]
                step(dve.tensor_scalar(acc[:, j % 2, :], src[:, 0:L], cw[:, 0, j:j + 1], None, ALU.mult))
                for tap in range(1, 5):
                    step.done()
                    ins = dve.scalar_tensor_tensor(out=acc[:, j % 2, :], in0=src[:, tap:tap + L],
                                                   scalar=cw[:, tap, j:j + 1], in1=acc[:, j % 2, :],
                                                   op0=ALU.mult, op1=ALU.add)
                    if tap < 4:
                        step(ins)
                ins.then_inc(cv, 1)
                if j >= 2:
                    rows_out(j - 2)
                    sum_squares(j - 3)
            rows_out(NJ - 2)
            dve.wait_ge(red, 8)
            dve.tensor_scalar(nss[:], nss[:], EPS, None, ALU.add).then_inc(qk_ss, 1)
            rows_out(NJ - 1)
            dve.wait_ge(qk_rt, 1)
            step(dve.reciprocal(nrs[:], nrt[:]))
            step.done()
            step(dve.tensor_scalar(nrs[:, 0], nrs[:, 0], DH ** -0.5, None, ALU.mult))
            step.done()
            dve.wait_ge(tr_ev, NJ)
            dve.wait_ge(pj_ev, AB + 1)
            g.decays(dve)
            for n in range(2 * TT):
                t = n // 2
                if n == 8:
                    g.totals(dve)
                view = rows[n % 2][:, t, :].rearrange("p (h d) -> p h d", h=H)
                scale = nrs[:, n % 2, :, t:t + 1].broadcast_to([P, H, DH])
                dve.tensor_tensor(view, view, scale, ALU.mult).then_inc(nrm, 1)


def persistent(low, core):
    return {
        "uT": low.sb("uT", [P, NG, NC5]),
        "qT": low.sb("qT", [P, H, L]),
        "kT": core.sb("kT", [P, H, L]),
        "kv": core.sb("kv_rows", [P, 2 * TT, DW]),
        "zs": core.sb("silu_z", [P, TT, DW]),
        "ab": core.sb("ab", [P, TT, 16]),
    }


def fill_expert_rows(sp, c, y_dram, filled):
    n = L * 2 // P
    rows = y_dram[n * P:, :].rearrange("(b p) (r c) -> p b r c", p=P, c=P)
    for b in range(rows.shape[1]):
        ones = c["ones"][:].rearrange("p (r c) -> p r c", r=1).broadcast_to([P, D // P, P])
        sp.dma_start(rows[:, b], ones).then_inc(filled, 16)


class gates:

    def __init__(self, core, c, a, out, tb, bank):
        self.c, self.a, self.tb, self.bank = c, a, tb, bank
        self.par = core.sb("gate_par", [P, 2, 8])
        self.t1 = core.sb("gate_t1", [P, TT, 8])
        self.t2 = core.sb("gate_t2", [P, TT, 8])
        self.t3 = core.sb("gate_t3", [P, TT, 8])
        self.ld, self.v, self.s, self.m = (core.sem("gate_" + n) for n in ("ld", "dve", "act", "pe"))
        self.xa, self.xb = out["ab"][:, :, 0:8], out["ab"][:, :, 8:16]

    def sync(self, sp):
        for i, name in enumerate(("gdn_dt_bias", "gdn_a_log")):
            sp.dma_start(self.par[:, i, :], self.a[name].rearrange("o d h -> o (d h)").partition_broadcast(P)
                         ).then_inc(self.ld, 16)

    def decays(self, dve):
        t1, par, s = self.t1, self.par, self.s
        self.step = step = Steps(dve, self.v)
        dve.wait_ge(self.ld, 32)
        bias = par[:, 0:1, :].broadcast_to([P, TT, 8])
        step(dve.tensor_tensor(t1[:], self.xa, bias, ALU.add))
        dve.wait_ge(s, 4)
        step(dve.tensor_scalar(t1[:], t1[:], 0.0, None, ALU.max))
        step.done()
        step(dve.tensor_tensor(t1[:], t1[:], self.t2[:], ALU.add))
        step.done()
        step(dve.scalar_tensor_tensor(out=self.tb["g"][:], in0=t1[:], scalar=-1.0,
                                      in1=par[:, 1:2, :].broadcast_to([P, TT, 8]),
                                      op0=ALU.mult, op1=ALU.mult))

    def totals(self, dve):
        tb, step, bank = self.tb, self.step, self.bank
        dve.wait_ge(self.m, 1)
        step(dve.tensor_copy(tb["G"][:, :, 0:4], bank[:, 0:32].rearrange("p (t h) -> p t h", h=4)))
        step(dve.tensor_copy(tb["G"][:, :, 4:8], bank[:, 32:64].rearrange("p (t h) -> p t h", h=4)))
        step(dve.tensor_copy(self.t2[:], bank[:, 64:128].rearrange("p (t h) -> p t h", h=8)))
        step.done()
        step(dve.tensor_tensor(self.t3[:], self.t2[:], tb["G"][:], ALU.subtract))
        dve.wait_ge(self.s, 6)
        step(dve.tensor_tensor(tb["betaG"][:], tb["beta"][:], tb["eG"][:], ALU.mult))

    def softplus(self, act):
        t1, t2, par, s = self.t1, self.t2, self.par, self.s
        act.wait_ge(self.v, 1)
        act.activation(t2[:], t1[:], ACT.Abs).then_inc(s, 1)
        act.wait_ge(s, 1)
        act.activation(t2[:], t2[:], ACT.Exp, scale=-1.0).then_inc(s, 1)
        act.wait_ge(s, 2)
        act.activation(t2[:], t2[:], ACT.Ln, bias=1.0).then_inc(s, 1)
        act.activation(par[:, 1, :], par[:, 1, :], ACT.Exp).then_inc(s, 1)
        act.activation(self.tb["beta"][:], self.xb, ACT.Sigmoid).then_inc(s, 1)

    def factors(self, act):
        tb, s = self.tb, self.s
        act.wait_ge(self.v, 8)
        act.activation(tb["eG"][:], tb["G"][:], ACT.Exp).then_inc(s, 1)
        act.activation(tb["eTot"][:], self.t2[:], ACT.Exp)
        act.activation(tb["kdec"][:], self.t3[:], ACT.Exp).then_inc(s, 1)

    def sums(self, pe):
        g = self.tb["g"]
        pe.wait_ge(self.v, 4)
        for d in range(2):
            pe.matmul(self.bank[:, 32 * d:32 * d + 32], self.c["upto"][d][:], g[:, :, 4 * d:4 * d + 4],
                      start=True, stop=True)
        pe.matmul(self.bank[:, 64:128], self.c["ones"][:], g[:].rearrange("p t h -> p (t h)"),
                  start=True, stop=True).then_inc(self.m, 1)


def gate_tables(core):
    return {n: core.sb("tab_" + n, [P, TT, 8]) for n in ("g", "G", "beta", "eG", "eTot", "kdec", "betaG")}


def delta_schedule():
    prepare = ["decay", "scores", "first"]
    for t in range(-1, TT + 1):
        if t < 0:
            steps = [(name, 0, 0) for name in prepare]
        elif t == TT:
            steps = [("read_state", 0, t - 1), ("new_state", 0, t - 1)]
        else:
            steps = []
            for lv in range(1, 7):
                steps.append(("z", lv, t))
                if lv <= 2 and t >= 1:
                    steps.append((("read_state", "new_state")[lv - 1], 0, t - 1))
                if 3 <= lv <= 5 and t + 1 < TT:
                    steps.append((prepare[lv - 3], 0, t + 1))
                steps.append(("d", lv, t))
                if lv < 6:
                    steps.append(("turn", lv, t))
            steps.append(("solve", 0, t))
        for name, lv, at in steps:
            for d in range(2):
                yield name, lv, at, d


def delta_net(nc, core, c, a, out, tb, o_sum):
    qT, kT, kv = out["qT"], out["kT"], out["kv"]

    def buf(name, n=1):
        return [core.sb(f"{name}{d}", [P, n, H, P]) for d in range(2)]

    e_b, ab_b, as_b, t_b, tt_b, z_b = (buf("decay"), buf("amat", 2), buf("alev", 2), buf("T", 2), buf("TT", 2),
                                       buf("zc"))
    at_b, u_b, w_b, vb_b, kbg_b, kd_b = buf("attn", 2), buf("u"), buf("wT"), buf("vb"), buf("kbg"), buf("kdec")
    vn_b, tmp_b, s_b, sd_b = buf("vnew"), buf("otmp"), buf("state"), buf("state_dec")
    X = [core.ps(f"bank_x{d}", [P, H, P]) for d in range(2)]
    Y = [core.ps(f"bank_y{d}", [P, H, P]) for d in range(2)]
    V = [core.ps(f"bank_v{d}", [P, H, P]) for d in range(2)]
    O = [core.ps(f"bank_o{d}", [P, H, P]) for d in range(2)]
    names = ("gsum kk kq diff absd decay masked betad amat attn alev t_first tt_first tt0 tt z zc dd turned t "
             "u_mm w_mm u w vb kbg kd ws qs vnew o_part av kv o o_added s_dec state tmp0").split()
    S = {n: [core.sem(f"dn_{n}{d}") for d in range(2)] for n in names}

    def chunk(t, d):
        return t if d == 0 else TT - 1 - t

    def cols(t, d):
        ch = chunk(t, d)
        return slice(ch * P, ch * P + P)

    def per_head(table, t, d):
        return table[:, chunk(t, d), 4 * d:4 * d + 4].rearrange("p (h o) -> p h o", o=1).broadcast_to([P, H, P])

    def rows(which, t, d):
        return kv[:, which * TT + chunk(t, d), :].rearrange("p (h n) -> p h n", h=H)

    def over_heads(m):
        return m.rearrange("p (o n) -> p o n", o=1).broadcast_to([P, H, P])

    with nc.Block() as block:
        @block.tensor
        def _(pe):
            def wait(name, d, n):
                if n > 0:
                    pe.wait_ge(S[name][d], n)

            def heads(dst, lhs, rhs):
                for h in range(H):
                    mm = pe.matmul(dst[:, h, :], lhs(h), rhs(h), start=True, stop=True)
                return mm

            for name, lv, t, d in delta_schedule():
                cs, b = cols(t, d), t % 2
                if name == "decay":
                    wait("o", d, t - 1)
                    heads(V[d], lambda h: tb["g"][:, chunk(t, d), 4 * d + h:4 * d + h + 1].broadcast_to([P, P]),
                          lambda h: c["upto"][d][:]).then_inc(S["gsum"][d], 1)
                    wait("state", d, t)
                    heads(O[d], lambda h: kT[:, h, cs], lambda h: kT[:, h, cs]).then_inc(S["kk"][d], 1)
                elif name == "scores":
                    wait("diff", d, t + 1)
                    heads(V[d], lambda h: kT[:, h, cs], lambda h: qT[:, h, cs]).then_inc(S["kq"][d], 1)
                elif name == "first":
                    wait("t_first", d, t + 1)
                    wait("amat", d, t + 1)
                    for h in range(H):
                        mm = pe.transpose(O[d][:, h, :], t_b[d][:, b, h, :], c["ident"][:])
                    mm.then_inc(S["tt_first"][d], 1)
                elif name == "z":
                    wait("alev", d, 6 * t + lv)
                    if lv == 1:
                        wait("tt0", d, t + 1)
                        wait("u", d, t)
                    else:
                        wait("tt", d, 6 * t + lv - 1)
                        wait("t", d, 5 * t + lv - 1)
                    heads(X[d], lambda h: as_b[d][:, (lv - 1) % 2, h, :], lambda h: tt_b[d][:, b, h, :]
                          ).then_inc(S["z"][d], 1)
                elif name == "d":
                    wait("zc", d, 6 * t + lv)
                    if lv == 1:
                        wait("w", d, t)
                    heads(Y[d], lambda h: t_b[d][:, b, h, :], lambda h: z_b[d][:, 0, h, :]
                          ).then_inc(S["dd"][d], 1)
                elif name == "turn":
                    wait("tt", d, 6 * t + lv)
                    for h in range(H):
                        mm = pe.transpose(X[d][:, h, :], tt_b[d][:, b, h, :], c["ident"][:])
                    mm.then_inc(S["turned"][d], 1)
                elif name == "solve":
                    wait("tt", d, 6 * t + 6)
                    wait("vb", d, t + 1)
                    heads(X[d], lambda h: tt_b[d][:, b, h, :], lambda h: vb_b[d][:, 0, h, :]
                          ).then_inc(S["u_mm"][d], 1)
                    wait("kbg", d, t + 1)
                    heads(Y[d], lambda h: kbg_b[d][:, 0, h, :], lambda h: tt_b[d][:, b, h, :]
                          ).then_inc(S["w_mm"][d], 1)
                elif name == "read_state":
                    wait("w", d, t + 1)
                    wait("state", d, t + 1)
                    wait("attn", d, min(t + 2, TT))
                    heads(V[d], lambda h: w_b[d][:, 0, h, :], lambda h: s_b[d][:, 0, h, :]).then_inc(S["ws"][d], 1)
                    wait("tt0", d, min(t + 2, TT))
                    heads(O[d], lambda h: qT[:, h, cs], lambda h: s_b[d][:, 0, h, :]).then_inc(S["qs"][d], 1)
                elif name == "new_state":
                    wait("vnew", d, t + 1)
                    heads(V[d], lambda h: at_b[d][:, t % 2, h, :], lambda h: vn_b[d][:, 0, h, :]
                          ).then_inc(S["av"][d], 1)
                    wait("o_part", d, t + 1)
                    wait("kd", d, t + 1)
                    heads(O[d], lambda h: kd_b[d][:, 0, h, :], lambda h: vn_b[d][:, 0, h, :]
                          ).then_inc(S["kv"][d], 1)

        @block.vector
        def _(dve):
            def wait(name, d, n):
                if n > 0:
                    dve.wait_ge(S[name][d], n)

            for d in range(2):
                dve.memset(s_b[d][:], 0.0).then_inc(S["state"][d], 1)
            for name, lv, t, d in delta_schedule():
                ch, b = chunk(t, d), t % 2
                if name == "decay":
                    wait("gsum", d, t + 1)
                    wait("betad", d, t)
                    dve.tensor_tensor(e_b[d][:, 0], per_head(tb["G"], t, d), V[d][:], ALU.subtract
                                      ).then_inc(S["diff"][d], 1)
                elif name == "scores":
                    wait("kk", d, t + 1)
                    wait("betad", d, t + 1)
                    dve.tensor_tensor(ab_b[d][:, b], O[d][:], ab_b[d][:, b], ALU.mult).then_inc(S["amat"][d], 1)
                    wait("amat", d, t + 1)
                    wait("dd", d, 6 * (t - 1))
                    dve.tensor_tensor(t_b[d][:, b], ab_b[d][:, b], over_heads(c["level"][d][:, 0, :]), ALU.mult
                                      ).then_inc(S["tmp0"][d], 1)
                    wait("tmp0", d, t + 1)
                    dve.tensor_tensor(t_b[d][:, b], over_heads(c["ident"][:]), t_b[d][:, b], ALU.subtract
                                      ).then_inc(S["t_first"][d], 1)
                    wait("kq", d, t + 1)
                    wait("masked", d, t + 1)
                    dve.tensor_tensor(at_b[d][:, b], V[d][:], at_b[d][:, b], ALU.mult).then_inc(S["attn"][d], 1)
                elif name == "first":
                    wait("tt_first", d, t + 1)
                    wait("w_mm", d, t - 1)
                    dve.tensor_copy(tt_b[d][:, b], O[d][:]).then_inc(S["tt0"][d], 1)
                elif name == "d":
                    wait("dd", d, 6 * t + lv)
                    if lv == 1:
                        wait("tt0", d, t + 1)
                    else:
                        wait("tt", d, 6 * t + lv - 1)
                    dve.tensor_tensor(tt_b[d][:, b], tt_b[d][:, b], Y[d][:], ALU.subtract).then_inc(S["tt"][d], 1)
                elif name == "read_state":
                    wait("ws", d, t + 1)
                    wait("u", d, t + 1)
                    dve.tensor_tensor(vn_b[d][:, 0], u_b[d][:, 0], V[d][:], ALU.subtract).then_inc(S["vnew"][d], 1)
                    wait("qs", d, t + 1)
                    wait("o", d, t)
                    wait("o_added", d, t - 4)
                    dve.tensor_tensor(tmp_b[d][:, 0], O[d][:], per_head(tb["eG"], t, d), ALU.mult
                                      ).then_inc(S["o_part"][d], 1)
                elif name == "new_state":
                    wait("av", d, t + 1)
                    wait("o_part", d, t + 1)
                    dst = o_sum[:, ch, :].rearrange("p (h n) -> p h n", h=H) if t < TT // 2 else tmp_b[d][:, 0]
                    dve.tensor_tensor(dst, tmp_b[d][:, 0], V[d][:], ALU.add).then_inc(S["o"][d], 1)
                    wait("kv", d, t + 1)
                    wait("s_dec", d, t + 1)
                    dve.tensor_tensor(s_b[d][:, 0], sd_b[d][:, 0], O[d][:], ALU.add).then_inc(S["state"][d], 1)

        @block.scalar
        def _(act):
            def wait(name, d, n):
                if n > 0:
                    act.wait_ge(S[name][d], n)

            for name, lv, t, d in delta_schedule():
                if name == "decay":
                    wait("diff", d, t + 1)
                    act.activation(e_b[d][:, 0], e_b[d][:, 0], ACT.Abs).then_inc(S["absd"][d], 1)
                    wait("absd", d, t + 1)
                    act.activation(e_b[d][:, 0], e_b[d][:, 0], ACT.Exp, scale=-1.0).then_inc(S["decay"][d], 1)
                elif name == "z":
                    wait("z", d, 6 * t + lv)
                    act.activation(z_b[d][:, 0], X[d][:], ACT.Copy).then_inc(S["zc"][d], 1)
                elif name == "turn":
                    wait("turned", d, 5 * t + lv)
                    act.activation(t_b[d][:, t % 2], X[d][:], ACT.Copy).then_inc(S["t"][d], 1)
                elif name == "solve":
                    wait("u_mm", d, t + 1)
                    wait("vnew", d, t)
                    act.activation(u_b[d][:, 0], X[d][:], ACT.Copy).then_inc(S["u"][d], 1)
                    wait("w_mm", d, t + 1)
                    act.activation(w_b[d][:, 0], Y[d][:], ACT.Copy).then_inc(S["w"][d], 1)

        @block.gpsimd
        def _(pool):
            def wait(name, d, n):
                if n > 0:
                    pool.wait_ge(S[name][d], n)

            def level(t, lv, d):
                wait("amat", d, t + 1)
                wait("z", d, 6 * t + lv - 2)
                pool.tensor_tensor(as_b[d][:, lv % 2 ^ 1], ab_b[d][:, t % 2], over_heads(c["level"][d][:, lv, :]),
                                   ALU.mult).then_inc(S["alev"][d], 1)

            for name, lv, t, d in delta_schedule():
                ch = chunk(t, d)
                if name == "decay":
                    wait("decay", d, t + 1)
                    wait("av", d, t - 1)
                    pool.tensor_tensor(at_b[d][:, t % 2], e_b[d][:, 0], over_heads(c["upto"][d][:]), ALU.mult
                                       ).then_inc(S["masked"][d], 1)
                    wait("alev", d, 6 * (t - 1))
                    pool.tensor_tensor(ab_b[d][:, t % 2], e_b[d][:, 0], per_head(tb["beta"], t, d), ALU.mult
                                       ).then_inc(S["betad"][d], 1)
                elif name == "first" and t == 0:
                    level(0, 1, d)
                    level(0, 2, d)
                elif name == "z":
                    if lv <= 4:
                        level(t, lv + 2, d)
                    elif t + 1 < TT:
                        level(t + 1, lv - 4, d)
                    if lv == 3:
                        wait("u_mm", d, t)
                        pool.tensor_tensor(vb_b[d][:, 0], rows(1, t, d), per_head(tb["beta"], t, d), ALU.mult
                                           ).then_inc(S["vb"][d], 1)
                    elif lv == 4:
                        wait("w_mm", d, t)
                        pool.tensor_tensor(kbg_b[d][:, 0], rows(0, t, d), per_head(tb["betaG"], t, d), ALU.mult
                                           ).then_inc(S["kbg"][d], 1)
                elif name == "read_state":
                    wait("kv", d, t)
                    pool.tensor_tensor(kd_b[d][:, 0], rows(0, t, d), per_head(tb["kdec"], t, d), ALU.mult
                                       ).then_inc(S["kd"][d], 1)
                    wait("state", d, t + 1)
                    pool.tensor_tensor(sd_b[d][:, 0], s_b[d][:, 0], per_head(tb["eTot"], t, d), ALU.mult
                                       ).then_inc(S["s_dec"][d], 1)
                elif name == "new_state" and t >= TT // 2:
                    wait("o", d, t + 1)
                    wait("o", 1 - d, TT - t)
                    acc = o_sum[:, ch, :].rearrange("p (h n) -> p h n", h=H)
                    pool.tensor_tensor(acc, acc, tmp_b[d][:, 0], ALU.add).then_inc(S["o_added"][d], 1)


def s5_tables(core):
    return {
        "E": core.sb("s5_E", [P, 2 * NP5, 2, P]),
        "G": core.sb("s5_G", [P, 2, 2 * NP5, T5 + 1, GC]),
        "M": core.sb("s5_M", [P, NG, P]),
        "cos": core.sb("s5_cos", [P, 2 * NP5, NC5]),
        "sin": core.sb("s5_sin", [P, 2 * NP5, NC5]),
        "rho": core.sb("s5_rho", [P, 2 * NP5]),
    }


def s5_parameters(nc, core, c, a, tb):
    DJ = 2 * NP5
    raw = core.sb("s5_raw", [DJ, 3, P])
    ldt = core.sb("s5_ldt", [DJ, 2])
    lam = core.sb("s5_lam", [P, 3, DJ])
    BC = core.sb("s5_BC_in", [P, 2 * DJ * 2 * GC])
    B = BC[:, 0:2 * DJ * GC].rearrange("p (i j q) -> p i j q", i=2, j=DJ)
    Cn = BC[:, 2 * DJ * GC:].rearrange("p (i n) -> p i n", i=8)
    BD = BC[:].rearrange("p (i j q) -> p i j q", i=2, j=DJ)
    Bb = core.sb("s5_Bbar", [P, 2, DJ, GC])
    C = core.sb("s5_C", [P, 2, DJ, GC])
    s = core.sb("s5_small", [P, 20, DJ])
    pw = core.sb("s5_powers", [P, 2, T5 + 1, DJ])
    scr = core.sb("s5_scratch", [P, 6144])
    Dc = core.sb("s5_dcol", [2 * GC, NP5])
    dm = core.sb("s5_dmask", [2 * GC, GC])
    ramp = core.sb("s5_ramp", [P, NC5])
    ps = core.ps("s5_ps", [P, 4, 512])
    ld, v, g, acts, m, ev, mv, kd = (core.sem("s5p_" + n) for n in
                                     ("ld", "dve", "pool", "act", "pe", "out", "kcopy", "kmove"))
    (RE, IM, LD, DTC, AR, TH, TN, EM, EE, SN, SH, DR, DI, MM, T1, T2, QR, QI, TAU, HALF) = range(20)
    made = {n: core.sem("s5p_made_" + n) for n in ("ar", "theta", "turns", "E", "BD")}
    E, G = tb["E"], tb["G"]
    KKn = 2 * T5 - 1
    mv2 = core.sem("s5p_kbank_out")

    def EB(ri):
        return scr[:, 2048 * ri:2048 * ri + 2048].rearrange("p (j n) -> p j n", j=NP5)

    KK = scr[0:2 * GC, 0:NP5 * KKn * GC].rearrange("p (j k q) -> p j k q", j=NP5, k=KKn)

    with nc.Block() as block:
        @block.sync
        def _(sp):
            for i, n in enumerate(("s5_lam_re", "s5_lam_im")):
                sp.dma_start(raw[:, i, :], a[n][0].rearrange("d (j a) n -> (d j) (a n)", a=2)).then_inc(ld, 16)
            with nc.allow_non_contiguous_dma(reason="small parameters"):
                sp.dma_start(ldt[:], a["s5_log_dt"][0].rearrange("d (j a) -> (d j) a", a=2)).then_inc(ld, 16)
                sp.dma_start(Dc[:], a["s5_d"][0].rearrange("(j r) -> r j", r=2 * GC)).then_inc(ld, 16)
                for i, n in enumerate(("s5_b_re", "s5_b_im")):
                    sp.dma_start(B[:, i], a[n][0].rearrange("d (j a) n q -> (a n) (d j) q", a=2)).then_inc(ld, 16)
                for i, n in enumerate(("s5_c_re", "s5_c_im")):
                    for d in range(2):
                        for half in range(2):
                            src = a[n][0, d].rearrange("(h j a) p n -> h j p a n", h=2, a=2)[half]
                            for j in range(8):
                                sp.dma_start(Cn[j * GC:(j + 1) * GC, 4 * i + 2 * d + half, :]
                                             .rearrange("p (a n) -> p a n", a=2), src[j]).then_inc(ld, 16)

            sp.wait_ge(mv, 1)
            with nc.allow_non_contiguous_dma(reason="rows of 512 bytes"):
                for t in range(T5):
                    for h in range(2):
                        sp.dma_start(
                            tb["M"][t * GC:(t + 1) * GC].rearrange("p (j a) n -> p j a n", a=2)[:, :, h, :],
                            KK[h * GC:(h + 1) * GC, :, T5 - 1 - t:2 * T5 - 1 - t, :].rearrange("p j k q -> p j (k q)")
                        ).then_inc(kd, 16)
            sp.wait_ge(kd, 16 * 2 * T5)

        @block.gpsimd
        def _(pool):
            pool.iota(ramp[:], [[1, NC5]], base=0, channel_multiplier=0,
                      allow_small_or_imprecise_dtypes=True).then_inc(g, 1)
            pool.wait_ge(made["turns"], 1)
            pool.wait_ge(m, 3)
            pool.memset(BD[:], 0.0).then_inc(g, 1)

        @block.scalar
        def _(act):
            act.wait_ge(m, 1)
            act.activation(lam[:].rearrange("p i n -> p (i n)"), ps[:, 0, 0:3 * DJ], ACT.Copy).then_inc(acts, 1)
            act.wait_ge(acts, 1)
            act.activation(s[:, DTC], lam[:, 2], ACT.Exp).then_inc(acts, 1)
            act.wait_ge(made["ar"], 1)
            act.activation(s[:, TN], s[:, AR], ACT.Tanh, scale=0.5).then_inc(acts, 1)
            act.wait_ge(made["theta"], 1)
            act.activation(s[:, SN], s[:, TH], ACT.Sin).then_inc(acts, 1)
            act.activation(s[:, SH], s[:, TH], ACT.Sin, scale=0.5).then_inc(acts, 1)
            for i in range(8):
                act.wait_ge(m, 2 + i // 4)
                ri, d, half = i // 4, (i // 2) % 2, i % 2
                dj = NP5 * d + 8 * half
                act.activation(C[:, ri, dj:dj + 8, :], ps[:, 1 + i // 4, (i % 4) * P:(i % 4 + 1) * P]
                               .rearrange("p (j q) -> p j q", q=GC), ACT.Copy).then_inc(ev, 1)
            act.wait_ge(made["turns"], 1)
            act.activation(tb["cos"][:], tb["sin"][:], ACT.Abs).then_inc(acts, 1)
            act.wait_ge(acts, 6)
            act.activation(tb["sin"][:], tb["sin"][:], ACT.Sin, scale=6.283185).then_inc(acts, 1)
            act.activation(tb["cos"][:], tb["cos"][:], ACT.Sin, scale=-6.283185, bias=s[:, HALF, 0:1]
                           ).then_inc(acts, 1)
            for n in range(16):
                act.wait_ge(m, 3 + n + 1)
                act.activation(E[:, 2 * n:2 * n + 2].rearrange("p j r n -> p (j r n)"), ps[:, n % 2, :], ACT.Copy
                               ).then_inc(ev, 1)

        @block.tensor
        def _(pe):
            pe.wait_ge(ld, 16 * 70)
            pe.wait_ge(v, 1)
            for i in range(3):
                mm = pe.transpose(ps[:, 0, i * DJ:(i + 1) * DJ], raw[:, i, :], c["ident"][0:DJ, 0:DJ])
            mm.then_inc(m, 1)
            for i in range(8):
                mm = pe.transpose(ps[:, 1 + i // 4, (i % 4) * P:(i % 4 + 1) * P], Cn[:, i, :], c["ident"][:])
                if i % 4 == 3:
                    mm.then_inc(m, 1)
            for n in range(16):
                d = n // 8
                pe.wait_ge(made["E"], d + 1)
                pe.wait_ge(ev, 8 + n - 1 if n >= 2 else 8)
                for x in range(4):
                    j, ri = (2 * n + x // 2) % NP5, x % 2
                    mm = pe.transpose(ps[:, n % 2, x * P:(x + 1) * P], EB(ri)[:, j, :], c["ident"][:])
                mm.then_inc(m, 1)
            pe.wait_ge(made["BD"], 1)
            for d in (1, 0):
                for q in range(4):
                    bank = 2 + q % 2
                    n = (1 - d) * 4 + q
                    if n >= 2:
                        pe.wait_ge(mv2, n - 1)
                    for x in range(4):
                        dj = NP5 * d + 4 * q + x
                        for ri in range(2):
                            mm = pe.matmul(ps[0:2 * GC, bank, x * P:(x + 1) * P], BD[:, ri, dj, :],
                                           G[:, ri, dj, d:d + T5, :].rearrange("p k q -> p (k q)"),
                                           start=ri == 0, stop=ri == 1)
                    mm.then_inc(m, 1)

        @block.vector
        def _(dve):
            step = Steps(dve, v)
            TTo, STT = dve.tensor_tensor, dve.scalar_tensor_tensor

            def ew(dst, x, y, op, mark=None, n=1):
                step.done()
                if mark is None:
                    step(TTo(dst, x, y, op))
                else:
                    TTo(dst, x, y, op).then_inc(made[mark], 1)
                    dve.wait_ge(made[mark], n)

            dve.wait_ge(ld, 16 * 70)
            step(dve.tensor_copy(raw[:, 2, :].rearrange("p (a n) -> p a n", a=2),
                                 ldt[:].rearrange("p (a o) -> p a o", o=1).broadcast_to([DJ, 2, NS])))
            dve.wait_ge(acts, 2)
            step(dve.tensor_scalar(s[:, RE], lam[:, 0], -1e-4, None, ALU.min))
            ew(s[:, AR], s[:, RE], s[:, DTC], ALU.mult, "ar")
            step(TTo(s[:, TH], lam[:, 1], s[:, DTC], ALU.mult))
            step.done()
            step(dve.tensor_scalar(s[:, T1], s[:, TH], 1.0 / TWO_PI, MAGIC, ALU.mult, ALU.add))
            step.done()
            step(dve.tensor_scalar(s[:, T1], s[:, T1], MAGIC, None, ALU.subtract))
            step.done()
            step(STT(out=s[:, TH], in0=s[:, T1], scalar=-6.28125, in1=s[:, TH], op0=ALU.mult, op1=ALU.add))
            step.done()
            step(STT(out=s[:, TH], in0=s[:, T1], scalar=-(TWO_PI - 6.28125), in1=s[:, TH],
                     op0=ALU.mult, op1=ALU.add))
            step.done()
            dve.tensor_scalar(s[:, TH], s[:, TH], 3.141592, -3.141592, ALU.min, ALU.max).then_inc(made["theta"], 1)
            dve.wait_ge(made["theta"], 1)
            step(dve.tensor_scalar(s[:, TAU], s[:, TH], T5 / TWO_PI, None, ALU.mult))
            step.done()
            step(dve.tensor_scalar(s[:, T1], s[:, TAU], MAGIC, MAGIC, ALU.add, ALU.subtract))
            ew(s[:, TAU], s[:, TAU], s[:, T1], ALU.subtract)
            dve.wait_ge(acts, 3)
            step.done()
            step(dve.tensor_scalar(s[:, T1], s[:, TN], -1.0, 1.0, ALU.mult, ALU.add))
            step.done()
            step(dve.reciprocal(s[:, T2], s[:, T1]))
            step.done()
            step(STT(out=s[:, EM], in0=s[:, TN], scalar=2.0, in1=s[:, T2], op0=ALU.mult, op1=ALU.mult))
            step.done()
            step(dve.tensor_scalar(s[:, EE], s[:, EM], 1.0, None, ALU.add))
            dve.wait_ge(acts, 5)
            step.done()
            step(STT(out=s[:, T1], in0=s[:, SH], scalar=-2.0, in1=s[:, SH], op0=ALU.mult, op1=ALU.mult))
            step.done()
            step(dve.tensor_scalar(s[:, T2], s[:, T1], 1.0, None, ALU.add))
            ew(s[:, T2], s[:, T2], s[:, EM], ALU.mult)
            ew(s[:, DR], s[:, T2], s[:, T1], ALU.add)
            ew(s[:, DI], s[:, EE], s[:, SN], ALU.mult)
            ew(s[:, T1], s[:, RE], s[:, RE], ALU.mult)
            ew(s[:, T2], lam[:, 1], lam[:, 1], ALU.mult)
            ew(s[:, MM], s[:, T1], s[:, T2], ALU.add)
            step.done()
            step(dve.reciprocal(s[:, MM], s[:, MM]))
            ew(s[:, T1], s[:, DR], s[:, RE], ALU.mult)
            ew(s[:, T2], s[:, DI], lam[:, 1], ALU.mult)
            ew(s[:, T1], s[:, T1], s[:, T2], ALU.add)
            ew(s[:, QR], s[:, T1], s[:, MM], ALU.mult)
            ew(s[:, T1], s[:, DI], s[:, RE], ALU.mult)
            ew(s[:, T2], s[:, DR], lam[:, 1], ALU.mult)
            ew(s[:, T1], s[:, T1], s[:, T2], ALU.subtract)
            ew(s[:, QI], s[:, T1], s[:, MM], ALU.mult)
            ew(tb["rho"][:], s[:, EE], s[:, EE], ALU.mult)
            ew(tb["rho"][:], tb["rho"][:], tb["rho"][:], ALU.mult)
            ew(tb["rho"][:], tb["rho"][:], tb["rho"][:], ALU.mult)
            step(dve.memset(pw[:, 0, 0, :], 1.0))
            step(dve.memset(pw[:, 1, 0, :], 0.0))
            step(dve.memset(s[:, HALF, :], math.pi / 2))
            step(dve.tensor_scalar(pw[:, 0, 1, :], s[:, DR], 1.0, None, ALU.add))
            step(dve.tensor_copy(pw[:, 1, 1, :], s[:, DI]))
            tmp = scr[:, 0:4 * DJ].rearrange("p (k n) -> p k n", k=4)
            for w in (1, 2, 4):
                xr = pw[:, 0, w:w + 1, :].broadcast_to([P, w, DJ])
                xi = pw[:, 1, w:w + 1, :].broadcast_to([P, w, DJ])
                yr, yi = pw[:, 0, 1:w + 1, :], pw[:, 1, 1:w + 1, :]
                zr, zi = pw[:, 0, w + 1:2 * w + 1, :], pw[:, 1, w + 1:2 * w + 1, :]
                ew(zr, xr, yr, ALU.mult)
                ew(tmp[:, 0:w], xi, yi, ALU.mult)
                ew(zr, zr, tmp[:, 0:w], ALU.subtract)
                ew(zi, xr, yi, ALU.mult)
                ew(tmp[:, 0:w], xi, yr, ALU.mult)
                ew(zi, zi, tmp[:, 0:w], ALU.add)

            def spread(x, n):
                return x.rearrange("p (j o) -> p j o", o=1).broadcast_to([P, x.shape[1], n])

            qr, qi = spread(s[:, QR], GC), spread(s[:, QI], GC)
            t16 = scr[:, 0:DJ * GC].rearrange("p (j q) -> p j q", j=DJ)
            ew(Bb[:, 0], qr, B[:, 0], ALU.mult)
            ew(t16, qi, B[:, 1], ALU.mult)
            ew(Bb[:, 0], Bb[:, 0], t16, ALU.subtract)
            ew(Bb[:, 1], qr, B[:, 1], ALU.mult)
            ew(t16, qi, B[:, 0], ALU.mult)
            ew(Bb[:, 1], Bb[:, 1], t16, ALU.add)
            dve.wait_ge(g, 1)
            tau = spread(s[:, TAU], NC5)
            rmp = ramp[:].rearrange("p (o n) -> p o n", o=1).broadcast_to([P, DJ, NC5])
            ew(tb["sin"][:], tau, rmp, ALU.mult)
            step.done()
            step(dve.tensor_scalar(tb["cos"][:], tb["sin"][:], MAGIC, MAGIC, ALU.add, ALU.subtract))
            ew(tb["sin"][:], tb["sin"][:], tb["cos"][:], ALU.subtract, "turns")

            def power(d, ri, lo, n, reverse):
                x = pw[:, ri, lo:lo + n, NP5 * d:NP5 * d + NP5]
                if reverse:
                    x = x[:, ::-1, :]
                return x.rearrange("p k (j o) -> p j k o", o=1).broadcast_to([P, NP5, n, GC])

            def along(x, n):
                return x.rearrange("p j (o q) -> p j o q", o=1).broadcast_to([P, NP5, n, GC])

            dve.wait_ge(ev, 8)
            tg = scr[:, 0:NP5 * 9 * GC].rearrange("p (j k q) -> p j k q", j=NP5, k=9)
            for d in range(2):
                dj = slice(NP5 * d, NP5 * d + NP5)
                pr, pi = power(d, 0, 0, 9, d == 1), power(d, 1, 0, 9, d == 1)
                cr, ci = along(C[:, 0, dj, :], 9), along(C[:, 1, dj, :], 9)
                gr, gn = G[:, 0, dj], G[:, 1, dj]
                ew(gr, cr, pr, ALU.mult)
                ew(tg, ci, pi, ALU.mult)
                ew(gr, gr, tg, ALU.subtract)
                ew(gn, cr, pi, ALU.mult)
                ew(tg, ci, pr, ALU.mult)
                step.done()
                for j in range(0, NP5):
                    ins = STT(out=gn[:, j].rearrange("p k q -> p (k q)"), in0=gn[:, j].rearrange("p k q -> p (k q)"),
                              scalar=-1.0, in1=tg[:, j].rearrange("p k q -> p (k q)"), op0=ALU.mult,
                              op1=ALU.subtract)
                    step(ins)
            te = scr[:, 4096:6144].rearrange("p (j k q) -> p j k q", j=NP5, k=T5)
            for d in range(2):
                dj = slice(NP5 * d, NP5 * d + NP5)
                pr, pi = power(d, 0, 0, T5, d == 0), power(d, 1, 0, T5, d == 0)
                br, bi = along(Bb[:, 0, dj, :], T5), along(Bb[:, 1, dj, :], T5)
                er = EB(0).rearrange("p j (k q) -> p j k q", k=T5)
                ei = EB(1).rearrange("p j (k q) -> p j k q", k=T5)
                step.done()
                if d:
                    dve.wait_ge(m, 3 + 8)
                ew(er, pr, br, ALU.mult)
                ew(te, pi, bi, ALU.mult)
                ew(er, er, te, ALU.subtract)
                ew(ei, pr, bi, ALU.mult)
                ew(te, pi, br, ALU.mult)
                ew(ei, ei, te, ALU.add, "E", d + 1)
            dve.wait_ge(g, 2)
            for h in range(2):
                rows = slice(NS * h, NS * h + NS)
                step(dve.tensor_copy(BD[rows, :, :, h * GC:(h + 1) * GC], Bb[rows]))
            ew(dm[:], c["ident"][0:2 * GC, 0:GC], c["ident"][0:2 * GC, GC:2 * GC], ALU.add, "BD")
            dve.wait_ge(m, 3 + 16)
            for d in (1, 0):
                for q in range(4):
                    n = (1 - d) * 4 + q
                    dve.wait_ge(m, 3 + 16 + n + 1)
                    kp = ps[0:2 * GC, 2 + q % 2, :].rearrange("p (j k q) -> p j k q", j=4, k=T5)
                    if d == 1:
                        dve.tensor_copy(KK[:, 4 * q:4 * q + 4, 0:T5, :], kp).then_inc(mv2, 1)
                    else:
                        dve.wait_ge(mv2, 4 + q)
                        step(dve.tensor_copy(KK[:, 4 * q:4 * q + 4, T5:KKn, :], kp[:, :, 1:T5, :]))
                        mid = KK[:, 4 * q:4 * q + 4, T5 - 1, :]
                        dve.tensor_tensor(mid, mid, kp[:, :, 0, :], ALU.add).then_inc(mv2, 1)
            dve.wait_ge(mv2, 8)
            t7 = BD[0:2 * GC, 0, 0:NP5, 0:GC]
            dve.wait_ge(m, 3 + 16 + 8)
            step(TTo(t7, Dc[:].rearrange("p (j o) -> p j o", o=1).broadcast_to([2 * GC, NP5, GC]),
                     dm[:].rearrange("p (o q) -> p o q", o=1).broadcast_to([2 * GC, NP5, GC]), ALU.mult))
            step.done()
            mid = KK[:, :, T5 - 1, :]
            dve.tensor_tensor(mid, mid, t7, ALU.add).then_inc(mv, 1)


def s5_mixer(nc, core, c, a, uT, tb, yT):
    E, G, M = tb["E"], tb["G"], tb["M"]
    rot = core.sb("s5_rotp", [P, 2, 2, 2, NC5])
    z = core.sb("s5_z", [P, 2, 2, 2, NC5])
    zs = core.sb("s5_zs", [P, 2, 2, NC5])
    back = core.sb("s5_back", [P, 2, 2, 2, NC5])
    st = core.sb("s5_state", [P, 2, 2, 2, NC5])
    ys = core.sb("s5_y", [P, T5, S5W])
    bg = core.sb("s5_bglu", [P, 4])
    free = E[:].rearrange("p j r n -> p (j r n)")
    yg = free[:, 0:4 * L].rearrange("p (k n) -> p k n", k=4)
    sg = free[:, 4 * L:6 * L].rearrange("p (k n) -> p k n", k=2)
    wg = free[:, 6 * L:8 * L].rearrange("p (k n) -> p k n", k=4)
    vps = core.ps("s5_v", [P, 2, 2, 2, NC5])
    tps = core.ps("s5_tps", [P, 4, 512])
    yps = tps[:].rearrange("p (b h) (j n) -> p b h j n", b=2, j=4)
    names = "ld vmm rot z scan back state ymm yout turned gelu glu gate out zero".split()
    S = {n: core.sem("s5m_" + n) for n in names}
    cosv = tb["cos"][:].rearrange("p (d j) n -> p d j n", d=2)
    sinv = tb["sin"][:].rearrange("p (d j) n -> p d j n", d=2)

    def table(x, j):
        return x[:, :, j:j + 1, :].broadcast_to([P, 2, 2, NC5])

    with nc.Block() as block:
        @block.sync
        def _(sp):
            with nc.allow_non_contiguous_dma(reason="small parameters"):
                sp.dma_start(bg[:], a["s5_b_glu"][0].rearrange("(k p) -> p k", p=P)).then_inc(S["ld"], 16)
            sp.wait_ge(S["vmm"], NP5)
            sp.dma_start(wg[:], a["s5_w_glu"][0].rearrange("(k p) n -> p k n", p=P)).then_inc(S["ld"], 16)

        @block.tensor
        def _(pe):
            def inputs(j):
                if j >= 2:
                    pe.wait_ge(S["rot"], 2 * (j - 1))
                for d in range(2):
                    for ri in range(2):
                        for h in range(2):
                            u = uT[:, 2 * j + h, :]
                            rows = slice(NS * h, NS * h + NS)
                            mm = pe.matmul(vps[rows, j % 2, d, ri, :], E[:, NP5 * d + j, ri, rows],
                                           u if d == 0 else u[:, ::-1], start=True, stop=True)
                mm.then_inc(S["vmm"], 1)

            def outputs(j):
                if j % 4 == 0 and j >= 8:
                    pe.wait_ge(S["yout"], 2 * (j // 4 - 1))
                pe.wait_ge(S["state"], 4 * (j + 1))
                for h in range(2):
                    g = 2 * j + h
                    dst = yps[:, (j // 4) % 2, h, j % 4, :]
                    rows = slice(NS * h, NS * h + NS)
                    pe.matmul(dst, uT[:, g, :], M[:, g, :], start=True, stop=False)
                    for d in range(2):
                        for ri in range(2):
                            mm = pe.matmul(dst, st[rows, j % 2, d, ri, :],
                                           G[rows, ri, NP5 * d + j, 1 - d:1 - d + T5, :]
                                           .rearrange("p k q -> p (k q)"),
                                           start=False, stop=d == 1 and ri == 1)
                mm.then_inc(S["ymm"], 1)

            inputs(0)
            inputs(1)
            for j in range(NP5):
                outputs(j)
                if j + 2 < NP5:
                    inputs(j + 2)
            pe.wait_ge(S["yout"], NP5 // 2)
            for k in range(4):
                for half in range(2):
                    n = 2 * k + half
                    if n >= 4:
                        pe.wait_ge(S["gelu"], n - 3)
                    for t in range(4):
                        mm = pe.transpose(tps[:, n % 4, t * P:(t + 1) * P],
                                          ys[:, 4 * half + t, k * P:(k + 1) * P], c["ident"][:])
                    mm.then_inc(S["turned"], 1)
            pe.wait_ge(S["gelu"], 8)
            pe.wait_ge(S["ld"], 32)
            for m in range(4):
                if m >= 2:
                    pe.wait_ge(S["gate"], m - 1)
                for half in range(2):
                    for k in range(4):
                        mm = pe.matmul(tps[:, 2 * (m % 2) + half, :], wg[:, k, m * P:(m + 1) * P],
                                       yg[:, k, half * 512:half * 512 + 512], start=k == 0, stop=k == 3)
                mm.then_inc(S["glu"], 1)

        @block.vector
        def _(dve):
            for slot in range(2):
                for ri in range(2):
                    dve.memset(st[:, slot, 0, ri, 0:1], 0.0).then_inc(S["out"], 1)
                    dve.memset(st[:, slot, 1, ri, NC5 - 1:NC5], 0.0).then_inc(S["out"], 1)
            for j in range(NP5):
                b = j % 2
                dve.wait_ge(S["vmm"], j + 1)
                if j:
                    dve.wait_ge(S["z"], 2 * j)
                dve.tensor_tensor(rot[:, 0], vps[:, b], table(cosv, j), ALU.mult).then_inc(S["rot"], 1)
                dve.tensor_tensor(rot[:, 1], vps[:, b], table(sinv, j), ALU.mult).then_inc(S["rot"], 1)
                dve.wait_ge(S["rot"], 2 * (j + 1))
                if j >= 2:
                    dve.wait_ge(S["scan"], 4 * (j - 1))
                dve.tensor_tensor(z[:, b, :, 0], rot[:, 0, :, 0], rot[:, 1, :, 1], ALU.add).then_inc(S["z"], 1)
                dve.tensor_tensor(z[:, b, :, 1], rot[:, 0, :, 1], rot[:, 1, :, 0], ALU.subtract
                                  ).then_inc(S["z"], 1)
                dve.wait_ge(S["z"], 2 * (j + 1))
                if j:
                    dve.wait_ge(S["back"], 2 * j)
                for d in range(2):
                    rho = tb["rho"][:, NP5 * d + j:NP5 * d + j + 1].broadcast_to([P, NC5])
                    for ri in range(2):
                        dve.tensor_tensor_scan(zs[:, d, ri], rho, z[:, b, d, ri], 0.0, ALU.mult, ALU.add
                                               ).then_inc(S["scan"], 1)
            for m in range(4):
                dve.wait_ge(S["gate"], m + 1)
                dve.tensor_tensor(yT[:, m, :], yg[:, m, :], sg[:, m % 2, :], ALU.mult).then_inc(S["out"], 1)

        @block.gpsimd
        def _(pool):
            n = NC5 - 1
            for j in range(NP5):
                b = j % 2
                pool.wait_ge(S["scan"], 4 * (j + 1))
                if j:
                    pool.wait_ge(S["state"], 4 * j)
                pool.tensor_tensor(back[:, 0], zs[:], table(cosv, j), ALU.mult).then_inc(S["back"], 1)
                pool.tensor_tensor(back[:, 1], zs[:], table(sinv, j), ALU.mult).then_inc(S["back"], 1)
                pool.wait_ge(S["back"], 2 * (j + 1))
                if j == 0:
                    pool.wait_ge(S["out"], 8)
                elif j >= 2:
                    pool.wait_ge(S["ymm"], j - 1)
                pool.tensor_tensor(st[:, b, 0, 0, 1:], back[:, 0, 0, 0, 0:n], back[:, 1, 0, 1, 0:n],
                                   ALU.subtract).then_inc(S["state"], 1)
                pool.tensor_tensor(st[:, b, 0, 1, 1:], back[:, 0, 0, 1, 0:n], back[:, 1, 0, 0, 0:n],
                                   ALU.add).then_inc(S["state"], 1)
                pool.tensor_tensor(st[:, b, 1, 0, 0:n][:, ::-1], back[:, 0, 1, 0, 0:n], back[:, 1, 1, 1, 0:n],
                                   ALU.subtract).then_inc(S["state"], 1)
                pool.tensor_tensor(st[:, b, 1, 1, 0:n][:, ::-1], back[:, 0, 1, 1, 0:n], back[:, 1, 1, 0, 0:n],
                                   ALU.add).then_inc(S["state"], 1)

        @block.scalar
        def _(act):
            yv = ys[:].rearrange("p t (j h q) -> p h j t q", j=NP5, h=2)
            for n in range(NP5 // 4):
                act.wait_ge(S["ymm"], 4 * (n + 1))
                for h in range(2):
                    act.activation(yv[:, h, 4 * n:4 * n + 4], yps[:, n % 2, h].rearrange("p j (t q) -> p j t q", t=T5),
                                   ACT.Copy).then_inc(S["yout"], 1)
            for k in range(4):
                for half in range(2):
                    n = 2 * k + half
                    act.wait_ge(S["turned"], n + 1)
                    act.activation(yg[:, k, :].rearrange("p (n t) -> p t n", t=T5)[:, 4 * half:4 * half + 4, :],
                                   tps[:, n % 4].rearrange("p (t n) -> p t n", t=4), ACT.Gelu
                                   ).then_inc(S["gelu"], 1)
            act.wait_ge(S["ld"], 32)
            for m in range(4):
                act.wait_ge(S["glu"], m + 1)
                if m >= 2:
                    act.wait_ge(S["out"], 8 + m - 1)
                act.activation(sg[:, m % 2, :], tps[:, 2 * (m % 2):2 * (m % 2) + 2, :].rearrange("p a n -> p (a n)"),
                               ACT.Sigmoid, bias=bg[:, m:m + 1]).then_inc(S["gate"], 1)


def gated_norm(nc, core, c, a, o_sum, zs, ydn):
    sq = core.sb("gn_sq", [P, 2, DW])
    ss = core.sb("gn_ss", [P, TT, H])
    rt = core.sb("gn_rt", [P, TT, H])
    rs = core.sb("gn_rs", [P, TT, H])
    nw = core.sb("gn_w", [P, 1])
    ps = core.ps("gn_ps", [P, 2, 512])
    ld, sqd, red, rtd, rsd, nrm, turned, out, part = (core.sem("gn_" + n) for n in
                                                      "ld sq red rt rs nrm turned out part".split())

    def heads(x):
        return x.rearrange("p (h n) -> p h n", h=H)

    with nc.Block() as block:
        @block.sync
        def _(sp):
            with nc.allow_non_contiguous_dma(reason="small parameters"):
                sp.dma_start(nw[:], a["gdn_norm_w"].rearrange("o n -> n o")).then_inc(ld, 16)

        @block.scalar
        def _(act):
            for t in range(TT):
                if t >= 2:
                    act.wait_ge(red, t - 1)
                act.activation(sq[:, t % 2, :], o_sum[:, t, :], ACT.Square).then_inc(sqd, 1)
            act.wait_ge(rsd, 1)
            act.activation(rt[:], ss[:], ACT.Sqrt).then_inc(rtd, 1)
            act.wait_ge(ld, 16)
            for t in range(TT):
                act.wait_ge(turned, t + 1)
                act.activation(ydn[:, :, t * P:(t + 1) * P], ps[:, t % 2, :].rearrange("p (h n) -> p h n", h=H),
                               ACT.Copy, scale=nw[:, 0:1]).then_inc(out, 1)

        @block.vector
        def _(dve):
            for t in range(TT):
                dve.wait_ge(sqd, t + 1)
                dve.tensor_reduce(ss[:, t, :], heads(sq[:, t % 2, :]), AX.X, ALU.add).then_inc(red, 1)
            dve.wait_ge(red, TT)
            dve.tensor_scalar(ss[:], ss[:], 1.0 / DH, EPS, ALU.mult, ALU.add).then_inc(rsd, 1)
            dve.wait_ge(rtd, 1)
            dve.reciprocal(rs[:], rt[:]).then_inc(rsd, 1)
            dve.wait_ge(rsd, 2)
            for t in range(TT):
                scale = rs[:, t, :].rearrange("p (h o) -> p h o", o=1).broadcast_to([P, H, DH])
                dve.tensor_tensor(heads(o_sum[:, t, :]), heads(o_sum[:, t, :]), scale, ALU.mult
                                  ).then_inc(part, 1)
                dve.wait_ge(part, t + 1)
                dve.tensor_tensor(o_sum[:, t, :], o_sum[:, t, :], zs[:, t, :], ALU.mult).then_inc(nrm, 1)

        @block.tensor
        def _(pe):
            for t in range(TT):
                pe.wait_ge(nrm, t + 1)
                if t >= 2:
                    pe.wait_ge(out, t - 1)
                for h in range(H):
                    mm = pe.transpose(ps[:, t % 2, h * P:(h + 1) * P], o_sum[:, t, h * DH:(h + 1) * DH],
                                      c["ident"][:])
                mm.then_inc(turned, 1)


def out_projection(nc, core, c, a, ys5, ydn, x1, logits, h_dram, filled):
    NR = NGRP + NEXP
    wo = core.sb("w_out_sb", [P, KT, D])
    nf = core.sb("norm_ffn_row", [P, D])
    h2 = core.sb("h_row", [P, 2, D])
    hT = core.sb("h_turned", [P, 2, KT, P])
    sq = core.sb("op_sq", [P, D])
    ss = core.sb("op_ss", [P, TT])
    ms = core.sb("op_ms", [P, TT])
    rt = core.sb("op_rt", [P, TT])
    rs = core.sb("op_rs", [P, TT])
    wr = core.sb("w_router", [P, KT, NR])
    br = core.sb("b_router", [P, NR])
    mm_ps = core.ps("op_ps", [P, 2, 2, 512])
    tr_ps = core.ps("op_turn", [P, 2, 512])
    lg_ps = core.ps("op_logits", [P, 2, 512])
    names = "x w par mm x1 sq ms rt rs h turned hT lg store0 store1".split()
    S = {n: core.sem("op_" + n) for n in names}
    store = [S["store0"], S["store1"]]

    with nc.Block() as block:
        @block.sync
        def _(sp):
            sp.dma_start(wo[:], a["w_out"][0].rearrange("(k p) n -> p k n", p=P)).then_inc(S["w"], 16)
            sp.dma_start(x1[:], a["x"].rearrange("b (t p) d -> p (b t) d", p=P)).then_inc(S["x"], 16)
            sp.dma_start(nf[:], a["norm_ffn"].partition_broadcast(P)).then_inc(S["par"], 16)
            with nc.allow_non_contiguous_dma(reason="small parameters"):
                sp.dma_start(wr[:, :, 0:NGRP], a["router_w_group"][0].rearrange("(k p) n -> p k n", p=P)
                             ).then_inc(S["par"], 16)
                for g in range(NGRP):
                    sp.dma_start(wr[:, :, NGRP + EPG * g:NGRP + EPG * (g + 1)],
                                 a["router_w_expert"][0, g].rearrange("(k p) n -> p k n", p=P)
                                 ).then_inc(S["par"], 16)
                sp.dma_start(br[:, 0:NGRP], a["router_b_group"].partition_broadcast(P)).then_inc(S["par"], 16)
                sp.dma_start(br[:, NGRP:], a["router_b_expert"].rearrange("o g e -> o (g e)")
                             .partition_broadcast(P)).then_inc(S["par"], 16)
            for t in range(TT):
                sp.wait_ge(S["h"], t + 1)
                sp.dma_start(h_dram[t * P:(t + 1) * P, :], h2[:, t % 2, :]).then_inc(store[t % 2], 16)
            sp.wait_ge(filled, 16 * (MAXB + 1 - L * 2 // P))
            for s in range(2):
                sp.wait_ge(store[s], 16 * TT // 2)

        @block.tensor
        def _(pe):
            def project(t):
                if t >= 2:
                    pe.wait_ge(S["x1"], t - 1)
                for half in range(2):
                    for k in range(KT):
                        y = ys5[:, k] if k < 4 else ydn[:, k - 4]
                        mm = pe.matmul(mm_ps[:, t % 2, half, :], y[:, t * P:(t + 1) * P],
                                       wo[:, k, half * 512:half * 512 + 512], start=k == 0, stop=k == KT - 1)
                mm.then_inc(S["mm"], 1)

            def route(t):
                pe.wait_ge(S["h"], t + 1)
                for half in range(2):
                    n = 2 * t + half
                    if n >= 2:
                        pe.wait_ge(S["hT"], n - 1)
                    for k in range(4):
                        mm = pe.transpose(tr_ps[:, half, k * P:(k + 1) * P],
                                          h2[:, t % 2, (4 * half + k) * P:(4 * half + k + 1) * P], c["ident"][:])
                    mm.then_inc(S["turned"], 1)

            def logit(t):
                pe.wait_ge(S["hT"], 2 * t + 2)
                for k in range(KT):
                    mm = pe.matmul(lg_ps[:, 0, t * NR:(t + 1) * NR], hT[:, t % 2, k, :], wr[:, k, :],
                                   start=k == 0, stop=k == KT - 1)
                mm.then_inc(S["lg"], 1)

            pe.wait_ge(S["w"], 16)
            pe.wait_ge(S["par"], 16 * 8)
            for t in range(TT + 2):
                if t < TT:
                    project(t)
                if 1 <= t <= TT:
                    route(t - 1)
                if t >= 2:
                    logit(t - 2)

        @block.vector
        def _(dve):
            dve.wait_ge(S["x"], 16)
            dve.wait_ge(S["par"], 16 * 8)
            for t in range(TT):
                dve.wait_ge(S["mm"], t + 1)
                dve.tensor_tensor(x1[:, t, :], x1[:, t, :], mm_ps[:, t % 2].rearrange("p a n -> p (a n)"), ALU.add
                                  ).then_inc(S["x1"], 1)
                dve.wait_ge(S["sq"], t + 1)
                dve.tensor_scalar(ms[:, t:t + 1], ss[:, t:t + 1], 1.0 / D, EPS, ALU.mult, ALU.add
                                  ).then_inc(S["ms"], 1)
                dve.wait_ge(S["rt"], t + 1)
                dve.reciprocal(rs[:, t:t + 1], rt[:, t:t + 1]).then_inc(S["rs"], 1)
                dve.wait_ge(S["rs"], t + 1)
                if t >= 2:
                    dve.wait_ge(store[t % 2], 16 * (t // 2))
                    dve.wait_ge(S["turned"], 2 * (t - 1))
                dve.scalar_tensor_tensor(out=h2[:, t % 2, :], in0=x1[:, t, :], scalar=rs[:, t:t + 1], in1=nf[:],
                                         op0=ALU.mult, op1=ALU.mult).then_inc(S["h"], 1)
            dve.wait_ge(S["lg"], TT)
            dve.tensor_tensor(logits[:], lg_ps[:, 0, 0:TT * NR].rearrange("p (t n) -> p t n", n=NR),
                              br[:].rearrange("p (o n) -> p o n", o=1).broadcast_to([P, TT, NR]), ALU.add
                              ).then_inc(S["x1"], 1)

        @block.scalar
        def _(act):
            def turned(t):
                for half in range(2):
                    n = 2 * t + half
                    act.wait_ge(S["turned"], n + 1)
                    if t >= 2:
                        act.wait_ge(S["lg"], t - 1)
                    act.activation(hT[:, t % 2, 4 * half:4 * half + 4, :],
                                   tr_ps[:, half, :].rearrange("p (k n) -> p k n", k=4), ACT.Copy
                                   ).then_inc(S["hT"], 1)

            for t in range(TT):
                act.wait_ge(S["x1"], t + 1)
                if t:
                    act.wait_ge(S["sq"], t)
                act.activation(sq[:], x1[:, t, :], ACT.Square, accum_out=ss[:, t:t + 1]).then_inc(S["sq"], 1)
                act.wait_ge(S["ms"], t + 1)
                act.activation(rt[:, t:t + 1], ms[:, t:t + 1], ACT.Sqrt).then_inc(S["rt"], 1)
                if t >= 1:
                    turned(t - 1)
            turned(TT - 1)


def router_tables(core):
    return {
        "slot_tok": core.sb("slot_token", [P, MAXB + 3], I32),
        "block": core.sb("block_expert", [P, MAXB + 2], I32),
        "count": core.sb("block_count", [P, 1], I32),
        "dest": core.sb("dest_slot", [P, 2, TT], I32),
        "gate": core.sb("gate", [P, 2, TT]),
    }


def router(nc, core, c, logits, rt):
    NB = MAXB + 2
    strict = core.sb("r_strict", [P, P])
    iota = core.sb("r_iota", [P, P])
    tokid = core.sb("r_tokid", [P, TT])
    ge = core.sb("r_group", [P, TT, NGRP])
    one_g = core.sb("r_one_group", [P, TT, NGRP])
    em = core.sb("r_masked", [P, TT, NEXP])
    t32 = core.sb("r_t32", [P, TT, NEXP])
    one = core.sb("r_one", [P, 2, TT, NEXP])
    both = core.sb("r_both", [P, TT, NEXP])
    pos = core.sb("r_pos", [P, TT, NEXP])
    off = core.sb("r_off", [P, TT + 1, NEXP])
    blocks = core.sb("r_blocks", [P, 3, NEXP])
    cmp8 = core.sb("r_cmp8", [P, NEXP, TT])
    cmpb = core.sb("r_cmpb", [P, NB, NEXP])
    col = core.sb("r_cols", [P, 8, TT])
    dest = core.sb("r_dest", [P, 2, TT])
    blk = core.sb("r_blk", [P, 2, TT])
    slot = core.sb("r_slot", [P, 2, TT])
    hit_s = core.sb("r_hit_slot", [P, 2 * TT, P])
    hit_b = core.sb("r_hit_block", [P, 2 * TT, NB])
    ebf = core.sb("r_ebf", [P, NB])
    ps = core.ps("r_ps", [P, 3, 512])
    pg, v, s, m, hit = (core.sem("r_" + n) for n in "pool dve act pe hit".split())
    s_ready = [core.sem("r_ready_" + n) for n in ("groups", "gap", "experts")]
    GMAX, GSUM, M1, M2, W, TMP = range(6)

    def last(x, n):
        return x.rearrange("p (t o) -> p t o", o=1).broadcast_to([P, x.shape[1], n])

    def tiles(x, n=TT):
        return x.rearrange("p (o e) -> p o e", o=1).broadcast_to([P, n, x.shape[1]])

    with nc.Block() as block:
        @block.gpsimd
        def _(pool):
            step = Steps(pool, pg)
            step(pool.iota(iota[:], [[1, P]], base=0, channel_multiplier=0, allow_small_or_imprecise_dtypes=True))
            step(pool.iota(tokid[:], [[P, TT]], base=0, channel_multiplier=1, allow_small_or_imprecise_dtypes=True))
            step(pool.affine_select(out=strict[:], in_=c["ones"][:], compare_op=ALU.is_gt, fill=0.0, base=0,
                                    pattern=[[1, P]], channel_multiplier=-1))
            step(pool.memset(rt["slot_tok"][:], 0))

        @block.scalar
        def _(act):
            act.wait_ge(s_ready[0], 1)
            act.activation(ge[:], ge[:], ACT.Exp).then_inc(s, 1)
            act.wait_ge(s_ready[1], 1)
            act.activation(col[:, TMP], col[:, TMP], ACT.Exp).then_inc(s, 1)

        @block.tensor
        def _(pe):
            pe.wait_ge(s_ready[2], 1)
            pe.wait_ge(pg, 3)
            flat = both[:].rearrange("p t e -> p (t e)")
            pe.matmul(ps[:, 0, 0:TT * NEXP], strict[:], flat, start=True, stop=True)
            pe.matmul(ps[:, 1, 0:TT * NEXP], c["ones"][:], flat, start=True, stop=True).then_inc(m, 1)
            for n in range(2 * TT):
                pe.wait_ge(hit, 2 * (n + 1))
                mm = pe.matmul(ps[:, 2, 0:NB], hit_s[:, n, :], hit_b[:, n, :], start=n == 0, stop=n == 2 * TT - 1)
            mm.then_inc(m, 1)

        @block.vector
        def _(dve):
            step = Steps(dve, v)
            TTo = dve.tensor_tensor

            def seq(ins_of, mark=None):
                step.done()
                ins = ins_of()
                if mark is None:
                    step(ins)
                else:
                    ins.then_inc(mark, 1)
                    dve.wait_ge(mark, 1)

            dve.wait_ge(pg, 4)
            lg, le = logits[:, :, 0:NGRP], logits[:, :, NGRP:]
            step(dve.tensor_reduce(col[:, GMAX], lg, AX.X, ALU.max))
            seq(lambda: TTo(ge[:], lg, last(col[:, GMAX], NGRP), ALU.subtract))

            def first_max(dst, x, n, mx, tmp):
                seq(lambda: TTo(tmp, x, last(mx, n), ALU.is_equal))
                seq(lambda: dve.tensor_scalar(tmp, tmp, -BIG, BIG, ALU.mult, ALU.add))
                seq(lambda: TTo(tmp, tmp, tiles(iota[:, 0:n]), ALU.add))
                seq(lambda: dve.tensor_reduce(col[:, W], tmp, AX.X, ALU.min))
                seq(lambda: TTo(dst, last(col[:, W], n), tiles(iota[:, 0:n]), ALU.is_equal))

            first_max(one_g[:], lg, NGRP, col[:, GMAX], t32[:, :, 0:NGRP])
            step.done()
            dve.tensor_copy(t32[:, :, 0:NGRP], one_g[:]).then_inc(s_ready[0], 1)
            dve.wait_ge(s_ready[0], 1)
            g4 = one_g[:].rearrange("p t (g o) -> p t g o", o=1).broadcast_to([P, TT, NGRP, EPG])
            e4 = em[:].rearrange("p t (g e) -> p t g e", g=NGRP)
            t4 = t32[:].rearrange("p t (g e) -> p t g e", g=NGRP)
            l4 = le.rearrange("p t (g e) -> p t g e", g=NGRP)
            seq(lambda: TTo(e4, l4, g4, ALU.mult))
            seq(lambda: dve.tensor_copy(t4, g4))
            seq(lambda: dve.tensor_scalar(t32[:], t32[:], BIG, -BIG, ALU.mult, ALU.add))
            seq(lambda: TTo(em[:], em[:], t32[:], ALU.add))
            seq(lambda: dve.tensor_reduce(col[:, M1], em[:], AX.X, ALU.max))
            first_max(one[:, 0], em[:], NEXP, col[:, M1], t32[:])
            seq(lambda: dve.tensor_scalar(t32[:], one[:, 0], -3.0 * BIG, None, ALU.mult))
            seq(lambda: TTo(em[:], em[:], t32[:], ALU.add))
            seq(lambda: dve.tensor_reduce(col[:, M2], em[:], AX.X, ALU.max))
            first_max(one[:, 1], em[:], NEXP, col[:, M2], t32[:])
            seq(lambda: TTo(both[:], one[:, 0], one[:, 1], ALU.add), s_ready[2])
            seq(lambda: TTo(col[:, TMP], col[:, M2], col[:, M1], ALU.subtract), s_ready[1])
            dve.wait_ge(s, 2)
            seq(lambda: dve.tensor_reduce(col[:, GSUM], ge[:], AX.X, ALU.add))
            seq(lambda: dve.tensor_scalar(col[:, W], col[:, TMP], 1.0, None, ALU.add))
            seq(lambda: TTo(col[:, W], col[:, W], col[:, GSUM], ALU.mult))
            seq(lambda: dve.reciprocal(rt["gate"][:, 0], col[:, W]))
            seq(lambda: TTo(rt["gate"][:, 1], rt["gate"][:, 0], col[:, TMP], ALU.mult))
            dve.wait_ge(m, 1)
            tot = ps[:, 1, 0:TT * NEXP].rearrange("p (t e) -> p t e", t=TT)
            seq(lambda: dve.memset(off[:, 0, :], 0.0))
            for t in range(TT):
                seq(lambda: TTo(off[:, t + 1, :], off[:, t, :], tot[:, t, :], ALU.add))
            cnt = off[:, TT, :]
            seq(lambda: dve.tensor_scalar(ebf[:, 0:TT], iota[:, 0:TT], float(P), None, ALU.mult))
            seq(lambda: TTo(cmp8[:], last(cnt, TT), tiles(ebf[:, 0:TT], NEXP), ALU.is_gt))
            seq(lambda: dve.tensor_reduce(blocks[:, 0], cmp8[:], AX.X, ALU.add))
            seq(lambda: dve.tensor_tensor_scan(blocks[:, 1], c["ones"][:, 0:NEXP], blocks[:, 0], 0.0,
                                               ALU.mult, ALU.add))
            seq(lambda: TTo(blocks[:, 2], blocks[:, 1], blocks[:, 0], ALU.subtract))
            seq(lambda: dve.tensor_scalar(blocks[:, 2], blocks[:, 2], float(P), None, ALU.mult))
            seq(lambda: TTo(pos[:], off[:, 0:TT, :], ps[:, 0, 0:TT * NEXP].rearrange("p (t e) -> p t e", t=TT),
                            ALU.add))
            seq(lambda: TTo(pos[:], pos[:], tiles(blocks[:, 2]), ALU.add))
            for k in range(2):
                seq(lambda: TTo(t32[:], pos[:], one[:, k], ALU.mult))
                seq(lambda: dve.tensor_reduce(dest[:, k], t32[:], AX.X, ALU.add))
            seq(lambda: dve.tensor_copy(rt["dest"][:], dest[:]))
            seq(lambda: dve.tensor_scalar(blk[:], dest[:], 1.0 / P, -(P - 1) / (2.0 * P), ALU.mult, ALU.add))
            seq(lambda: dve.tensor_scalar(blk[:], blk[:], MAGIC, MAGIC, ALU.add, ALU.subtract))
            seq(lambda: dve.scalar_tensor_tensor(out=slot[:], in0=blk[:], scalar=-float(P), in1=dest[:],
                                                 op0=ALU.mult, op1=ALU.add))
            step.done()
            for n in range(2 * TT):
                k, t = n // TT, n % TT
                dve.tensor_scalar(hit_s[:, n, :], iota[:], slot[:, k, t:t + 1], tokid[:, t:t + 1],
                                  ALU.is_equal, ALU.mult).then_inc(hit, 1)
                dve.tensor_scalar(hit_b[:, n, :], iota[:, 0:NB], blk[:, k, t:t + 1], None,
                                  ALU.is_equal).then_inc(hit, 1)
            step(TTo(cmpb[:], tiles(blocks[:, 1], NB), last(iota[:, 0:NB], NEXP), ALU.is_le))
            seq(lambda: dve.tensor_reduce(ebf[:], cmpb[:], AX.X, ALU.add))
            seq(lambda: dve.tensor_scalar(ebf[:], ebf[:], float(NEXP - 1), None, ALU.min))
            seq(lambda: dve.tensor_copy(rt["block"][:], ebf[:]))
            seq(lambda: dve.tensor_copy(rt["count"][:], blocks[:, 1, NEXP - 1:NEXP]))
            dve.wait_ge(m, 2)
            seq(lambda: dve.tensor_copy(rt["slot_tok"][:, 0:NB], ps[:, 2, 0:NB]))


def experts(nc, core, c, a, rt, h_dram, y_dram):
    KD = DE // P
    wg = core.sb("w_gate", [P, 2, KT, DE])
    wu = core.sb("w_up", [P, 2, KT, DE])
    wd = core.sb("w_down", [P, 2, KD, D])
    idx = core.sb("gather_idx", [P, 2], I32)
    xg = core.sb("gathered", [P, 2, D])
    xT = core.sb("gathered_T", [P, 2, KT, P])
    sg = core.sb("silu_gate", [P, DE])
    hid = core.sb("hidden", [P, DE])
    hT = core.sb("hidden_T", [P, KD, P])
    y = core.sb("expert_out", [P, 2, D])
    g_ps = core.ps("gate_mm", [P, 512])
    u_ps = core.ps("up_mm", [P, 512])
    x_ps = core.ps("x_turned", [P, 2, 512])
    h_ps = core.ps("h_turned_ps", [P, 512])
    y_ps = core.ps("down_mm", [P, 2, 512])
    names = "gate_mm up_mm x_turned xT silu hid h_turned hT down_mm y_out idx turn".split()
    S = {n: core.sem("ex_" + n) for n in names}
    ld = {n: [core.sem(f"ex_ld_{n}{s}") for s in range(2)] for n in "gud"}
    gathered = [core.sem(f"ex_gathered{s}") for s in range(2)]
    stored = [core.sem(f"ex_stored{s}") for s in range(2)]
    w_gate = a["expert_w_gate"].rearrange("o e (p k) n -> p (o e) k n", k=KT)
    w_up = a["expert_w_up"].rearrange("o e (p k) n -> p (o e) k n", k=KT)
    w_down = a["expert_w_down"].rearrange("o e (p k) n -> p (o e) k n", k=KD)
    y_blocks = y_dram.rearrange("(b p) d -> b p d", p=P)
    PAIRS = (MAXB + 1) // 2

    def odd_and_even(i):
        return ((i * 2 + 1, 1), (i * 2 + 2, 0))

    with nc.Block() as block:
        @block.sync
        def _(sp):
            count = sp.value_load(rt["count"][0:1, 0:1], min_val=16, max_val=MAXB)

            def expert(b):
                return sp.value_load(rt["block"][0:1, bass.ds(b, 1)], min_val=0, max_val=NEXP - 1)

            def load_gate_up(b, s):
                e = expert(b)
                sp.wait_ge(S["up_mm"], b + 1)
                sp.dma_start(wg[:, s], w_gate[:, bass.ds(e, 1)].rearrange("p o k n -> p (o k) n")
                             ).then_inc(ld["g"][s], 16)
                sp.dma_start(wu[:, s], w_up[:, bass.ds(e, 1)].rearrange("p o k n -> p (o k) n")
                             ).then_inc(ld["u"][s], 16)

            def load_down(b, s):
                e = expert(b)
                sp.wait_ge(S["down_mm"], b + 1)
                sp.dma_start(wd[:, s], w_down[:, bass.ds(e, 1)].rearrange("p o k n -> p (o k) n")
                             ).then_inc(ld["d"][s], 16)

            load_gate_up(0, 0)
            with sp.Fori(0, PAIRS) as i:
                for b, s in odd_and_even(i):
                    with sp.If(b < count):
                        load_gate_up(b, s)
                    with sp.If(b < count + 1):
                        load_down(b - 1, 1 - s)

        @block.gpsimd
        def _(pool):
            count = pool.value_load(rt["count"][0:1, 0:1], min_val=16, max_val=MAXB)

            def gather(s, b, wait_idx):
                pool.tensor_copy(idx[:, s:s + 1], rt["slot_tok"][:, bass.ds(b, 1)]).then_inc(S["idx"], 1)
                pool.wait_ge(S["idx"], wait_idx)
                pool.sem_inc(S["turn"], 1)
                pool.indirect_dma_start(out=xg[:, s, :], out_offset=None, in_=h_dram,
                                        in_offset=bass.IndirectOffsetOnAxis(ap=idx[:, s:s + 1], axis=0)
                                        ).then_inc(gathered[s], 16)

            gather(0, 0, 1)
            with pool.Fori(0, PAIRS) as i:
                for s in range(2):
                    b = i * 2 + s
                    with pool.If(b < count):
                        pool.wait_ge(S["x_turned"], b + 1)
                        gather(1 - s, b + 1, b + 2)
            pool.wait_ge(gathered[0], 16 * (count // 2 + 1))
            pool.wait_ge(gathered[1], 16 * ((count + 1) // 2))
            pool.sem_inc(S["turn"], 1)

        @block.tensor
        def _(pe):
            count = pe.value_load(rt["count"][0:1, 0:1], min_val=16, max_val=MAXB)
            pe.sem_inc(S["up_mm"], 2)
            pe.sem_inc(S["down_mm"], 2)

            def turn_rows(s):
                for k in range(KT):
                    mm = pe.transpose(x_ps[:, k // 4, (k % 4) * P:(k % 4 + 1) * P], xg[:, s, k:D:KT],
                                      c["ident"][:])
                mm.then_inc(S["x_turned"], 1)

            def times_gate(s):
                for k in range(KT):
                    mm = pe.matmul(g_ps[:], xT[:, s, k, :], wg[:, s, k, :], start=k == 0, stop=k == KT - 1)
                mm.then_inc(S["gate_mm"], 1)

            def times_up(s):
                for k in range(KT):
                    mm = pe.matmul(u_ps[:], xT[:, s, k, :], wu[:, s, k, :], start=k == 0, stop=k == KT - 1)
                mm.then_inc(S["up_mm"], 1)

            def turn_hidden(b):
                pe.wait_ge(S["hid"], b + 1)
                for k in range(KD):
                    mm = pe.transpose(h_ps[:, k * P:(k + 1) * P], hid[:, k:DE:KD], c["ident"][:])
                mm.then_inc(S["h_turned"], 1)

            def times_down(b, s, i):
                pe.wait_ge(ld["d"][s], i * 16 + 16)
                pe.wait_ge(S["hT"], b)
                pe.wait_ge(S["y_out"], b * 2)
                for half in range(2):
                    for k in range(KD):
                        mm = pe.matmul(y_ps[:, half, :], hT[:, k, :], wd[:, s, k, half * 512:half * 512 + 512],
                                       start=k == 0, stop=k == KD - 1)
                mm.then_inc(S["down_mm"], 1)

            pe.wait_ge(gathered[0], 16)
            turn_rows(0)
            pe.wait_ge(ld["g"][0], 16)
            pe.wait_ge(S["xT"], 1)
            times_gate(0)
            pe.wait_ge(ld["u"][0], 16)
            times_up(0)
            pe.wait_ge(gathered[1], 16)
            turn_rows(1)
            with pe.Fori(0, PAIRS) as i:
                for b, s in odd_and_even(i):
                    with pe.If(b < count):
                        pe.wait_ge(ld["g"][s], i * 16 + (16 if s else 32))
                        pe.wait_ge(S["xT"], b + 1)
                        pe.wait_ge(S["silu"], b + 1)
                        times_gate(s)
                        turn_hidden(b)
                        pe.wait_ge(ld["u"][s], i * 16 + (16 if s else 32))
                        times_up(s)
                        pe.wait_ge(gathered[1 - s], i * 16 + 32)
                        turn_rows(1 - s)
                        times_down(b, 1 - s, i)
                    with pe.If(b == count):
                        turn_hidden(b)
                        times_down(b, 1 - s, i)

        @block.scalar
        def _(act):
            count = act.value_load(rt["count"][0:1, 0:1], min_val=16, max_val=MAXB)
            act.sem_inc(S["silu"], 1)
            act.sem_inc(S["y_out"], 2)
            for s in range(2):
                act.sem_inc(stored[s], 16)

            def rows_out(s):
                act.activation(xT[:, s].rearrange("p k n -> p (k n)"), x_ps[:].rearrange("p a n -> p (a n)"),
                               ACT.Copy).then_inc(S["xT"], 1)

            def store(b, s, i):
                act.wait_ge(S["down_mm"], b + 2)
                act.wait_ge(stored[s], i * 16 + 16)
                act.activation(y[:, s, 0:512], y_ps[:, 0, :], ACT.Copy).then_inc(S["y_out"], 1)
                act.wait_ge(S["y_out"], b * 2 + 2)
                act.dma_start(y_blocks[bass.ds(b - 1, 1)].rearrange("o p d -> p (o d)"), y[:, s, :]
                              ).then_inc(stored[s], 16)

            act.wait_ge(S["x_turned"], 1)
            rows_out(0)
            act.wait_ge(S["gate_mm"], 1)
            act.activation(sg[:], g_ps[:], ACT.Silu).then_inc(S["silu"], 1)
            act.wait_ge(S["x_turned"], 2)
            rows_out(1)
            with act.Fori(0, PAIRS) as i:
                for b, s in odd_and_even(i):
                    with act.If(b < count):
                        act.wait_ge(S["gate_mm"], b + 1)
                        act.wait_ge(S["hid"], b + 1)
                        act.activation(sg[:], g_ps[:], ACT.Silu).then_inc(S["silu"], 1)
                        act.wait_ge(S["x_turned"], b + 2)
                        rows_out(1 - s)
                    with act.If(b < count + 1):
                        store(b, 1 - s, i)
            act.wait_ge(stored[0], 16 * ((count + 1) // 2) + 16)
            act.wait_ge(stored[1], 16 * (count // 2) + 16)
            act.activation(sg[:, 0:1], c["ones"][:, 0:1], ACT.Copy)

        @block.vector
        def _(dve):
            count = dve.value_load(rt["count"][0:1, 0:1], min_val=16, max_val=MAXB)
            dve.sem_inc(S["hid"], 1)
            dve.wait_ge(S["up_mm"], 3)
            dve.wait_ge(S["silu"], 2)
            dve.tensor_tensor(hid[:], sg[:], u_ps[:], ALU.mult).then_inc(S["hid"], 1)
            with dve.Fori(0, PAIRS) as i:
                for b, s in odd_and_even(i):
                    with dve.If(b < count + 1):
                        dve.wait_ge(S["h_turned"], b)
                        dve.wait_ge(S["down_mm"], b + 1)
                        dve.tensor_copy(hT[:].rearrange("p k n -> p (k n)"), h_ps[:]).then_inc(S["hT"], 1)
                    with dve.If(b < count):
                        dve.wait_ge(S["up_mm"], b + 3)
                        dve.wait_ge(S["silu"], b + 2)
                        dve.tensor_tensor(hid[:], sg[:], u_ps[:], ALU.mult).then_inc(S["hid"], 1)
                    with dve.If(b < count + 1):
                        dve.wait_ge(S["down_mm"], b + 2)
                        dve.wait_ge(stored[1 - s], i * 16 + 16)
                        dve.tensor_copy(y[:, 1 - s, 512:], y_ps[:, 1, :]).then_inc(S["y_out"], 1)


def combine(nc, core, c, a, x1, rt, y_dram, out):
    rows = core.sb("expert_rows", [P, 4, 2, D])
    res = core.sb("result", [P, 2, D])
    sq = core.sb("cb_sq", [P, D])
    nf = core.sb("norm_final_row", [P, D])
    st = core.sb("cb_stats", [P, 4, TT])
    par = core.sem("cb_par")
    got = [[core.sem(f"cb_got{s}{k}") for k in range(2)] for s in range(4)]
    stored = [core.sem(f"cb_stored{s}") for s in range(2)]
    add, sqd, msd, rtd, rsd, res_s = (core.sem("cb_" + n) for n in "add sq ms rt rs res".split())
    out_rows = out.rearrange("b (t p) d -> p (b t) d", p=P)

    with nc.Block() as block:
        @block.gpsimd
        def _(pool):
            for t in range(TT):
                if t >= 4:
                    pool.wait_ge(add, 2 * (t - 3))
                for k in range(2):
                    pool.indirect_dma_start(out=rows[:, t % 4, k, :], out_offset=None, in_=y_dram,
                                            in_offset=bass.IndirectOffsetOnAxis(ap=rt["dest"][:, k, t:t + 1], axis=0)
                                            ).then_inc(got[t % 4][k], 16)

        @block.sync
        def _(sp):
            sp.dma_start(nf[:], a["norm_final"].rearrange("(o n) -> o n", o=1).partition_broadcast(P)
                         ).then_inc(par, 16)
            for t in range(TT):
                sp.wait_ge(res_s, t + 1)
                sp.dma_start(out_rows[:, t, :], res[:, t % 2, :]).then_inc(stored[t % 2], 16)
            for s in range(2):
                sp.wait_ge(stored[s], 16 * TT // 2)

        @block.vector
        def _(dve):
            def norm(t):
                dve.wait_ge(sqd, t + 1)
                dve.tensor_scalar(st[:, 1, t:t + 1], st[:, 0, t:t + 1], 1.0 / D, EPS, ALU.mult, ALU.add
                                  ).then_inc(msd, 1)
                dve.wait_ge(rtd, t + 1)
                dve.reciprocal(st[:, 3, t:t + 1], st[:, 2, t:t + 1]).then_inc(rsd, 1)
                dve.wait_ge(rsd, t + 1)
                if t >= 2:
                    dve.wait_ge(stored[t % 2], 16 * (t // 2))
                dve.scalar_tensor_tensor(out=res[:, t % 2, :], in0=x1[:, t, :], scalar=st[:, 3, t:t + 1],
                                         in1=nf[:], op0=ALU.mult, op1=ALU.mult).then_inc(res_s, 1)

            dve.wait_ge(par, 16)
            for t in range(TT):
                for k in range(2):
                    dve.wait_ge(got[t % 4][k], 16 * (t // 4 + 1))
                    if k:
                        dve.wait_ge(add, 2 * t + 1)
                    dve.scalar_tensor_tensor(out=x1[:, t, :], in0=rows[:, t % 4, k, :],
                                             scalar=rt["gate"][:, k, t:t + 1], in1=x1[:, t, :],
                                             op0=ALU.mult, op1=ALU.add).then_inc(add, 1)
                if t:
                    norm(t - 1)
            norm(TT - 1)

        @block.scalar
        def _(act):
            for t in range(TT):
                act.wait_ge(add, 2 * (t + 1))
                if t:
                    act.wait_ge(sqd, t)
                act.activation(sq[:], x1[:, t, :], ACT.Square, accum_out=st[:, 0, t:t + 1]).then_inc(sqd, 1)
                act.wait_ge(msd, t + 1)
                act.activation(st[:, 2, t:t + 1], st[:, 1, t:t + 1], ACT.Sqrt).then_inc(rtd, 1)


def hybrid_encoder(nc, a, out):
    h_dram = nc.dram_tensor("h_rows", [L, D], F32).ap()
    y_dram = nc.dram_tensor("expert_rows_dram", [(MAXB + 1) * P, D], F32).ap()
    with ExitStack() as whole:
        core = Core(nc, whole)
        c = constants(core)
        filled = core.sem("expert_rows_filled")
        with ExitStack() as late:
            with ExitStack() as mixers:
                mc = Core(nc, mixers)
                with ExitStack() as st:
                    dc = Core(nc, st)
                    o = persistent(mc, dc)
                    tb = gate_tables(dc)
                    with ExitStack() as s:
                        in_projection(nc, Core(nc, s), c, a, o, tb, y_dram, filled)
                    o_sum = dc.sb("o_sum", [P, TT, DW])
                    with ExitStack() as s:
                        delta_net(nc, Core(nc, s), c, a, o, tb, o_sum)
                    ydn = o["qT"]
                    with ExitStack() as s:
                        gated_norm(nc, Core(nc, s), c, a, o_sum, o["zs"], ydn)
                ys5 = o["uT"][:].rearrange("p (k g) n -> p k (g n)", k=4)
                with ExitStack() as st:
                    s5t = s5_tables(Core(nc, st))
                    with ExitStack() as s:
                        s5_parameters(nc, Core(nc, s), c, a, s5t)
                    with ExitStack() as s:
                        s5_mixer(nc, Core(nc, s), c, a, o["uT"], s5t, ys5)
                lc = Core(nc, late)
                x1 = lc.sb("x1", [P, TT, D], side="right")
                logits = lc.sb("logits", [P, TT, NGRP + NEXP], side="right")
                with ExitStack() as s:
                    out_projection(nc, Core(nc, s), c, a, ys5, ydn, x1, logits, h_dram, filled)
            rt = router_tables(lc)
            with ExitStack() as s:
                router(nc, Core(nc, s), c, logits, rt)
            with ExitStack() as s:
                experts(nc, Core(nc, s), c, a, rt, h_dram, y_dram)
            with ExitStack() as s:
                combine(nc, Core(nc, s), c, a, x1, rt, y_dram, out)


_INS = ["x", "norm_mix", "w_in", "s5_lam_re", "s5_lam_im", "s5_log_dt", "s5_b_re", "s5_b_im", "s5_c_re", "s5_c_im",
        "s5_d", "s5_w_glu", "s5_b_glu", "gdn_conv_w", "gdn_a_log", "gdn_dt_bias", "gdn_norm_w", "w_out", "norm_ffn",
        "router_w_group", "router_b_group", "router_w_expert", "router_b_expert",
        "expert_w_gate", "expert_w_up", "expert_w_down", "norm_final"]


def kernel(**inputs):
    import numpy as np
    import concourse.bacc as bacc
    from concourse.bass_utils import run_bass_kernel_spmd

    nc = bacc.Bacc("TRN2", target_bir_lowering=False, num_devices=1)
    arrays, aps = {}, {}
    for name in _INS:
        arr = np.ascontiguousarray(inputs[name])
        arrays[f"in_{name}"] = arr
        aps[name] = nc.dram_tensor(f"in_{name}", arr.shape, mybir.dt.from_np(arr.dtype), kind="ExternalInput").ap()
    out = nc.dram_tensor("out", (1, L, D), F32, kind="ExternalOutput").ap()
    hybrid_encoder(nc, aps, out)
    r = run_bass_kernel_spmd(nc, [arrays], core_ids=[0])
    return r.results[0]["out"]
```

```python
from contextlib import ExitStack, contextmanager
import math

import concourse.bass as bass
from concourse import mybir

F32 = mybir.dt.float32
F32R = mybir.dt.float32r
I32 = mybir.dt.int32
U32 = mybir.dt.uint32
ALU = mybir.AluOpType
ACT = mybir.ActivationFunctionType
AX = mybir.AxisListType

P = 128
D = 1024
L = 1024
KT = D // P
TT = L // P
H = 4
DH = 128
DW = H * DH
S5W = 512
NG = 32
GC = 16
NS = 64
T5 = 8
NC5 = L // T5
NP5 = NG // 2
IN_COLS = 2576
EPS = 1e-6
NEXP = 32
NGRP = 4
EPG = 8
DE = 512
MAXB = L * 2 // P + NEXP - 1
TWO_PI = 2.0 * math.pi
MAGIC = 1.5 * 2.0 ** 23
BIG = 1.0e30


class Steps:

    def __init__(self, eng, sem):
        self.eng, self.sem, self.n = eng, sem, 0

    def __call__(self, ins):
        self.n += 1
        ins.then_inc(self.sem, 1)
        return self.n

    def done(self, n=None):
        self.eng.wait_ge(self.sem, self.n if n is None else n)


class Core:

    def __init__(self, nc, stack):
        self.nc, self.stack, self.sems = nc, stack, []
        stack.callback(self.release)

    def sb(self, name, shape, dt=F32, side="left"):
        return self.stack.enter_context(self.nc.sbuf_tensor(name, shape, dt, side=side))

    def ps(self, name, shape, dt=F32):
        return self.stack.enter_context(self.nc.psum_tensor(name, shape, dt))

    def sem(self, name):
        self.sems.append(self.nc.alloc_semaphore(name))
        return self.sems[-1]

    def release(self):
        if self.sems:
            self.nc.clear_and_free_semaphores(self.sems)
            self.nc.all_engine_barrier()


def constants(core):
    c = {}
    c["ident"] = core.sb("ident", [P, P])
    c["ones"] = core.sb("ones", [P, P])
    c["upto"] = [core.sb("upto_f", [P, P]), core.sb("upto_b", [P, P])]
    return c


def make_constants(pool, c, made):
    step = Steps(pool, made)
    step(pool.memset(c["ones"][:], 1.0))
    step.done()
    one = c["ones"][:]
    step(pool.affine_select(out=c["ident"][:], in_=one, compare_op=ALU.is_equal, fill=0.0, base=0,
                            pattern=[[1, P]], channel_multiplier=-1))
    step(pool.affine_select(out=c["upto"][0][:], in_=one, compare_op=ALU.is_ge, fill=0.0, base=0,
                            pattern=[[1, P]], channel_multiplier=-1))
    step(pool.affine_select(out=c["upto"][1][:], in_=one, compare_op=ALU.is_ge, fill=0.0, base=0,
                            pattern=[[-1, P]], channel_multiplier=1))
    for lv in range(7):
        s, n = 2 ** lv, P // 2 ** (lv + 1)
        for d in range(2):
            v = c["level"][d][:, lv, :].rearrange("p (m a s) -> p m a s", m=n, a=2)
            step(pool.memset(c["level"][d][:, lv, :], 0.0))
            step.done()
            half = v[:, :, d, :]
            ones = one.rearrange("p (m a s) -> p m a s", m=n, a=2)[:, :, 0, :]
            lo = s if d == 0 else 0
            step(pool.affine_select(out=half, in_=ones, compare_op=ALU.is_ge, fill=0.0, base=-lo,
                                    pattern=[[-2 * s, n], [0, s]], channel_multiplier=1))
            step.done()
            step(pool.affine_select(out=half, in_=half, compare_op=ALU.is_ge, fill=0.0, base=lo + s - 1,
                                    pattern=[[2 * s, n], [0, s]], channel_multiplier=-1))
            step.done()


def in_projection(nc, core, c, a, out, tb, y_dram, filled, s5_dram):
    kv, zs, uT, qT, kT = (out[n] for n in ("kv", "zs", "uT", "qT", "kT"))
    hT = core.sb("hT", [P, KT, L])
    wblk = core.sb("wblk", [P, 2, KT, 528])
    work = core.sb("conv_work", [P, 2 * (L + 4) + 2 * L])
    convin = work[:, 0:2 * (L + 4)].rearrange("p (a n) -> p a n", a=2)
    acc = work[:, 2 * (L + 4):].rearrange("p (a n) -> p a n", a=2)
    uS = work[:, 0:NG * T5 * GC].rearrange("p (g n) -> p g n", g=NG)
    act_t = core.sb("conv_silu", [P, L])
    sq = core.sb("square", [P, D])
    xs = kv[:].rearrange("p (t a) n -> p t (a n)", a=2)
    q_rows = uT[:].rearrange("p (t a) n -> p t (a n)", a=4)
    rows = [q_rows, kv[:, 0:TT], kv[:, TT:2 * TT]]
    ss = core.sb("x_ss", [P, TT])
    ms = core.sb("x_ms", [P, TT])
    rs = core.sb("x_rs", [P, TT])
    nss = core.sb("qk_ss", [P, 2, H, TT])
    nrt = core.sb("qk_rt", [P, 2, H, TT])
    nrs = core.sb("qk_rs", [P, 2, H, TT])
    normw = core.sb("norm_mix_w", [P, KT])
    cw = core.sb("conv_w", [P, 5, 12])
    mm_ps = core.ps("proj_ps", [P, 2, 2, 512])
    tr_ps = core.ps("turn_ps", [P, 2, 2, 512])

    made = core.sem("const_made")
    x_ld = [core.sem(f"x_ld{i}") for i in range(4)]
    par_ld = core.sem("par_ld")
    w_ld = [core.sem("w_ld0"), core.sem("w_ld1")]
    x_sq, x_ms, x_rt, x_h, x_tr, x_ev = (core.sem("x_" + n) for n in ("sq", "ms", "rt", "h", "tr", "ev"))
    dv = core.sem("proj_dve_step")
    pj = core.sem("projected")
    pj_ev = core.sem("projected_out")
    cv = core.sem("convolved")
    sl = core.sem("silu_done")
    tr = core.sem("tile_turned")
    tr_ev = core.sem("rows_out")
    sqd = core.sem("squared")
    red = core.sem("squares_summed")
    qk_ss, qk_rt = core.sem("qk_ss_done"), core.sem("qk_rt_done")
    nrm = core.sem("rows_normalised")
    qk_tr, qk_ev = core.sem("qk_turned"), core.sem("qk_out")
    x_rows = a["x"].rearrange("b (t p) d -> p (b t) d", p=P)
    w_in = a["w_in"][0].rearrange("(k p) n -> p k n", p=P)
    starts = [512, 1024, 1536, 2048, 0]
    NJ = 12
    ZH = 528 // 2
    g = gates(core, c, a, out, tb, mm_ps[:, 0, 1, :])

    s5 = s5_discretised(core, c, a, qT[:].rearrange("p h n -> p (h n)"), kT[:].rearrange("p h n -> p (h n)"),
                        [tr_ps[:, 0, 0, :], tr_ps[:, 0, 1, :], tr_ps[:, 1, 0, :]], s5_dram)

    def turned_bank(n):
        return tr_ps[:, n // 2 % 2, n % 2, :]

    def turned_after(t):
        return range(4 * t, 4 * t + 4) if t < 4 else ()

    with nc.Block() as block:
        @block.sync
        def _(sp):
            for i in range(4):
                sp.dma_start(xs[:, 2 * i:2 * i + 2], x_rows[:, 2 * i:2 * i + 2]).then_inc(x_ld[i], 16)
            with nc.allow_non_contiguous_dma(reason="small parameters"):
                sp.dma_start(normw[:], a["norm_mix"][0].rearrange("(k p) -> p k", p=P)).then_inc(par_ld, 16)
                for j in range(5):
                    sp.dma_start(cw[:, j, :], a["gdn_conv_w"][0, j].rearrange("(t p) -> p t", p=P)
                                 ).then_inc(par_ld, 16)
            for n in range(5):
                if n >= 2:
                    sp.wait_ge(pj, 4 * (n - 1))
                cols = 528 if n == 3 else 512
                sp.dma_start(wblk[:, n % 2, :, 0:cols], w_in[:, :, starts[n]:starts[n] + cols]
                             ).then_inc(w_ld[n % 2], 16)
            g.sync(sp)
            s5.spill(sp)
            sp.wait_ge(made, 1)
            fill_expert_rows(sp, c, y_dram, filled)

        @block.gpsimd
        def _(pool):
            make_constants(pool, c, made)
            with nc.allow_non_contiguous_dma(reason="small parameters"):
                s5.loads(pool)

        @block.scalar
        def _(act):
            def silu(j):
                act.wait_ge(cv, j + 1)
                if j >= 1:
                    act.wait_ge(tr, j)
                act.activation(act_t[:], acc[:, j % 2, :], ACT.Silu).then_inc(sl, 1)

            def square(j):
                if j < 8:
                    act.wait_ge(tr_ev, j + 1)
                    if j >= 1:
                        act.wait_ge(red, j)
                    act.activation(sq[:].rearrange("p (t n) -> p t n", n=P),
                                   rows[j // 4][:, :, (j % 4) * P:(j % 4 + 1) * P], ACT.Square).then_inc(sqd, 1)

            def evacuate_x(half):
                for n in range(KT * half, KT * half + KT):
                    k = n % KT
                    act.wait_ge(x_tr, n + 1)
                    act.activation(hT[:, k, half * 512:half * 512 + 512], turned_bank(n), ACT.Copy,
                                   scale=normw[:, k:k + 1]).then_inc(x_ev, 1)

            for t in range(TT):
                act.wait_ge(x_ld[t // 2], 16)
                if t:
                    act.wait_ge(x_sq, t)
                act.activation(sq[:], xs[:, t, :], ACT.Square, accum_out=ss[:, t:t + 1]).then_inc(x_sq, 1)
                if t % 4 == 3:
                    act.wait_ge(x_ms, t // 4 + 1)
                    act.activation(rs[:, t - 3:t + 1], ms[:, t - 3:t + 1], ACT.Sqrt).then_inc(x_rt, 1)
            act.wait_ge(par_ld, 16 * 6)
            evacuate_x(0)
            evacuate_x(1)
            for j in range(NJ):
                if j >= 1:
                    silu(j - 1)
                if j >= 3:
                    square(j - 3)
                act.wait_ge(pj, j + 1)
                if j < 2:
                    act.wait_ge(dv, 2)
                else:
                    act.wait_ge(cv, j - 1)
                act.activation(convin[:, j % 2, 2:2 + L], mm_ps[:, j % 2].rearrange("p a n -> p (a n)"),
                               ACT.Copy).then_inc(pj_ev, 1)
            silu(NJ - 1)
            act.wait_ge(qk_ss, 1)
            act.activation(nrt[:], nss[:], ACT.Sqrt).then_inc(qk_rt, 1)
            for t in range(TT):
                act.wait_ge(pj, NJ + t + 1)
                act.activation(zs[:, t, 0:ZH], mm_ps[:, t % 2, 0, 0:ZH], ACT.Silu)
                act.activation(zs[:, t, ZH:], mm_ps[:, t % 2, 1, 0:DW - ZH], ACT.Silu)
                act.activation(out["ab"][:, t, :], mm_ps[:, t % 2, 1, DW - ZH:ZH], ACT.Copy).then_inc(pj_ev, 1)
                for part in ((0, 1, 2), (3,))[t] if t < 2 else ():
                    s5.act_part(act, part)
            act.wait_ge(pj_ev, NJ + TT)
            g.softplus(act)
            act.wait_ge(sl, NJ)
            for t in range(T5):
                act.wait_ge(pj, NJ + TT + t + 1)
                act.activation(uS[:, :, t * GC:(t + 1) * GC],
                               mm_ps[:, t % 2, 0, :].rearrange("p (g q) -> p g q", q=GC), ACT.Copy
                               ).then_inc(pj_ev, 1)
                if t == 0:
                    act.wait_ge(s5.spilled, 16)
                for n in turned_after(t):
                    act.wait_ge(qk_tr, n + 1)
                    act.activation((qT, kT)[n % 2][:, :, (n // 2) * P:(n // 2 + 1) * P],
                                   turned_bank(n).rearrange("p (h n) -> p h n", h=H), ACT.Copy
                                   ).then_inc(qk_ev, 1)
                if t == 1:
                    g.factors(act)
            for m in range(NG // 4):
                act.wait_ge(qk_tr, 2 * TT + m + 1)
                act.activation(uT[:, 4 * m:4 * m + 4, :],
                               turned_bank(2 * TT + m).rearrange("p (g n) -> p g n", g=4), ACT.Copy
                               ).then_inc(qk_ev, 1)

        @block.tensor
        def _(pe):
            pe.wait_ge(made, 2)
            for n in range(2 * KT):
                half, k = n // KT, n % KT
                pe.wait_ge(x_h, 4 * half + 4)
                if n >= 4:
                    pe.wait_ge(x_ev, n - 3)
                for t in range(4):
                    mm = pe.transpose(turned_bank(n)[:, t * P:(t + 1) * P],
                                      xs[:, 4 * half + t, k * P:(k + 1) * P], c["ident"][:])
                mm.then_inc(x_tr, 1)
            pe.wait_ge(x_ev, 2 * KT)

            def turn(j):
                pe.wait_ge(sl, j + 1)
                if j >= 2:
                    pe.wait_ge(tr_ev, j - 1)
                for t in range(TT):
                    mm = pe.transpose(tr_ps[:, j % 2, t // 4, (t % 4) * P:(t % 4 + 1) * P],
                                      act_t[:, t * P:(t + 1) * P], c["ident"][:])
                mm.then_inc(tr, 1)

            for j in range(NJ):
                blk = j // 4
                if j % 4 == 0:
                    pe.wait_ge(w_ld[blk % 2], 16 * (blk // 2 + 1))
                if j >= 2:
                    pe.wait_ge(pj_ev, j - 1)
                for half in range(2):
                    for k in range(KT):
                        mm = pe.matmul(mm_ps[:, j % 2, half, :], wblk[:, blk % 2, k, (j % 4) * P:(j % 4 + 1) * P],
                                       hT[:, k, half * 512:half * 512 + 512], start=k == 0, stop=k == KT - 1)
                mm.then_inc(pj, 1)
                if j >= 1:
                    turn(j - 1)
            pe.wait_ge(w_ld[1], 32)
            for t in range(TT):
                pe.wait_ge(pj_ev, NJ + t - 1)
                for half in range(2):
                    for k in range(KT):
                        mm = pe.matmul(mm_ps[:, t % 2, half, 0:ZH], hT[:, k, t * P:(t + 1) * P],
                                       wblk[:, 1, k, half * ZH:half * ZH + ZH], start=k == 0, stop=k == KT - 1)
                mm.then_inc(pj, 1)
                if t == 0:
                    turn(NJ - 1)
                    pe.wait_ge(tr_ev, NJ)
                    s5.turn(pe)
            pe.wait_ge(w_ld[0], 48)
            for t in range(T5):
                pe.wait_ge(pj_ev, NJ + TT + t - 1)
                for k in range(KT):
                    mm = pe.matmul(mm_ps[:, t % 2, 0, :], hT[:, k, t:L:T5], wblk[:, 0, k, 0:512],
                                   start=k == 0, stop=k == KT - 1)
                mm.then_inc(pj, 1)
                if t == 0:
                    pe.wait_ge(s5.acts, 1)
                    pe.wait_ge(s5.ev, 8)
                if t == 1:
                    pe.wait_ge(made, 4)
                    g.sums(pe)
                for n in turned_after(t):
                    if n >= 4:
                        pe.wait_ge(qk_ev, n - 3)
                    pe.wait_ge(nrm, n + 1)
                    for h in range(H):
                        mm = pe.transpose(turned_bank(n)[:, h * P:(h + 1) * P],
                                          rows[n % 2][:, n // 2, h * P:(h + 1) * P], c["ident"][:])
                    mm.then_inc(qk_tr, 1)
            pe.wait_ge(pj_ev, NJ + TT + T5)
            for m in range(NG // 4):
                n = 2 * TT + m
                pe.wait_ge(qk_ev, n - 3)
                for x in range(4):
                    mm = pe.transpose(turned_bank(n)[:, x * P:(x + 1) * P], uS[:, 4 * m + x, :], c["ident"][:])
                mm.then_inc(qk_tr, 1)

        @block.vector
        def _(dve):
            step = Steps(dve, dv)
            step(dve.memset(convin[:, :, 0:2], 0.0))
            step(dve.memset(convin[:, :, L + 2:L + 4], 0.0))
            for half in range(2):
                ts = slice(4 * half, 4 * half + 4)
                dve.wait_ge(x_sq, 4 * half + 4)
                dve.tensor_scalar(ms[:, ts], ss[:, ts], 1.0 / D, EPS, ALU.mult, ALU.add).then_inc(x_ms, 1)
                dve.wait_ge(x_rt, half + 1)
                step(dve.reciprocal(ms[:, ts], rs[:, ts]))
                step.done()
                for t in range(4 * half, 4 * half + 4):
                    dve.tensor_scalar(xs[:, t, :], xs[:, t, :], ms[:, t:t + 1], None, ALU.mult).then_inc(x_h, 1)

            def rows_out(j):
                dve.wait_ge(tr, j + 1)
                if j == 0:
                    dve.wait_ge(x_tr, 2 * KT)
                dve.tensor_copy(rows[j // 4][:, :, (j % 4) * P:(j % 4 + 1) * P],
                                tr_ps[:, j % 2].rearrange("p a (t n) -> p (a t) n", n=P)).then_inc(tr_ev, 1)

            def sum_squares(j):
                if 0 <= j < 8:
                    dve.wait_ge(sqd, j + 1)
                    dve.tensor_reduce(nss[:, j // 4, j % 4, :], sq[:].rearrange("p (t n) -> p t n", n=P),
                                      AX.X, ALU.add).then_inc(red, 1)

            for j in range(NJ):
                dve.wait_ge(pj_ev, j + 1)
                if j >= 2:
                    dve.wait_ge(sl, j - 1)
                src = convin[:, j % 2, :]
                step(dve.tensor_scalar(acc[:, j % 2, :], src[:, 0:L], cw[:, 0, j:j + 1], None, ALU.mult))
                for tap in range(1, 5):
                    step.done()
                    ins = dve.scalar_tensor_tensor(out=acc[:, j % 2, :], in0=src[:, tap:tap + L],
                                                   scalar=cw[:, tap, j:j + 1], in1=acc[:, j % 2, :],
                                                   op0=ALU.mult, op1=ALU.add)
                    if tap < 4:
                        step(ins)
                ins.then_inc(cv, 1)
                if j >= 2:
                    rows_out(j - 2)
                    sum_squares(j - 3)
            rows_out(NJ - 2)
            s5.first(dve)
            dve.wait_ge(red, 8)
            dve.tensor_scalar(nss[:], nss[:], EPS, None, ALU.add).then_inc(qk_ss, 1)
            rows_out(NJ - 1)
            dve.wait_ge(qk_rt, 1)
            step(dve.reciprocal(nrs[:], nrt[:]))
            step.done()
            step(dve.tensor_scalar(nrs[:, 0], nrs[:, 0], DH ** -0.5, None, ALU.mult))
            step.done()
            s5.factors(dve)
            dve.wait_ge(tr_ev, NJ)
            for n in range(2 * TT):
                t = n // 2
                if n == 4:
                    dve.wait_ge(pj_ev, NJ + TT)
                    g.decays(dve)
                if n == 12:
                    g.totals(dve)
                view = rows[n % 2][:, t, :].rearrange("p (h d) -> p h d", h=H)
                scale = nrs[:, n % 2, :, t:t + 1].broadcast_to([P, H, DH])
                dve.tensor_tensor(view, view, scale, ALU.mult).then_inc(nrm, 1)


def persistent(low, core):
    return {
        "uT": low.sb("uT", [P, NG, NC5]),
        "qT": low.sb("qT", [P, H, L]),
        "kT": core.sb("kT", [P, H, L]),
        "kv": core.sb("kv_rows", [P, 2 * TT, DW]),
        "zs": core.sb("silu_z", [P, TT, DW]),
        "ab": core.sb("ab", [P, TT, 16]),
    }


def fill_expert_rows(sp, c, y_dram, filled):
    n = L * 2 // P
    rows = y_dram[n * P:, :].rearrange("(b p) (r c) -> p b r c", p=P, c=P)
    for b in range(rows.shape[1]):
        ones = c["ones"][:].rearrange("p (r c) -> p r c", r=1).broadcast_to([P, D // P, P])
        sp.dma_start(rows[:, b], ones).then_inc(filled, 16)


class gates:

    def __init__(self, core, c, a, out, tb, bank):
        self.c, self.a, self.tb, self.bank = c, a, tb, bank
        self.par = core.sb("gate_par", [P, 2, 8])
        self.t1 = core.sb("gate_t1", [P, TT, 8])
        self.t2 = core.sb("gate_t2", [P, TT, 8])
        self.t3 = core.sb("gate_t3", [P, TT, 8])
        self.ld, self.v, self.s, self.m = (core.sem("gate_" + n) for n in ("ld", "dve", "act", "pe"))
        self.xa, self.xb = out["ab"][:, :, 0:8], out["ab"][:, :, 8:16]

    def sync(self, sp):
        for i, name in enumerate(("gdn_dt_bias", "gdn_a_log")):
            sp.dma_start(self.par[:, i, :], self.a[name].rearrange("o d h -> o (d h)").partition_broadcast(P)
                         ).then_inc(self.ld, 16)

    def decays(self, dve):
        t1, par, s = self.t1, self.par, self.s
        self.step = step = Steps(dve, self.v)
        dve.wait_ge(self.ld, 32)
        bias = par[:, 0:1, :].broadcast_to([P, TT, 8])
        step(dve.tensor_tensor(t1[:], self.xa, bias, ALU.add))
        dve.wait_ge(s, 4)
        step(dve.tensor_scalar(t1[:], t1[:], 0.0, None, ALU.max))
        step.done()
        step(dve.tensor_tensor(t1[:], t1[:], self.t2[:], ALU.add))
        step.done()
        step(dve.scalar_tensor_tensor(out=self.tb["g"][:], in0=t1[:], scalar=-1.0,
                                      in1=par[:, 1:2, :].broadcast_to([P, TT, 8]),
                                      op0=ALU.mult, op1=ALU.mult))

    def totals(self, dve):
        tb, step, bank = self.tb, self.step, self.bank
        dve.wait_ge(self.m, 1)
        step(dve.tensor_copy(tb["G"][:, :, 0:4], bank[:, 0:32].rearrange("p (t h) -> p t h", h=4)))
        step(dve.tensor_copy(tb["G"][:, :, 4:8], bank[:, 32:64].rearrange("p (t h) -> p t h", h=4)))
        step(dve.tensor_copy(self.t2[:], bank[:, 64:128].rearrange("p (t h) -> p t h", h=8)))
        step.done()
        step(dve.tensor_tensor(self.t3[:], self.t2[:], tb["G"][:], ALU.subtract))
        dve.wait_ge(self.s, 6)
        step(dve.tensor_tensor(tb["betaG"][:], tb["beta"][:], tb["eG"][:], ALU.mult))

    def softplus(self, act):
        t1, t2, par, s = self.t1, self.t2, self.par, self.s
        act.wait_ge(self.v, 1)
        act.activation(t2[:], t1[:], ACT.Abs).then_inc(s, 1)
        act.wait_ge(s, 1)
        act.activation(t2[:], t2[:], ACT.Exp, scale=-1.0).then_inc(s, 1)
        act.wait_ge(s, 2)
        act.activation(t2[:], t2[:], ACT.Ln, bias=1.0).then_inc(s, 1)
        act.activation(par[:, 1, :], par[:, 1, :], ACT.Exp).then_inc(s, 1)
        act.activation(self.tb["beta"][:], self.xb, ACT.Sigmoid).then_inc(s, 1)

    def factors(self, act):
        tb, s = self.tb, self.s
        act.wait_ge(self.v, 8)
        act.activation(tb["eG"][:], tb["G"][:], ACT.Exp).then_inc(s, 1)
        act.activation(tb["eTot"][:], self.t2[:], ACT.Exp)
        act.activation(tb["kdec"][:], self.t3[:], ACT.Exp).then_inc(s, 1)

    def sums(self, pe):
        g = self.tb["g"]
        pe.wait_ge(self.v, 4)
        for d in range(2):
            pe.matmul(self.bank[:, 32 * d:32 * d + 32], self.c["upto"][d][:], g[:, :, 4 * d:4 * d + 4],
                      start=True, stop=True)
        pe.matmul(self.bank[:, 64:128], self.c["ones"][:], g[:].rearrange("p t h -> p (t h)"),
                  start=True, stop=True).then_inc(self.m, 1)


def gate_tables(core):
    return {n: core.sb("tab_" + n, [P, TT, 8]) for n in ("g", "G", "beta", "eG", "eTot", "kdec", "betaG")}


def delta_schedule():
    prepare = ["decay", "scores", "first"]
    for t in range(-1, TT + 1):
        if t < 0:
            steps = [(name, 0, 0) for name in prepare]
        elif t == TT:
            steps = [("read_state", 0, t - 1), ("new_state", 0, t - 1)]
        else:
            steps = []
            for lv in range(1, 7):
                steps.append(("z", lv, t))
                if lv <= 2 and t >= 1:
                    steps.append((("read_state", "new_state")[lv - 1], 0, t - 1))
                if 3 <= lv <= 5 and t + 1 < TT:
                    steps.append((prepare[lv - 3], 0, t + 1))
                steps.append(("d", lv, t))
                if lv < 6:
                    steps.append(("turn", lv, t))
            steps.append(("solve", 0, t))
        for name, lv, at in steps:
            for d in range(2):
                yield name, lv, at, d


def delta_net(nc, core, c, a, out, tb, o_sum):
    qT, kT, kv = out["qT"], out["kT"], out["kv"]

    def buf(name, n=1):
        return [core.sb(f"{name}{d}", [P, n, H, P]) for d in range(2)]

    e_b, ab_b, as_b, t_b, tt_b, z_b = (buf("decay"), buf("amat", 2), buf("alev", 2), buf("T", 2), buf("TT", 2),
                                       buf("zc"))
    at_b, u_b, w_b, vb_b, kbg_b, kd_b = buf("attn", 2), buf("u"), buf("wT"), buf("vb"), buf("kbg"), buf("kdec")
    vn_b, tmp_b, s_b, sd_b = buf("vnew"), buf("otmp"), buf("state"), buf("state_dec")
    X = [core.ps(f"bank_x{d}", [P, H, P]) for d in range(2)]
    Y = [core.ps(f"bank_y{d}", [P, H, P]) for d in range(2)]
    V = [core.ps(f"bank_v{d}", [P, H, P]) for d in range(2)]
    O = [core.ps(f"bank_o{d}", [P, H, P]) for d in range(2)]
    names = ("gsum kk kq diff absd decay masked betad amat attn alev t_first tt_first tt0 tt z zc dd turned t "
             "u_mm w_mm u w vb kbg kd ws qs vnew o_part av kv o o_added s_dec state tmp0").split()
    S = {n: [core.sem(f"dn_{n}{d}") for d in range(2)] for n in names}

    def chunk(t, d):
        return t if d == 0 else TT - 1 - t

    def cols(t, d):
        ch = chunk(t, d)
        return slice(ch * P, ch * P + P)

    def per_head(table, t, d):
        return table[:, chunk(t, d), 4 * d:4 * d + 4].rearrange("p (h o) -> p h o", o=1).broadcast_to([P, H, P])

    def rows(which, t, d):
        return kv[:, which * TT + chunk(t, d), :].rearrange("p (h n) -> p h n", h=H)

    def over_heads(m):
        return m.rearrange("p (o n) -> p o n", o=1).broadcast_to([P, H, P])

    with nc.Block() as block:
        @block.tensor
        def _(pe):
            def wait(name, d, n):
                if n > 0:
                    pe.wait_ge(S[name][d], n)

            def heads(dst, lhs, rhs):
                for h in range(H):
                    mm = pe.matmul(dst[:, h, :], lhs(h), rhs(h), start=True, stop=True)
                return mm

            for name, lv, t, d in delta_schedule():
                cs, b = cols(t, d), t % 2
                if name == "decay":
                    wait("o", d, t - 1)
                    heads(V[d], lambda h: tb["g"][:, chunk(t, d), 4 * d + h:4 * d + h + 1].broadcast_to([P, P]),
                          lambda h: c["upto"][d][:]).then_inc(S["gsum"][d], 1)
                    wait("state", d, t)
                    heads(O[d], lambda h: kT[:, h, cs], lambda h: kT[:, h, cs]).then_inc(S["kk"][d], 1)
                elif name == "scores":
                    wait("diff", d, t + 1)
                    heads(V[d], lambda h: kT[:, h, cs], lambda h: qT[:, h, cs]).then_inc(S["kq"][d], 1)
                elif name == "first":
                    wait("t_first", d, t + 1)
                    wait("amat", d, t + 1)
                    for h in range(H):
                        mm = pe.transpose(O[d][:, h, :], t_b[d][:, b, h, :], c["ident"][:])
                    mm.then_inc(S["tt_first"][d], 1)
                elif name == "z":
                    wait("alev", d, 6 * t + lv)
                    if lv == 1:
                        wait("tt0", d, t + 1)
                        wait("u", d, t)
                    else:
                        wait("tt", d, 6 * t + lv - 1)
                        wait("t", d, 5 * t + lv - 1)
                    heads(X[d], lambda h: as_b[d][:, (lv - 1) % 2, h, :], lambda h: tt_b[d][:, b, h, :]
                          ).then_inc(S["z"][d], 1)
                elif name == "d":
                    wait("zc", d, 6 * t + lv)
                    if lv == 1:
                        wait("w", d, t)
                    heads(Y[d], lambda h: t_b[d][:, b, h, :], lambda h: z_b[d][:, 0, h, :]
                          ).then_inc(S["dd"][d], 1)
                elif name == "turn":
                    wait("tt", d, 6 * t + lv)
                    for h in range(H):
                        mm = pe.transpose(X[d][:, h, :], tt_b[d][:, b, h, :], c["ident"][:])
                    mm.then_inc(S["turned"][d], 1)
                elif name == "solve":
                    wait("tt", d, 6 * t + 6)
                    wait("vb", d, t + 1)
                    heads(X[d], lambda h: tt_b[d][:, b, h, :], lambda h: vb_b[d][:, 0, h, :]
                          ).then_inc(S["u_mm"][d], 1)
                    wait("kbg", d, t + 1)
                    heads(Y[d], lambda h: kbg_b[d][:, 0, h, :], lambda h: tt_b[d][:, b, h, :]
                          ).then_inc(S["w_mm"][d], 1)
                elif name == "read_state":
                    wait("w", d, t + 1)
                    wait("state", d, t + 1)
                    wait("attn", d, min(t + 2, TT))
                    heads(V[d], lambda h: w_b[d][:, 0, h, :], lambda h: s_b[d][:, 0, h, :]).then_inc(S["ws"][d], 1)
                    wait("tt0", d, min(t + 2, TT))
                    heads(O[d], lambda h: qT[:, h, cs], lambda h: s_b[d][:, 0, h, :]).then_inc(S["qs"][d], 1)
                elif name == "new_state":
                    wait("vnew", d, t + 1)
                    heads(V[d], lambda h: at_b[d][:, t % 2, h, :], lambda h: vn_b[d][:, 0, h, :]
                          ).then_inc(S["av"][d], 1)
                    wait("o_part", d, t + 1)
                    wait("kd", d, t + 1)
                    heads(O[d], lambda h: kd_b[d][:, 0, h, :], lambda h: vn_b[d][:, 0, h, :]
                          ).then_inc(S["kv"][d], 1)

        @block.vector
        def _(dve):
            def wait(name, d, n):
                if n > 0:
                    dve.wait_ge(S[name][d], n)

            for d in range(2):
                dve.memset(s_b[d][:], 0.0).then_inc(S["state"][d], 1)
            for name, lv, t, d in delta_schedule():
                ch, b = chunk(t, d), t % 2
                if name == "decay":
                    wait("gsum", d, t + 1)
                    wait("betad", d, t)
                    dve.tensor_tensor(e_b[d][:, 0], per_head(tb["G"], t, d), V[d][:], ALU.subtract
                                      ).then_inc(S["diff"][d], 1)
                elif name == "scores":
                    wait("kk", d, t + 1)
                    wait("betad", d, t + 1)
                    dve.tensor_tensor(ab_b[d][:, b], O[d][:], ab_b[d][:, b], ALU.mult).then_inc(S["amat"][d], 1)
                    wait("amat", d, t + 1)
                    wait("dd", d, 6 * (t - 1))
                    dve.tensor_tensor(t_b[d][:, b], ab_b[d][:, b], over_heads(c["level"][d][:, 0, :]), ALU.mult
                                      ).then_inc(S["tmp0"][d], 1)
                    wait("tmp0", d, t + 1)
                    dve.tensor_tensor(t_b[d][:, b], over_heads(c["ident"][:]), t_b[d][:, b], ALU.subtract
                                      ).then_inc(S["t_first"][d], 1)
                    wait("kq", d, t + 1)
                    wait("masked", d, t + 1)
                    dve.tensor_tensor(at_b[d][:, b], V[d][:], at_b[d][:, b], ALU.mult).then_inc(S["attn"][d], 1)
                elif name == "first":
                    wait("tt_first", d, t + 1)
                    wait("w_mm", d, t - 1)
                    dve.tensor_copy(tt_b[d][:, b], O[d][:]).then_inc(S["tt0"][d], 1)
                elif name == "d":
                    wait("dd", d, 6 * t + lv)
                    if lv == 1:
                        wait("tt0", d, t + 1)
                    else:
                        wait("tt", d, 6 * t + lv - 1)
                    dve.tensor_tensor(tt_b[d][:, b], tt_b[d][:, b], Y[d][:], ALU.subtract).then_inc(S["tt"][d], 1)
                elif name == "read_state":
                    wait("ws", d, t + 1)
                    wait("u", d, t + 1)
                    dve.tensor_tensor(vn_b[d][:, 0], u_b[d][:, 0], V[d][:], ALU.subtract).then_inc(S["vnew"][d], 1)
                    wait("qs", d, t + 1)
                    wait("o", d, t)
                    wait("o_added", d, t - 4)
                    dve.tensor_tensor(tmp_b[d][:, 0], O[d][:], per_head(tb["eG"], t, d), ALU.mult
                                      ).then_inc(S["o_part"][d], 1)
                elif name == "new_state":
                    wait("av", d, t + 1)
                    wait("o_part", d, t + 1)
                    dst = o_sum[:, ch, :].rearrange("p (h n) -> p h n", h=H) if t < TT // 2 else tmp_b[d][:, 0]
                    dve.tensor_tensor(dst, tmp_b[d][:, 0], V[d][:], ALU.add).then_inc(S["o"][d], 1)
                    wait("kv", d, t + 1)
                    wait("s_dec", d, t + 1)
                    dve.tensor_tensor(s_b[d][:, 0], sd_b[d][:, 0], O[d][:], ALU.add).then_inc(S["state"][d], 1)

        @block.scalar
        def _(act):
            def wait(name, d, n):
                if n > 0:
                    act.wait_ge(S[name][d], n)

            for name, lv, t, d in delta_schedule():
                if name == "decay":
                    wait("diff", d, t + 1)
                    act.activation(e_b[d][:, 0], e_b[d][:, 0], ACT.Abs).then_inc(S["absd"][d], 1)
                    wait("absd", d, t + 1)
                    act.activation(e_b[d][:, 0], e_b[d][:, 0], ACT.Exp, scale=-1.0).then_inc(S["decay"][d], 1)
                elif name == "z":
                    wait("z", d, 6 * t + lv)
                    act.activation(z_b[d][:, 0], X[d][:], ACT.Copy).then_inc(S["zc"][d], 1)
                elif name == "turn":
                    wait("turned", d, 5 * t + lv)
                    act.activation(t_b[d][:, t % 2], X[d][:], ACT.Copy).then_inc(S["t"][d], 1)
                elif name == "solve":
                    wait("u_mm", d, t + 1)
                    wait("vnew", d, t)
                    act.activation(u_b[d][:, 0], X[d][:], ACT.Copy).then_inc(S["u"][d], 1)
                    wait("w_mm", d, t + 1)
                    act.activation(w_b[d][:, 0], Y[d][:], ACT.Copy).then_inc(S["w"][d], 1)

        @block.gpsimd
        def _(pool):
            def wait(name, d, n):
                if n > 0:
                    pool.wait_ge(S[name][d], n)

            def level(t, lv, d):
                wait("amat", d, t + 1)
                wait("z", d, 6 * t + lv - 2)
                pool.tensor_tensor(as_b[d][:, lv % 2 ^ 1], ab_b[d][:, t % 2], over_heads(c["level"][d][:, lv, :]),
                                   ALU.mult).then_inc(S["alev"][d], 1)

            for name, lv, t, d in delta_schedule():
                ch = chunk(t, d)
                if name == "decay":
                    wait("decay", d, t + 1)
                    wait("av", d, t - 1)
                    pool.tensor_tensor(at_b[d][:, t % 2], e_b[d][:, 0], over_heads(c["upto"][d][:]), ALU.mult
                                       ).then_inc(S["masked"][d], 1)
                    wait("alev", d, 6 * (t - 1))
                    pool.tensor_tensor(ab_b[d][:, t % 2], e_b[d][:, 0], per_head(tb["beta"], t, d), ALU.mult
                                       ).then_inc(S["betad"][d], 1)
                elif name == "first" and t == 0:
                    level(0, 1, d)
                    level(0, 2, d)
                elif name == "z":
                    if lv <= 4:
                        level(t, lv + 2, d)
                    elif t + 1 < TT:
                        level(t + 1, lv - 4, d)
                    if lv == 3:
                        wait("u_mm", d, t)
                        pool.tensor_tensor(vb_b[d][:, 0], rows(1, t, d), per_head(tb["beta"], t, d), ALU.mult
                                           ).then_inc(S["vb"][d], 1)
                    elif lv == 4:
                        wait("w_mm", d, t)
                        pool.tensor_tensor(kbg_b[d][:, 0], rows(0, t, d), per_head(tb["betaG"], t, d), ALU.mult
                                           ).then_inc(S["kbg"][d], 1)
                elif name == "read_state":
                    wait("kv", d, t)
                    pool.tensor_tensor(kd_b[d][:, 0], rows(0, t, d), per_head(tb["kdec"], t, d), ALU.mult
                                       ).then_inc(S["kd"][d], 1)
                    wait("state", d, t + 1)
                    pool.tensor_tensor(sd_b[d][:, 0], s_b[d][:, 0], per_head(tb["eTot"], t, d), ALU.mult
                                       ).then_inc(S["s_dec"][d], 1)
                elif name == "new_state" and t >= TT // 2:
                    wait("o", d, t + 1)
                    wait("o", 1 - d, TT - t)
                    acc = o_sum[:, ch, :].rearrange("p (h n) -> p h n", h=H)
                    pool.tensor_tensor(acc, acc, tmp_b[d][:, 0], ALU.add).then_inc(S["o_added"][d], 1)


COOKED = (("B", 2 * 2 * NP5 * GC), ("C", 2 * 2 * NP5 * GC), ("pw", 2 * (T5 + 1) * 2 * NP5),
          ("npi", (T5 + 1) * 2 * NP5), ("tau", 2 * NP5), ("rho", 2 * NP5))
COOKED_COLS = sum(n for _, n in COOKED)


def s5_cooked(flat):
    parts, at = {}, 0
    for name, n in COOKED:
        parts[name] = flat[:, at:at + n]
        at += n
    for name in ("B", "C"):
        parts[name] = parts[name].rearrange("p (i j q) -> p i j q", i=2, q=GC)
    parts["pw"] = parts["pw"].rearrange("p (i k j) -> p i k j", i=2, k=T5 + 1)
    parts["npi"] = parts["npi"].rearrange("p (k j) -> p k j", k=T5 + 1)
    return parts


class s5_discretised:

    def __init__(self, core, c, a, space, results, banks, dram):
        DJ = 2 * NP5
        self.c, self.a, self.banks, self.dram = c, a, banks, dram
        at = 0

        def take(n):
            nonlocal at
            at += n
            return space[:, at - n:at]

        BC = take(2 * DJ * GC + 8 * P)
        self.B = BC[:, 0:2 * DJ * GC].rearrange("p (i j q) -> p i j q", i=2, j=DJ)
        self.Cn = BC[:, 2 * DJ * GC:].rearrange("p (i n) -> p i n", i=8)
        self.raw = take(3 * P)[0:DJ].rearrange("p (i n) -> p i n", i=3)
        self.ldt = take(2)[0:DJ]
        self.lam = take(3 * DJ).rearrange("p (i n) -> p i n", i=3)
        self.s = take(17 * DJ).rearrange("p (i n) -> p i n", i=17)
        self.cooked = results[:, 0:COOKED_COLS]
        self.tmp = results[:, COOKED_COLS:COOKED_COLS + DJ * GC]
        self.ld, self.v, self.acts, self.m, self.ev, self.spilled = (
            core.sem("s5d_" + n) for n in ("ld", "dve", "act", "pe", "c_out", "spilled"))
        self.made = {n: core.sem("s5d_made_" + n) for n in ("ar", "theta", "cooked")}

    N_LD = 2 + 1 + 2 + 64
    RE, DTC, AR, TH, TN, EM, EE, SN, SH, DR, DI, MM, T1, T2, QR, QI, TAU = range(17)

    def loads(self, eng):
        a, ld = self.a, self.ld
        for i, n in enumerate(("s5_lam_re", "s5_lam_im")):
            eng.dma_start(self.raw[:, i, :], a[n][0].rearrange("d (j a) n -> (d j) (a n)", a=2)).then_inc(ld, 16)
        eng.dma_start(self.ldt, a["s5_log_dt"][0].rearrange("d (j a) -> (d j) a", a=2)).then_inc(ld, 16)
        for i, n in enumerate(("s5_b_re", "s5_b_im")):
            eng.dma_start(self.B[:, i], a[n][0].rearrange("d (j a) n q -> (a n) (d j) q", a=2)).then_inc(ld, 16)
        for i, n in enumerate(("s5_c_re", "s5_c_im")):
            for d in range(2):
                for half in range(2):
                    src = a[n][0, d].rearrange("(h j a) p n -> h j p a n", h=2, a=2)[half]
                    for j in range(8):
                        eng.dma_start(self.Cn[j * GC:(j + 1) * GC, 4 * i + 2 * d + half, :]
                                      .rearrange("p (a n) -> p a n", a=2), src[j]).then_inc(ld, 16)

    def spill(self, sp):
        sp.wait_ge(self.made["cooked"], 1)
        sp.wait_ge(self.ev, 8)
        sp.dma_start(self.dram, self.cooked).then_inc(self.spilled, 16)

    def turn(self, pe):
        DJ, ident = 2 * NP5, self.c["ident"]
        pe.wait_ge(self.ld, 16 * self.N_LD)
        pe.wait_ge(self.v, 1)
        for i in range(3):
            mm = pe.transpose(self.banks[0][:, i * DJ:(i + 1) * DJ], self.raw[:, i, :], ident[0:DJ, 0:DJ])
        mm.then_inc(self.m, 1)
        for i in range(8):
            mm = pe.transpose(self.banks[1 + i // 4][:, (i % 4) * P:(i % 4 + 1) * P], self.Cn[:, i, :], ident[:])
        mm.then_inc(self.m, 1)

    def act_part(self, act, part):
        s, lam, DJ = self.s, self.lam, 2 * NP5
        if part == 0:
            act.wait_ge(self.m, 1)
            act.activation(lam.rearrange("p i n -> p (i n)"), self.banks[0][:, 0:3 * DJ], ACT.Copy
                           ).then_inc(self.acts, 1)
            act.wait_ge(self.acts, 1)
            act.activation(s[:, self.DTC], lam[:, 2], ACT.Exp).then_inc(self.acts, 1)
        elif part == 1:
            act.wait_ge(self.made["ar"], 1)
            act.activation(s[:, self.TN], s[:, self.AR], ACT.Tanh, scale=0.5).then_inc(self.acts, 1)
        elif part == 2:
            act.wait_ge(self.made["theta"], 1)
            act.activation(s[:, self.SN], s[:, self.TH], ACT.Sin).then_inc(self.acts, 1)
            act.activation(s[:, self.SH], s[:, self.TH], ACT.Sin, scale=0.5).then_inc(self.acts, 1)
        elif part == 3:
            C = s5_cooked(self.cooked)["C"]
            act.wait_ge(self.m, 2)
            for i in range(8):
                ri, d, half = i // 4, (i // 2) % 2, i % 2
                dj = NP5 * d + 8 * half
                act.activation(C[:, ri, dj:dj + 8, :], self.banks[1 + i // 4][:, (i % 4) * P:(i % 4 + 1) * P]
                               .rearrange("p (j q) -> p j q", q=GC), ACT.Copy).then_inc(self.ev, 1)

    def first(self, dve):
        self.step = Steps(dve, self.v)
        dve.wait_ge(self.ld, 16 * self.N_LD)
        self.step(dve.tensor_copy(self.raw[:, 2, :].rearrange("p (a n) -> p a n", a=2),
                                  self.ldt.rearrange("p (a o) -> p a o", o=1).broadcast_to([2 * NP5, 2, NS])))

    def factors(self, dve):
        DJ, s, lam, step, made = 2 * NP5, self.s, self.lam, self.step, self.made
        RE, DTC, AR, TH, TN, EM, EE, SN, SH, DR, DI, MM, T1, T2, QR, QI, TAU = range(17)
        out = s5_cooked(self.cooked)
        TTo, STT = dve.tensor_tensor, dve.scalar_tensor_tensor

        def ew(dst, x, y, op, mark=None, n=1):
            step.done()
            if mark is None:
                step(TTo(dst, x, y, op))
            else:
                TTo(dst, x, y, op).then_inc(made[mark], 1)
                dve.wait_ge(made[mark], n)

        dve.wait_ge(self.acts, 2)
        step(dve.tensor_scalar(s[:, RE], lam[:, 0], -1e-4, None, ALU.min))
        ew(s[:, AR], s[:, RE], s[:, DTC], ALU.mult, "ar")
        step(TTo(s[:, TH], lam[:, 1], s[:, DTC], ALU.mult))
        step.done()
        step(dve.tensor_scalar(s[:, T1], s[:, TH], 1.0 / TWO_PI, MAGIC, ALU.mult, ALU.add))
        step.done()
        step(dve.tensor_scalar(s[:, T1], s[:, T1], MAGIC, None, ALU.subtract))
        step.done()
        step(STT(out=s[:, TH], in0=s[:, T1], scalar=-6.28125, in1=s[:, TH], op0=ALU.mult, op1=ALU.add))
        step.done()
        step(STT(out=s[:, TH], in0=s[:, T1], scalar=-(TWO_PI - 6.28125), in1=s[:, TH],
                 op0=ALU.mult, op1=ALU.add))
        step.done()
        dve.tensor_scalar(s[:, TH], s[:, TH], 3.141592, -3.141592, ALU.min, ALU.max).then_inc(made["theta"], 1)
        dve.wait_ge(made["theta"], 1)
        step(dve.tensor_scalar(s[:, TAU], s[:, TH], T5 / TWO_PI, None, ALU.mult))
        step.done()
        step(dve.tensor_scalar(s[:, T1], s[:, TAU], MAGIC, MAGIC, ALU.add, ALU.subtract))
        ew(out["tau"], s[:, TAU], s[:, T1], ALU.subtract)
        dve.wait_ge(self.acts, 3)
        step.done()
        step(dve.tensor_scalar(s[:, T1], s[:, TN], -1.0, 1.0, ALU.mult, ALU.add))
        step.done()
        step(dve.reciprocal(s[:, T2], s[:, T1]))
        step.done()
        step(STT(out=s[:, EM], in0=s[:, TN], scalar=2.0, in1=s[:, T2], op0=ALU.mult, op1=ALU.mult))
        step.done()
        step(dve.tensor_scalar(s[:, EE], s[:, EM], 1.0, None, ALU.add))
        dve.wait_ge(self.acts, 5)
        step.done()
        step(STT(out=s[:, T1], in0=s[:, SH], scalar=-2.0, in1=s[:, SH], op0=ALU.mult, op1=ALU.mult))
        step.done()
        step(dve.tensor_scalar(s[:, T2], s[:, T1], 1.0, None, ALU.add))
        ew(s[:, T2], s[:, T2], s[:, EM], ALU.mult)
        ew(s[:, DR], s[:, T2], s[:, T1], ALU.add)
        ew(s[:, DI], s[:, EE], s[:, SN], ALU.mult)
        ew(s[:, T1], s[:, RE], s[:, RE], ALU.mult)
        ew(s[:, T2], lam[:, 1], lam[:, 1], ALU.mult)
        ew(s[:, MM], s[:, T1], s[:, T2], ALU.add)
        step.done()
        step(dve.reciprocal(s[:, MM], s[:, MM]))
        ew(s[:, T1], s[:, DR], s[:, RE], ALU.mult)
        ew(s[:, T2], s[:, DI], lam[:, 1], ALU.mult)
        ew(s[:, T1], s[:, T1], s[:, T2], ALU.add)
        ew(s[:, QR], s[:, T1], s[:, MM], ALU.mult)
        ew(s[:, T1], s[:, DI], s[:, RE], ALU.mult)
        ew(s[:, T2], s[:, DR], lam[:, 1], ALU.mult)
        ew(s[:, T1], s[:, T1], s[:, T2], ALU.subtract)
        ew(s[:, QI], s[:, T1], s[:, MM], ALU.mult)
        ew(out["rho"], s[:, EE], s[:, EE], ALU.mult)
        ew(out["rho"], out["rho"], out["rho"], ALU.mult)
        ew(out["rho"], out["rho"], out["rho"], ALU.mult)
        step(dve.memset(out["pw"][:, 0, 0, :], 1.0))
        step(dve.memset(out["pw"][:, 1, 0, :], 0.0))
        step(dve.tensor_scalar(out["pw"][:, 0, 1, :], s[:, DR], 1.0, None, ALU.add))
        step(dve.tensor_copy(out["pw"][:, 1, 1, :], s[:, DI]))
        tmp = self.tmp[:, 0:4 * DJ].rearrange("p (k n) -> p k n", k=4)
        for w in (1, 2, 4):
            xr = out["pw"][:, 0, w:w + 1, :].broadcast_to([P, w, DJ])
            xi = out["pw"][:, 1, w:w + 1, :].broadcast_to([P, w, DJ])
            yr, yi = out["pw"][:, 0, 1:w + 1, :], out["pw"][:, 1, 1:w + 1, :]
            zr, zi = out["pw"][:, 0, w + 1:2 * w + 1, :], out["pw"][:, 1, w + 1:2 * w + 1, :]
            ew(zr, xr, yr, ALU.mult)
            ew(tmp[:, 0:w], xi, yi, ALU.mult)
            ew(zr, zr, tmp[:, 0:w], ALU.subtract)
            ew(zi, xr, yi, ALU.mult)
            ew(tmp[:, 0:w], xi, yr, ALU.mult)
            ew(zi, zi, tmp[:, 0:w], ALU.add)

        def spread(x, n):
            return x.rearrange("p (j o) -> p j o", o=1).broadcast_to([P, x.shape[1], n])

        qr, qi = spread(s[:, QR], GC), spread(s[:, QI], GC)
        t16 = self.tmp.rearrange("p (j q) -> p j q", j=DJ)
        ew(out["B"][:, 0], qr, self.B[:, 0], ALU.mult)
        ew(t16, qi, self.B[:, 1], ALU.mult)
        ew(out["B"][:, 0], out["B"][:, 0], t16, ALU.subtract)
        ew(out["B"][:, 1], qr, self.B[:, 1], ALU.mult)
        ew(t16, qi, self.B[:, 0], ALU.mult)
        ew(out["B"][:, 1], out["B"][:, 1], t16, ALU.add)
        step.done()
        dve.tensor_scalar(out["npi"], out["pw"][:, 1], -1.0, None, ALU.mult).then_inc(made["cooked"], 1)


def s5_tables(core, G, x1):
    return {
        "E": core.sb("s5_E", [P, 2 * NP5, 2, P]),
        "G": G,
        "M": core.sb("s5_M", [P, NG, P]),
        "cos": x1[:, 0:4, :].rearrange("p t (j n) -> p (t j) n", n=NC5),
        "sin": x1[:, 4:8, :].rearrange("p t (j n) -> p (t j) n", n=NC5),
    }


def s5_mixer(nc, core, c, a, cooked, cooked_ld, uT, yT, G, x1, wo, next_ld):
    tb, k5 = s5_tables(core, G, x1), s5_cooked(cooked[:])
    E, G, M = tb["E"], tb["G"], tb["M"]
    small = core.sb("s5_small", [P, 4608])
    sizes = dict(rot=1024, z=1024, zs=512, back=1024, state=1024)
    cuts = [sum(list(sizes.values())[:i]) for i in range(5)]
    rot, z, back, st = (small[:, cuts[i]:cuts[i] + 1024].rearrange("p (s d r n) -> p s d r n", s=2, d=2, r=2)
                        for i in (0, 1, 3, 4))
    zs = small[:, cuts[2]:cuts[3]].rearrange("p (d r n) -> p d r n", d=2, r=2)
    tmp = [small[:, 0:2304], small[:, 2304:4608]]
    ysf = core.sb("s5_y", [P, T5 * S5W])
    ys = ysf[:].rearrange("p (t n) -> p t n", t=T5)
    KKn = 2 * T5 - 1
    KK = ysf[0:2 * GC, 0:NP5 * KKn * GC].rearrange("p (j k q) -> p j k q", j=NP5, k=KKn)
    BD = core.sb("s5_BD", [P, 2, 2 * NP5, 2 * GC])
    ramp = core.sb("s5_ramp", [P, NC5])
    half_pi = core.sb("s5_half_pi", [P, 1])
    Dc = core.sb("s5_dcol", [2 * GC, NP5])
    dm = core.sb("s5_dmask", [2 * GC, GC])
    dd = core.sb("s5_diag", [2 * GC, NP5, GC])
    bg = core.sb("s5_bglu", [P, 4])
    free = E[:].rearrange("p j r n -> p (j r n)")
    yg = free[:, 0:4 * L].rearrange("p (k n) -> p k n", k=4)
    sg = free[:, 4 * L:6 * L].rearrange("p (k n) -> p k n", k=2)
    wg = free[:, 6 * L:8 * L].rearrange("p (k n) -> p k n", k=4)
    vps = core.ps("s5_v", [P, 2, 2, 2, NC5])
    tps = core.ps("s5_tps", [P, 4, 512])
    kps = core.ps("s5_kps", [P, 2, 512])
    yps = tps[:].rearrange("p (b h) (j n) -> p b h j n", b=2, j=4)
    names = ("ld vmm rot z scan back state ymm yout turned gelu glu gate out "
             "ramp bd0 bd E_made E_im E_turned E_out angles twiddle G0 G1 dve pool k_mm k_out kernel M dd").split()
    S = {n: core.sem("s5m_" + n) for n in names}
    cosv = tb["cos"].rearrange("p (d j) n -> p d j n", d=2)
    sinv = tb["sin"].rearrange("p (d j) n -> p d j n", d=2)

    def EB(ri):
        return ysf[:, 2048 * ri:2048 * ri + 2048].rearrange("p (j n) -> p j n", j=NP5)

    def table(x, j):
        return x[:, :, j:j + 1, :].broadcast_to([P, 2, 2, NC5])

    def power(d, ri, lo, n, reverse):
        dj = slice(NP5 * d, NP5 * d + NP5)
        x = k5["npi"][:, lo:lo + n, dj] if ri == 2 else k5["pw"][:, ri, lo:lo + n, dj]
        if reverse:
            x = x[:, ::-1, :]
        return x.rearrange("p k (j o) -> p j k o", o=1).broadcast_to([P, NP5, n, GC])

    def along(x, n):
        return x.rearrange("p j (o q) -> p j o q", o=1).broadcast_to([P, NP5, n, GC])

    def after(eng, step, dst, x, y, op, mark=None):
        step.done()
        ins = eng.tensor_tensor(dst, x, y, op)
        if mark is None:
            step(ins)
        else:
            ins.then_inc(S[mark], 1)

    def make_G(eng, step, d):
        dj = slice(NP5 * d, NP5 * d + NP5)
        pr, pi, npi = (power(d, ri, 0, 9, d == 1) for ri in range(3))
        cr, ci = along(k5["C"][:, 0, dj, :], 9), along(k5["C"][:, 1, dj, :], 9)
        gr, gn = G[:, 0, dj], G[:, 1, dj]
        t = tmp[d].rearrange("p (j k q) -> p j k q", j=NP5, k=9)
        after(eng, step, gr, cr, pr, ALU.mult)
        after(eng, step, t, ci, pi, ALU.mult)
        after(eng, step, gr, gr, t, ALU.subtract)
        after(eng, step, gn, cr, npi, ALU.mult)
        after(eng, step, t, ci, pr, ALU.mult)
        after(eng, step, gn, gn, t, ALU.subtract, f"G{d}")

    def E_factors(d):
        dj = slice(NP5 * d, NP5 * d + NP5)
        return (power(d, 0, 0, T5, d == 0), power(d, 1, 0, T5, d == 0),
                along(k5["B"][:, 0, dj, :], T5), along(k5["B"][:, 1, dj, :], T5))

    def E_term(x):
        return x.rearrange("p (j k q) -> p j k q", j=NP5, k=T5)

    def make_E_re(eng, step, d, t, mark=None):
        pr, pi, br, bi = E_factors(d)
        er, t = E_term(ysf[:, 0:2048]), E_term(t)
        after(eng, step, er, pr, br, ALU.mult)
        after(eng, step, t, pi, bi, ALU.mult)
        after(eng, step, er, er, t, ALU.subtract, mark)

    def make_E_im(eng, step, d, t, mark):
        pr, pi, br, bi = E_factors(d)
        ei, t = E_term(ysf[:, 2048:4096]), E_term(t)
        after(eng, step, ei, pr, bi, ALU.mult)
        after(eng, step, t, pi, br, ALU.mult)
        after(eng, step, ei, ei, t, ALU.add, mark)

    def load_M(eng, h):
        eng.wait_ge(S["kernel"], 1)
        with nc.allow_non_contiguous_dma(reason="rows of 512 bytes"):
            for t in range(T5):
                eng.dma_start(
                    M[t * GC:(t + 1) * GC].rearrange("p (j a) n -> p j a n", a=2)[:, :, h, :],
                    KK[h * GC:(h + 1) * GC, :, T5 - 1 - t:2 * T5 - 1 - t, :].rearrange("p j k q -> p j (k q)")
                ).then_inc(S["M"], 16)

    with nc.Block() as block:
        @block.sync
        def _(sp):
            with nc.allow_non_contiguous_dma(reason="small parameters"):
                sp.dma_start(Dc[:], a["s5_d"][0].rearrange("(j r) -> r j", r=2 * GC)).then_inc(S["dd"], 16)
                sp.dma_start(bg[:], a["s5_b_glu"][0].rearrange("(k p) -> p k", p=P)).then_inc(S["ld"], 16)
            load_M(sp, 0)
            sp.wait_ge(S["vmm"], NP5)
            sp.dma_start(wg[:], a["s5_w_glu"][0].rearrange("(k p) n -> p k n", p=P)).then_inc(S["ld"], 16)
            sp.wait_ge(S["ymm"], NP5)
            sp.dma_start(wo[:], a["w_out"][0].rearrange("(k p) n -> p k n", p=P)).then_inc(next_ld["w"], 16)
            sp.dma_start(x1[:], a["x"].rearrange("b (t p) d -> p (b t) d", p=P)).then_inc(next_ld["x"], 16)

        @block.tensor
        def _(pe):
            def inputs(j):
                if j >= 2:
                    pe.wait_ge(S["rot"], 2 * (j - 1))
                for d in range(2):
                    for ri in range(2):
                        for h in range(2):
                            u = uT[:, 2 * j + h, :]
                            rows = slice(NS * h, NS * h + NS)
                            mm = pe.matmul(vps[rows, j % 2, d, ri, :], E[:, NP5 * d + j, ri, rows],
                                           u if d == 0 else u[:, ::-1], start=True, stop=True)
                mm.then_inc(S["vmm"], 1)

            def outputs(j):
                if j % 4 == 0 and j >= 8:
                    pe.wait_ge(S["yout"], 2 * (j // 4 - 1))
                pe.wait_ge(S["state"], 4 * (j + 1))
                for h in range(2):
                    g = 2 * j + h
                    dst = yps[:, (j // 4) % 2, h, j % 4, :]
                    rows = slice(NS * h, NS * h + NS)
                    pe.matmul(dst, uT[:, g, :], M[:, g, :], start=True, stop=False)
                    for d in range(2):
                        for ri in range(2):
                            mm = pe.matmul(dst, st[rows, j % 2, d, ri, :],
                                           G[rows, ri, NP5 * d + j, 1 - d:1 - d + T5, :]
                                           .rearrange("p k q -> p (k q)"),
                                           start=False, stop=d == 1 and ri == 1)
                mm.then_inc(S["ymm"], 1)

            for n in range(16):
                pe.wait_ge(S["E_made"], n // 8 + 1)
                if n == 8:
                    pe.wait_ge(S["E_im"], 1)
                if n >= 4:
                    pe.wait_ge(S["E_out"], n - 3)
                for x in range(4):
                    j, ri = (2 * n + x // 2) % NP5, x % 2
                    mm = pe.transpose(tps[:, n % 4, x * P:(x + 1) * P], EB(ri)[:, j, :], c["ident"][:])
                mm.then_inc(S["E_turned"], 1)
            pe.wait_ge(S["bd"], 3)
            pe.wait_ge(S["G0"], 1)
            pe.wait_ge(S["G1"], 1)
            for n in range(8):
                d, q = 1 - n // 4, n % 4
                if n >= 2:
                    pe.wait_ge(S["k_out"], n - 1)
                for x in range(4):
                    dj = NP5 * d + 4 * q + x
                    for ri in range(2):
                        mm = pe.matmul(kps[0:2 * GC, n % 2, x * P:(x + 1) * P], BD[:, ri, dj, :],
                                       G[:, ri, dj, d:d + T5, :].rearrange("p k q -> p (k q)"),
                                       start=ri == 0, stop=ri == 1)
                mm.then_inc(S["k_mm"], 1)
            pe.wait_ge(S["E_out"], 16)
            inputs(0)
            inputs(1)
            for j in range(NP5):
                if j + 2 < NP5:
                    inputs(j + 2)
                if j == 0:
                    pe.wait_ge(S["M"], 16 * 2 * T5)
                outputs(j)
            pe.wait_ge(S["yout"], NP5 // 2)
            for k in range(4):
                for half in range(2):
                    n = 2 * k + half
                    if n >= 4:
                        pe.wait_ge(S["gelu"], n - 3)
                    for t in range(4):
                        mm = pe.transpose(tps[:, n % 4, t * P:(t + 1) * P],
                                          ys[:, 4 * half + t, k * P:(k + 1) * P], c["ident"][:])
                    mm.then_inc(S["turned"], 1)
            pe.wait_ge(S["gelu"], 8)
            pe.wait_ge(S["ld"], 32)
            for m in range(4):
                if m >= 2:
                    pe.wait_ge(S["gate"], m - 1)
                for half in range(2):
                    for k in range(4):
                        mm = pe.matmul(tps[:, 2 * (m % 2) + half, :], wg[:, k, m * P:(m + 1) * P],
                                       yg[:, k, half * 512:half * 512 + 512], start=k == 0, stop=k == 3)
                mm.then_inc(S["glu"], 1)

        @block.vector
        def _(dve):
            step = Steps(dve, S["dve"])
            step(dve.memset(half_pi[:], math.pi / 2))
            dve.wait_ge(cooked_ld, 16)
            make_E_re(dve, step, 0, tmp[0][:, 0:2048])
            make_E_im(dve, step, 0, tmp[0][:, 0:2048], "E_made")
            dve.wait_ge(S["E_made"], 1)
            dve.wait_ge(S["ramp"], 1)
            tau = k5["tau"].rearrange("p (j o) -> p j o", o=1).broadcast_to([P, 2 * NP5, NC5])
            rmp = ramp[:].rearrange("p (o n) -> p o n", o=1).broadcast_to([P, 2 * NP5, NC5])
            after(dve, step, tb["sin"], tau, rmp, ALU.mult)
            step.done()
            step(dve.tensor_scalar(tb["cos"], tb["sin"], MAGIC, MAGIC, ALU.add, ALU.subtract))
            after(dve, step, tb["sin"], tb["sin"], tb["cos"], ALU.subtract, "angles")
            dve.wait_ge(S["E_turned"], 8)
            make_E_re(dve, step, 1, tmp[0][:, 0:2048], "E_made")
            dve.wait_ge(S["E_made"], 2)
            dve.wait_ge(S["bd0"], 1)
            for h in range(2):
                rows = slice(NS * h, NS * h + NS)
                dve.tensor_copy(BD[rows, :, :, h * GC:(h + 1) * GC], k5["B"][rows]).then_inc(S["bd"], 1)
            dve.tensor_tensor(dm[:], c["ident"][0:2 * GC, 0:GC], c["ident"][0:2 * GC, GC:2 * GC], ALU.add
                              ).then_inc(S["bd"], 1)
            make_G(dve, step, 0)
            dve.wait_ge(S["bd"], 3)
            dve.wait_ge(S["dd"], 16)
            dve.tensor_tensor(dd[:], Dc[:].rearrange("p (j o) -> p j o", o=1).broadcast_to([2 * GC, NP5, GC]),
                              dm[:].rearrange("p (o q) -> p o q", o=1).broadcast_to([2 * GC, NP5, GC]), ALU.mult
                              ).then_inc(S["dd"], 1)
            dve.wait_ge(S["E_turned"], 16)
            for n in range(8):
                q = n % 4
                dve.wait_ge(S["k_mm"], n + 1)
                kp = kps[0:2 * GC, n % 2, :].rearrange("p (j k q) -> p j k q", j=4, k=T5)
                if n < 4:
                    dve.tensor_copy(KK[:, 4 * q:4 * q + 4, 0:T5, :], kp).then_inc(S["k_out"], 1)
                else:
                    step(dve.tensor_copy(KK[:, 4 * q:4 * q + 4, T5:KKn, :], kp[:, :, 1:T5, :]))
                    dve.wait_ge(S["k_out"], 4 + q)
                    mid = KK[:, 4 * q:4 * q + 4, T5 - 1, :]
                    dve.tensor_tensor(mid, mid, kp[:, :, 0, :], ALU.add).then_inc(S["k_out"], 1)
            dve.wait_ge(S["k_out"], 8)
            dve.wait_ge(S["dd"], 17)
            step.done()
            mid = KK[:, :, T5 - 1, :]
            dve.tensor_tensor(mid, mid, dd[:], ALU.add).then_inc(S["kernel"], 1)
            dve.wait_ge(S["twiddle"], 3)
            for slot in range(2):
                for ri in range(2):
                    dve.memset(st[:, slot, 0, ri, 0:1], 0.0).then_inc(S["out"], 1)
                    dve.memset(st[:, slot, 1, ri, NC5 - 1:NC5], 0.0).then_inc(S["out"], 1)
            for j in range(NP5):
                b = j % 2
                dve.wait_ge(S["vmm"], j + 1)
                if j:
                    dve.wait_ge(S["z"], 2 * j)
                dve.tensor_tensor(rot[:, 0], vps[:, b], table(cosv, j), ALU.mult).then_inc(S["rot"], 1)
                dve.tensor_tensor(rot[:, 1], vps[:, b], table(sinv, j), ALU.mult).then_inc(S["rot"], 1)
                dve.wait_ge(S["rot"], 2 * (j + 1))
                if j >= 2:
                    dve.wait_ge(S["scan"], 4 * (j - 1))
                dve.tensor_tensor(z[:, b, :, 0], rot[:, 0, :, 0], rot[:, 1, :, 1], ALU.add).then_inc(S["z"], 1)
                dve.tensor_tensor(z[:, b, :, 1], rot[:, 0, :, 1], rot[:, 1, :, 0], ALU.subtract
                                  ).then_inc(S["z"], 1)
                dve.wait_ge(S["z"], 2 * (j + 1))
                if j:
                    dve.wait_ge(S["back"], 2 * j)
                for d in range(2):
                    rho = k5["rho"][:, NP5 * d + j:NP5 * d + j + 1].broadcast_to([P, NC5])
                    for ri in range(2):
                        dve.tensor_tensor_scan(zs[:, d, ri], rho, z[:, b, d, ri], 0.0, ALU.mult, ALU.add
                                               ).then_inc(S["scan"], 1)
            for m in range(4):
                dve.wait_ge(S["gate"], m + 1)
                dve.tensor_tensor(yT[:, m, :], yg[:, m, :], sg[:, m % 2, :], ALU.mult).then_inc(S["out"], 1)

        @block.gpsimd
        def _(pool):
            step = Steps(pool, S["pool"])
            pool.iota(ramp[:], [[1, NC5]], base=0, channel_multiplier=0,
                      allow_small_or_imprecise_dtypes=True).then_inc(S["ramp"], 1)
            pool.memset(BD[:], 0.0).then_inc(S["bd0"], 1)
            pool.wait_ge(cooked_ld, 16)
            make_G(pool, step, 1)
            pool.wait_ge(S["G1"], 1)
            pool.wait_ge(S["E_turned"], 8)
            make_E_im(pool, step, 1, tmp[1][:, 0:2048], "E_im")
            n = NC5 - 1
            for j in range(NP5):
                b = j % 2
                pool.wait_ge(S["scan"], 4 * (j + 1))
                if j:
                    pool.wait_ge(S["state"], 4 * j)
                pool.tensor_tensor(back[:, 0], zs[:], table(cosv, j), ALU.mult).then_inc(S["back"], 1)
                pool.tensor_tensor(back[:, 1], zs[:], table(sinv, j), ALU.mult).then_inc(S["back"], 1)
                pool.wait_ge(S["back"], 2 * (j + 1))
                if j == 0:
                    pool.wait_ge(S["out"], 8)
                elif j >= 2:
                    pool.wait_ge(S["ymm"], j - 1)
                pool.tensor_tensor(st[:, b, 0, 0, 1:], back[:, 0, 0, 0, 0:n], back[:, 1, 0, 1, 0:n],
                                   ALU.subtract).then_inc(S["state"], 1)
                pool.tensor_tensor(st[:, b, 0, 1, 1:], back[:, 0, 0, 1, 0:n], back[:, 1, 0, 0, 0:n],
                                   ALU.add).then_inc(S["state"], 1)
                pool.tensor_tensor(st[:, b, 1, 0, 0:n][:, ::-1], back[:, 0, 1, 0, 0:n], back[:, 1, 1, 1, 0:n],
                                   ALU.subtract).then_inc(S["state"], 1)
                pool.tensor_tensor(st[:, b, 1, 1, 0:n][:, ::-1], back[:, 0, 1, 1, 0:n], back[:, 1, 1, 0, 0:n],
                                   ALU.add).then_inc(S["state"], 1)

        @block.scalar
        def _(act):
            def evacuate_E(d):
                for n in range(8 * d, 8 * d + 8):
                    act.wait_ge(S["E_turned"], n + 1)
                    act.activation(E[:, 2 * n:2 * n + 2].rearrange("p j r n -> p (j r n)"), tps[:, n % 4, :], ACT.Copy
                                   ).then_inc(S["E_out"], 1)

            evacuate_E(0)
            act.wait_ge(S["angles"], 1)
            act.wait_ge(S["dve"], 1)
            act.activation(tb["cos"], tb["sin"], ACT.Abs).then_inc(S["twiddle"], 1)
            act.wait_ge(S["twiddle"], 1)
            act.activation(tb["sin"], tb["sin"], ACT.Sin, scale=6.283185).then_inc(S["twiddle"], 1)
            act.activation(tb["cos"], tb["cos"], ACT.Sin, scale=-6.283185, bias=half_pi[:, 0:1]
                           ).then_inc(S["twiddle"], 1)
            evacuate_E(1)
            load_M(act, 1)
            yv = ys[:].rearrange("p t (j h q) -> p h j t q", j=NP5, h=2)
            for n in range(NP5 // 4):
                act.wait_ge(S["ymm"], 4 * (n + 1))
                for h in range(2):
                    act.activation(yv[:, h, 4 * n:4 * n + 4], yps[:, n % 2, h].rearrange("p j (t q) -> p j t q", t=T5),
                                   ACT.Copy).then_inc(S["yout"], 1)
            for k in range(4):
                for half in range(2):
                    n = 2 * k + half
                    act.wait_ge(S["turned"], n + 1)
                    act.activation(yg[:, k, :].rearrange("p (n t) -> p t n", t=T5)[:, 4 * half:4 * half + 4, :],
                                   tps[:, n % 4].rearrange("p (t n) -> p t n", t=4), ACT.Gelu
                                   ).then_inc(S["gelu"], 1)
            act.wait_ge(S["ld"], 32)
            for m in range(4):
                act.wait_ge(S["glu"], m + 1)
                if m >= 2:
                    act.wait_ge(S["out"], 8 + m - 1)
                act.activation(sg[:, m % 2, :], tps[:, 2 * (m % 2):2 * (m % 2) + 2, :].rearrange("p a n -> p (a n)"),
                               ACT.Sigmoid, bias=bg[:, m:m + 1]).then_inc(S["gate"], 1)


def gated_norm(nc, core, c, a, o_sum, zs, ydn, s5_dram, cooked, cooked_ld):
    sq = core.sb("gn_sq", [P, 2, DW])
    ss = core.sb("gn_ss", [P, TT, H])
    rt = core.sb("gn_rt", [P, TT, H])
    rs = core.sb("gn_rs", [P, TT, H])
    nw = core.sb("gn_w", [P, 1])
    ps = core.ps("gn_ps", [P, 2, 512])
    ld, sqd, red, rtd, rsd, nrm, turned, out, gated = (core.sem("gn_" + n) for n in
                                                       "ld sq red rt rs nrm turned out gated".split())

    def heads(x):
        return x.rearrange("p (h n) -> p h n", h=H)

    with nc.Block() as block:
        @block.sync
        def _(sp):
            sp.dma_start(cooked[:], s5_dram).then_inc(cooked_ld, 16)
            with nc.allow_non_contiguous_dma(reason="small parameters"):
                sp.dma_start(nw[:], a["gdn_norm_w"].rearrange("o n -> n o")).then_inc(ld, 16)

        @block.scalar
        def _(act):
            for t in range(TT):
                if t >= 2:
                    act.wait_ge(red, t - 1)
                act.activation(sq[:, t % 2, :], o_sum[:, t, :], ACT.Square).then_inc(sqd, 1)
            act.wait_ge(rsd, 1)
            act.activation(rt[:], ss[:], ACT.Sqrt).then_inc(rtd, 1)
            act.wait_ge(ld, 16)
            for t in range(TT):
                act.wait_ge(turned, t + 1)
                act.activation(ydn[:, :, t * P:(t + 1) * P], ps[:, t % 2, :].rearrange("p (h n) -> p h n", h=H),
                               ACT.Copy, scale=nw[:, 0:1]).then_inc(out, 1)

        @block.vector
        def _(dve):
            for t in range(TT):
                dve.wait_ge(sqd, t + 1)
                dve.tensor_reduce(ss[:, t, :], heads(sq[:, t % 2, :]), AX.X, ALU.add).then_inc(red, 1)
            dve.wait_ge(red, TT)
            dve.tensor_scalar(ss[:], ss[:], 1.0 / DH, EPS, ALU.mult, ALU.add).then_inc(rsd, 1)
            dve.wait_ge(rtd, 1)
            dve.reciprocal(rs[:], rt[:]).then_inc(rsd, 1)
            dve.wait_ge(rsd, 2)
            for t in range(TT):
                scale = rs[:, t, :].rearrange("p (h o) -> p h o", o=1).broadcast_to([P, H, DH])
                dve.wait_ge(gated, t + 1)
                dve.tensor_tensor(heads(zs[:, t, :]), heads(zs[:, t, :]), scale, ALU.mult).then_inc(nrm, 1)

        @block.gpsimd
        def _(pool):
            for t in range(TT):
                pool.tensor_tensor(zs[:, t, :], o_sum[:, t, :], zs[:, t, :], ALU.mult).then_inc(gated, 1)

        @block.tensor
        def _(pe):
            for t in range(TT):
                pe.wait_ge(nrm, t + 1)
                if t >= 2:
                    pe.wait_ge(out, t - 1)
                for h in range(H):
                    mm = pe.transpose(ps[:, t % 2, h * P:(h + 1) * P], zs[:, t, h * DH:(h + 1) * DH],
                                      c["ident"][:])
                mm.then_inc(turned, 1)


def out_projection(nc, core, c, a, ys5, ydn, x1, wo, sq, next_ld, logits, h_dram, filled):
    NR = NGRP + NEXP
    nf = core.sb("norm_ffn_row", [P, D])
    wo_hi = core.sb("w_out_hi", [P, KT, D], F32R)
    wo_lo = core.sb("w_out_lo", [P, KT, D], F32R)
    y_hi = core.sb("y_hi", [P, 2, KT, P], F32R)
    y_lo = core.sb("y_lo", [P, 2, KT, P], F32R)
    h2 = core.sb("h_row", [P, 2, D])
    hT = core.sb("h_turned", [P, 2, KT, P])
    ss = core.sb("op_ss", [P, TT])
    ms = core.sb("op_ms", [P, TT])
    rt = core.sb("op_rt", [P, TT])
    rs = core.sb("op_rs", [P, TT])
    wr = core.sb("w_router", [P, KT, NR])
    br = core.sb("b_router", [P, NR])
    mm_ps = core.ps("op_ps", [P, 2, 2, 512])
    tr_ps = core.ps("op_turn", [P, 2, 512])
    lg_ps = core.ps("op_logits", [P, 2, 512])
    names = "w_hi y_hi w_lo y_lo par mm x1 sq ms rt rs h turned hT lg store0 store1".split()
    S = {n: core.sem("op_" + n) for n in names}
    store = [S["store0"], S["store1"]]

    def piece(x, k, half):
        return x[:, k, half * 512:half * 512 + 512]

    def y_piece(t, half):
        return (ys5, ydn)[half][:, :, t * P:(t + 1) * P]

    def y_part(x, t, half):
        return x[:, t % 2, 4 * half:4 * half + 4, :]

    with nc.Block() as block:
        @block.sync
        def _(sp):
            sp.dma_start(nf[:], a["norm_ffn"].partition_broadcast(P)).then_inc(S["par"], 16)
            with nc.allow_non_contiguous_dma(reason="small parameters"):
                sp.dma_start(wr[:, :, 0:NGRP], a["router_w_group"][0].rearrange("(k p) n -> p k n", p=P)
                             ).then_inc(S["par"], 16)
                for g in range(NGRP):
                    sp.dma_start(wr[:, :, NGRP + EPG * g:NGRP + EPG * (g + 1)],
                                 a["router_w_expert"][0, g].rearrange("(k p) n -> p k n", p=P)
                                 ).then_inc(S["par"], 16)
                sp.dma_start(br[:, 0:NGRP], a["router_b_group"].partition_broadcast(P)).then_inc(S["par"], 16)
                sp.dma_start(br[:, NGRP:], a["router_b_expert"].rearrange("o g e -> o (g e)")
                             .partition_broadcast(P)).then_inc(S["par"], 16)
            for t in range(TT):
                sp.wait_ge(S["h"], t + 1)
                sp.dma_start(h_dram[t * P:(t + 1) * P, :], h2[:, t % 2, :]).then_inc(store[t % 2], 16)
            sp.wait_ge(filled, 16 * (MAXB + 1 - L * 2 // P))
            for s in range(2):
                sp.wait_ge(store[s], 16 * TT // 2)

        @block.tensor
        def _(pe):
            def project(t):
                if t >= 2:
                    pe.wait_ge(S["x1"], t - 1)
                for half in range(2):
                    for k in range(KT):
                        if half == 0 and k % 4 == 0:
                            pe.wait_ge(S["y_lo"], 2 * t + k // 4 + 1)
                        if t == 0:
                            pe.wait_ge(S["w_lo"], KT * half + k + 1)
                        hi, lo = y_hi[:, t % 2, k, :], y_lo[:, t % 2, k, :]
                        w_hi, w_lo = piece(wo_hi, k, half), piece(wo_lo, k, half)
                        dst = mm_ps[:, t % 2, half, :]
                        pe.matmul(dst, hi, w_hi, start=k == 0, stop=False)
                        pe.matmul(dst, hi, w_lo, start=False, stop=False)
                        mm = pe.matmul(dst, lo, w_hi, start=False, stop=k == KT - 1)
                mm.then_inc(S["mm"], 1)

            def route(t):
                pe.wait_ge(S["h"], t + 1)
                for half in range(2):
                    n = 2 * t + half
                    if n >= 2:
                        pe.wait_ge(S["hT"], n - 1)
                    for k in range(4):
                        mm = pe.transpose(tr_ps[:, half, k * P:(k + 1) * P],
                                          h2[:, t % 2, (4 * half + k) * P:(4 * half + k + 1) * P], c["ident"][:])
                    mm.then_inc(S["turned"], 1)

            def logit(t):
                pe.wait_ge(S["par"], 16 * 8)
                pe.wait_ge(S["hT"], 2 * t + 2)
                for k in range(KT):
                    mm = pe.matmul(lg_ps[:, 0, t * NR:(t + 1) * NR], hT[:, t % 2, k, :], wr[:, k, :],
                                   start=k == 0, stop=k == KT - 1)
                mm.then_inc(S["lg"], 1)

            for t in range(TT + 2):
                if t < TT:
                    project(t)
                if 1 <= t <= TT:
                    route(t - 1)
                if t >= 2:
                    logit(t - 2)

        @block.vector
        def _(dve):
            for half in range(2):
                for k in range(KT):
                    dve.wait_ge(S["w_hi"], KT * half + k + 1)
                    dve.tensor_tensor(piece(wo_lo, k, half), piece(wo, k, half),
                                      piece(wo_hi, k, half).bitcast(F32), ALU.subtract).then_inc(S["w_lo"], 1)
            dve.wait_ge(next_ld["x"], 16)
            for t in range(TT):
                dve.wait_ge(S["mm"], t + 1)
                dve.tensor_tensor(x1[:, t, :], x1[:, t, :], mm_ps[:, t % 2].rearrange("p a n -> p (a n)"), ALU.add
                                  ).then_inc(S["x1"], 1)
                dve.wait_ge(S["sq"], t + 1)
                dve.tensor_scalar(ms[:, t:t + 1], ss[:, t:t + 1], 1.0 / D, EPS, ALU.mult, ALU.add
                                  ).then_inc(S["ms"], 1)
                dve.wait_ge(S["rt"], t + 1)
                dve.reciprocal(rs[:, t:t + 1], rt[:, t:t + 1]).then_inc(S["rs"], 1)
                dve.wait_ge(S["rs"], t + 1)
                dve.wait_ge(S["par"], 16 * 8)
                if t >= 2:
                    dve.wait_ge(store[t % 2], 16 * (t // 2))
                    dve.wait_ge(S["turned"], 2 * (t - 1))
                dve.scalar_tensor_tensor(out=h2[:, t % 2, :], in0=x1[:, t, :], scalar=rs[:, t:t + 1], in1=nf[:],
                                         op0=ALU.mult, op1=ALU.mult).then_inc(S["h"], 1)
            dve.wait_ge(S["lg"], TT)
            dve.tensor_tensor(logits[:], lg_ps[:, 0, 0:TT * NR].rearrange("p (t n) -> p t n", n=NR),
                              br[:].rearrange("p (o n) -> p o n", o=1).broadcast_to([P, TT, NR]), ALU.add
                              ).then_inc(S["x1"], 1)

        @block.gpsimd
        def _(pool):
            for t in range(TT):
                for half in range(2):
                    pool.wait_ge(S["y_hi"], 2 * t + half + 1)
                    if t >= 2:
                        pool.wait_ge(S["mm"], t - 1)
                    pool.tensor_tensor(y_part(y_lo, t, half), y_piece(t, half),
                                       y_part(y_hi, t, half).bitcast(F32), ALU.subtract).then_inc(S["y_lo"], 1)

        @block.scalar
        def _(act):
            def turned(t):
                for half in range(2):
                    n = 2 * t + half
                    act.wait_ge(S["turned"], n + 1)
                    if t >= 2:
                        act.wait_ge(S["lg"], t - 1)
                    act.activation(hT[:, t % 2, 4 * half:4 * half + 4, :],
                                   tr_ps[:, half, :].rearrange("p (k n) -> p k n", k=4), ACT.Copy
                                   ).then_inc(S["hT"], 1)

            def split_w(half, k):
                act.activation(piece(wo_hi, k, half), piece(wo, k, half), ACT.Copy).then_inc(S["w_hi"], 1)

            def split_y(t, half):
                if t >= 2:
                    act.wait_ge(S["mm"], t - 1)
                act.activation(y_part(y_hi, t, half), y_piece(t, half), ACT.Copy).then_inc(S["y_hi"], 1)

            act.wait_ge(next_ld["w"], 16)
            for k in range(4):
                split_w(0, k)
            split_y(0, 0)
            for k in range(4, KT):
                split_w(0, k)
            split_y(0, 1)
            for k in range(KT):
                split_w(1, k)
            for half in range(2):
                split_y(1, half)
            for t in range(TT):
                act.wait_ge(S["x1"], t + 1)
                if t:
                    act.wait_ge(S["sq"], t)
                act.activation(sq[:], x1[:, t, :], ACT.Square, accum_out=ss[:, t:t + 1]).then_inc(S["sq"], 1)
                act.wait_ge(S["ms"], t + 1)
                act.activation(rt[:, t:t + 1], ms[:, t:t + 1], ACT.Sqrt).then_inc(S["rt"], 1)
                if t + 2 < TT:
                    for half in range(2):
                        split_y(t + 2, half)
                if t >= 1:
                    turned(t - 1)
            turned(TT - 1)


def router_tables(core):
    return {
        "slot_tok": core.sb("slot_token", [P, MAXB + 3], I32),
        "block": core.sb("block_expert", [P, MAXB + 2], I32),
        "count": core.sb("block_count", [P, 1], I32),
        "dest": core.sb("dest_slot", [P, 2, TT], I32),
        "gate": core.sb("gate", [P, 2, TT]),
    }


def router(nc, core, c, a, logits, rt, wg, wu, early):
    NB = MAXB + 2
    strict = core.sb("r_strict", [P, P])
    iota = core.sb("r_iota", [P, P])
    tokid = core.sb("r_tokid", [P, TT])
    ge = core.sb("r_group", [P, TT, NGRP])
    one_g = core.sb("r_one_group", [P, TT, NGRP])
    em = core.sb("r_masked", [P, TT, NEXP])
    t32 = core.sb("r_t32", [P, TT, NEXP])
    one = core.sb("r_one", [P, 2, TT, NEXP])
    both = core.sb("r_both", [P, TT, NEXP])
    pos = core.sb("r_pos", [P, TT, NEXP])
    off = core.sb("r_off", [P, TT + 1, NEXP])
    blocks = core.sb("r_blocks", [P, 3, NEXP])
    cmp8 = core.sb("r_cmp8", [P, NEXP, TT])
    cmpb = core.sb("r_cmpb", [P, NB, NEXP])
    col = core.sb("r_cols", [P, 8, TT])
    dest = core.sb("r_dest", [P, 2, TT])
    blk = core.sb("r_blk", [P, 2, TT])
    slot = core.sb("r_slot", [P, 2, TT])
    hit_s = core.sb("r_hit_slot", [P, 2 * TT, P])
    hit_b = core.sb("r_hit_block", [P, 2 * TT, NB])
    ebf = core.sb("r_ebf", [P, NB])
    ps = core.ps("r_ps", [P, 3, 512])
    pg, v, s, m, hit = (core.sem("r_" + n) for n in "pool dve act pe hit".split())
    s_ready = [core.sem("r_ready_" + n) for n in ("groups", "gap", "experts")]
    GMAX, GSUM, M1, M2, W, TMP = range(6)

    def last(x, n):
        return x.rearrange("p (t o) -> p t o", o=1).broadcast_to([P, x.shape[1], n])

    def tiles(x, n=TT):
        return x.rearrange("p (o e) -> p o e", o=1).broadcast_to([P, n, x.shape[1]])

    with nc.Block() as block:
        @block.sync
        def _(sp):
            for w, name in ((wg, "expert_w_gate"), (wu, "expert_w_up")):
                sp.dma_start(w[:, 0], a[name][0, 0].rearrange("(p k) n -> p k n", k=KT)).then_inc(early, 16)

        @block.gpsimd
        def _(pool):
            step = Steps(pool, pg)
            step(pool.iota(iota[:], [[1, P]], base=0, channel_multiplier=0, allow_small_or_imprecise_dtypes=True))
            step(pool.iota(tokid[:], [[P, TT]], base=0, channel_multiplier=1, allow_small_or_imprecise_dtypes=True))
            step(pool.affine_select(out=strict[:], in_=c["ones"][:], compare_op=ALU.is_gt, fill=0.0, base=0,
                                    pattern=[[1, P]], channel_multiplier=-1))
            step(pool.memset(rt["slot_tok"][:], 0))

        @block.scalar
        def _(act):
            act.wait_ge(s_ready[0], 1)
            act.activation(ge[:], ge[:], ACT.Exp).then_inc(s, 1)
            act.wait_ge(s_ready[1], 1)
            act.activation(col[:, TMP], col[:, TMP], ACT.Exp).then_inc(s, 1)

        @block.tensor
        def _(pe):
            pe.wait_ge(s_ready[2], 1)
            pe.wait_ge(pg, 3)
            flat = both[:].rearrange("p t e -> p (t e)")
            pe.matmul(ps[:, 0, 0:TT * NEXP], strict[:], flat, start=True, stop=True)
            pe.matmul(ps[:, 1, 0:TT * NEXP], c["ones"][:], flat, start=True, stop=True).then_inc(m, 1)
            for n in range(2 * TT):
                pe.wait_ge(hit, 2 * (n + 1))
                mm = pe.matmul(ps[:, 2, 0:NB], hit_s[:, n, :], hit_b[:, n, :], start=n == 0, stop=n == 2 * TT - 1)
            mm.then_inc(m, 1)

        @block.vector
        def _(dve):
            step = Steps(dve, v)
            TTo = dve.tensor_tensor

            def seq(ins_of, mark=None):
                step.done()
                ins = ins_of()
                if mark is None:
                    step(ins)
                else:
                    ins.then_inc(mark, 1)
                    dve.wait_ge(mark, 1)

            dve.wait_ge(pg, 4)
            lg, le = logits[:, :, 0:NGRP], logits[:, :, NGRP:]
            step(dve.tensor_reduce(col[:, GMAX], lg, AX.X, ALU.max))
            seq(lambda: TTo(ge[:], lg, last(col[:, GMAX], NGRP), ALU.subtract))

            def first_max(dst, x, n, mx, tmp):
                seq(lambda: TTo(tmp, x, last(mx, n), ALU.is_equal))
                seq(lambda: dve.tensor_scalar(tmp, tmp, -BIG, BIG, ALU.mult, ALU.add))
                seq(lambda: TTo(tmp, tmp, tiles(iota[:, 0:n]), ALU.add))
                seq(lambda: dve.tensor_reduce(col[:, W], tmp, AX.X, ALU.min))
                seq(lambda: TTo(dst, last(col[:, W], n), tiles(iota[:, 0:n]), ALU.is_equal))

            first_max(one_g[:], lg, NGRP, col[:, GMAX], t32[:, :, 0:NGRP])
            step.done()
            dve.tensor_copy(t32[:, :, 0:NGRP], one_g[:]).then_inc(s_ready[0], 1)
            dve.wait_ge(s_ready[0], 1)
            g4 = one_g[:].rearrange("p t (g o) -> p t g o", o=1).broadcast_to([P, TT, NGRP, EPG])
            e4 = em[:].rearrange("p t (g e) -> p t g e", g=NGRP)
            t4 = t32[:].rearrange("p t (g e) -> p t g e", g=NGRP)
            l4 = le.rearrange("p t (g e) -> p t g e", g=NGRP)
            seq(lambda: TTo(e4, l4, g4, ALU.mult))
            seq(lambda: dve.tensor_copy(t4, g4))
            seq(lambda: dve.tensor_scalar(t32[:], t32[:], BIG, -BIG, ALU.mult, ALU.add))
            seq(lambda: TTo(em[:], em[:], t32[:], ALU.add))
            seq(lambda: dve.tensor_reduce(col[:, M1], em[:], AX.X, ALU.max))
            first_max(one[:, 0], em[:], NEXP, col[:, M1], t32[:])
            seq(lambda: dve.tensor_scalar(t32[:], one[:, 0], -3.0 * BIG, None, ALU.mult))
            seq(lambda: TTo(em[:], em[:], t32[:], ALU.add))
            seq(lambda: dve.tensor_reduce(col[:, M2], em[:], AX.X, ALU.max))
            first_max(one[:, 1], em[:], NEXP, col[:, M2], t32[:])
            seq(lambda: TTo(both[:], one[:, 0], one[:, 1], ALU.add), s_ready[2])
            seq(lambda: TTo(col[:, TMP], col[:, M2], col[:, M1], ALU.subtract), s_ready[1])
            dve.wait_ge(s, 2)
            seq(lambda: dve.tensor_reduce(col[:, GSUM], ge[:], AX.X, ALU.add))
            seq(lambda: dve.tensor_scalar(col[:, W], col[:, TMP], 1.0, None, ALU.add))
            seq(lambda: TTo(col[:, W], col[:, W], col[:, GSUM], ALU.mult))
            seq(lambda: dve.reciprocal(rt["gate"][:, 0], col[:, W]))
            seq(lambda: TTo(rt["gate"][:, 1], rt["gate"][:, 0], col[:, TMP], ALU.mult))
            dve.wait_ge(m, 1)
            tot = ps[:, 1, 0:TT * NEXP].rearrange("p (t e) -> p t e", t=TT)
            seq(lambda: dve.memset(off[:, 0, :], 0.0))
            for t in range(TT):
                seq(lambda: TTo(off[:, t + 1, :], off[:, t, :], tot[:, t, :], ALU.add))
            cnt = off[:, TT, :]
            seq(lambda: dve.tensor_scalar(ebf[:, 0:TT], iota[:, 0:TT], float(P), None, ALU.mult))
            seq(lambda: TTo(cmp8[:], last(cnt, TT), tiles(ebf[:, 0:TT], NEXP), ALU.is_gt))
            seq(lambda: dve.tensor_reduce(blocks[:, 0], cmp8[:], AX.X, ALU.add))
            seq(lambda: dve.tensor_tensor_scan(blocks[:, 1], c["ones"][:, 0:NEXP], blocks[:, 0], 0.0,
                                               ALU.mult, ALU.add))
            seq(lambda: TTo(blocks[:, 2], blocks[:, 1], blocks[:, 0], ALU.subtract))
            seq(lambda: dve.tensor_scalar(blocks[:, 2], blocks[:, 2], float(P), None, ALU.mult))
            seq(lambda: TTo(pos[:], off[:, 0:TT, :], ps[:, 0, 0:TT * NEXP].rearrange("p (t e) -> p t e", t=TT),
                            ALU.add))
            seq(lambda: TTo(pos[:], pos[:], tiles(blocks[:, 2]), ALU.add))
            for k in range(2):
                seq(lambda: TTo(t32[:], pos[:], one[:, k], ALU.mult))
                seq(lambda: dve.tensor_reduce(dest[:, k], t32[:], AX.X, ALU.add))
            seq(lambda: dve.tensor_copy(rt["dest"][:], dest[:]))
            seq(lambda: dve.tensor_scalar(blk[:], dest[:], 1.0 / P, -(P - 1) / (2.0 * P), ALU.mult, ALU.add))
            seq(lambda: dve.tensor_scalar(blk[:], blk[:], MAGIC, MAGIC, ALU.add, ALU.subtract))
            seq(lambda: dve.scalar_tensor_tensor(out=slot[:], in0=blk[:], scalar=-float(P), in1=dest[:],
                                                 op0=ALU.mult, op1=ALU.add))
            step.done()
            for n in range(2 * TT):
                k, t = n // TT, n % TT
                dve.tensor_scalar(hit_s[:, n, :], iota[:], slot[:, k, t:t + 1], tokid[:, t:t + 1],
                                  ALU.is_equal, ALU.mult).then_inc(hit, 1)
                dve.tensor_scalar(hit_b[:, n, :], iota[:, 0:NB], blk[:, k, t:t + 1], None,
                                  ALU.is_equal).then_inc(hit, 1)
            step(TTo(cmpb[:], tiles(blocks[:, 1], NB), last(iota[:, 0:NB], NEXP), ALU.is_le))
            seq(lambda: dve.tensor_reduce(ebf[:], cmpb[:], AX.X, ALU.add))
            seq(lambda: dve.tensor_scalar(ebf[:], ebf[:], float(NEXP - 1), None, ALU.min))
            seq(lambda: dve.tensor_copy(rt["block"][:], ebf[:]))
            seq(lambda: dve.tensor_copy(rt["count"][:], blocks[:, 1, NEXP - 1:NEXP]))
            dve.wait_ge(m, 2)
            seq(lambda: dve.tensor_copy(rt["slot_tok"][:, 0:NB], ps[:, 2, 0:NB]))


def experts(nc, core, c, a, rt, h_dram, y_dram, wg, wu, early):
    KD = DE // P
    wd = core.sb("w_down", [P, 2, KD, D])
    idx = core.sb("gather_idx", [P, 2], I32)
    xg = core.sb("gathered", [P, 2, D])
    xT = core.sb("gathered_T", [P, 2, KT, P])
    sg = core.sb("silu_gate", [P, DE])
    hid = core.sb("hidden", [P, DE])
    wd_hi, wd_lo = core.sb("w_down_hi", [P, KD, D], F32R), core.sb("w_down_lo", [P, KD, D], F32R)
    hT_hi, hT_lo = core.sb("hidden_T_hi", [P, KD, P], F32R), core.sb("hidden_T_lo", [P, KD, P], F32R)
    y = core.sb("expert_out", [P, 2, D])
    g_ps = core.ps("gate_mm", [P, 512])
    u_ps = core.ps("up_mm", [P, 512])
    x_ps = core.ps("x_turned", [P, 2, 512])
    h_ps = core.ps("h_turned_ps", [P, 512])
    y_ps = core.ps("down_mm", [P, 2, 512])
    names = "gate_mm up_mm x_turned xT silu hid h_turned hT down_mm y_out idx turn w_hi w_lo".split()
    S = {n: core.sem("ex_" + n) for n in names}
    ld = {n: [core.sem(f"ex_ld_{n}{s}") for s in range(2)] for n in "gud"}
    gathered = [core.sem(f"ex_gathered{s}") for s in range(2)]
    stored = [core.sem(f"ex_stored{s}") for s in range(2)]
    w_gate = a["expert_w_gate"].rearrange("o e (p k) n -> p (o e) k n", k=KT)
    w_up = a["expert_w_up"].rearrange("o e (p k) n -> p (o e) k n", k=KT)
    w_down = a["expert_w_down"].rearrange("o e (p k) n -> p (o e) k n", k=KD)
    y_blocks = y_dram.rearrange("(b p) d -> b p d", p=P)
    PAIRS = (MAXB + 1) // 2

    @contextmanager
    def pairs(eng, count):
        with eng.Fori(0, PAIRS // 6) as q:
            with eng.If(q * 12 < count):
                with eng.Fori(0, 6) as r:
                    yield q * 6 + r

    def odd_and_even(i):
        return ((i * 2 + 1, 1), (i * 2 + 2, 0))

    with nc.Block() as block:
        @block.sync
        def _(sp):
            count = sp.value_load(rt["count"][0:1, 0:1], min_val=16, max_val=MAXB)

            def expert(b):
                return sp.value_load(rt["block"][0:1, bass.ds(b, 1)], min_val=0, max_val=NEXP - 1)

            def load_gate_up(b, s):
                e = expert(b)
                sp.wait_ge(S["up_mm"], b + 1)
                sp.dma_start(wg[:, s], w_gate[:, bass.ds(e, 1)].rearrange("p o k n -> p (o k) n")
                             ).then_inc(ld["g"][s], 16)
                sp.dma_start(wu[:, s], w_up[:, bass.ds(e, 1)].rearrange("p o k n -> p (o k) n")
                             ).then_inc(ld["u"][s], 16)

            def load_down(b, s):
                e = expert(b)
                sp.wait_ge(S["down_mm"], b + 1)
                sp.dma_start(wd[:, s], w_down[:, bass.ds(e, 1)].rearrange("p o k n -> p (o k) n")
                             ).then_inc(ld["d"][s], 16)

            sp.wait_ge(early, 32)
            first = expert(0)
            with sp.If(first < 1):
                sp.sem_inc(ld["g"][0], 16)
                sp.sem_inc(ld["u"][0], 16)
            with sp.If(first > 0):
                load_gate_up(0, 0)
            with pairs(sp, count) as i:
                for b, s in odd_and_even(i):
                    with sp.If(b < count):
                        load_gate_up(b, s)
                    with sp.If(b < count + 1):
                        load_down(b - 1, 1 - s)

        @block.gpsimd
        def _(pool):
            count = pool.value_load(rt["count"][0:1, 0:1], min_val=16, max_val=MAXB)

            def gather(s, b, wait_idx):
                pool.tensor_copy(idx[:, s:s + 1], rt["slot_tok"][:, bass.ds(b, 1)]).then_inc(S["idx"], 1)
                pool.wait_ge(S["idx"], wait_idx)
                pool.sem_inc(S["turn"], 1)
                pool.indirect_dma_start(out=xg[:, s, :], out_offset=None, in_=h_dram,
                                        in_offset=bass.IndirectOffsetOnAxis(ap=idx[:, s:s + 1], axis=0)
                                        ).then_inc(gathered[s], 16)

            gather(0, 0, 1)
            with pairs(pool, count) as i:
                for s in range(2):
                    b = i * 2 + s
                    with pool.If(b < count):
                        pool.wait_ge(S["x_turned"], b + 1)
                        gather(1 - s, b + 1, b + 2)
            pool.wait_ge(gathered[0], 16 * (count // 2 + 1))
            pool.wait_ge(gathered[1], 16 * ((count + 1) // 2))
            pool.sem_inc(S["turn"], 1)

        @block.tensor
        def _(pe):
            count = pe.value_load(rt["count"][0:1, 0:1], min_val=16, max_val=MAXB)
            pe.sem_inc(S["up_mm"], 2)
            pe.sem_inc(S["down_mm"], 2)

            def turn_rows(s):
                for k in range(KT):
                    mm = pe.transpose(x_ps[:, k // 4, (k % 4) * P:(k % 4 + 1) * P], xg[:, s, k:D:KT],
                                      c["ident"][:])
                mm.then_inc(S["x_turned"], 1)

            def times_gate(s):
                for k in range(KT):
                    mm = pe.matmul(g_ps[:], xT[:, s, k, :], wg[:, s, k, :], start=k == 0, stop=k == KT - 1)
                mm.then_inc(S["gate_mm"], 1)

            def times_up(s):
                for k in range(KT):
                    mm = pe.matmul(u_ps[:], xT[:, s, k, :], wu[:, s, k, :], start=k == 0, stop=k == KT - 1)
                mm.then_inc(S["up_mm"], 1)

            def turn_hidden(b):
                pe.wait_ge(S["hid"], b + 1)
                for k in range(KD):
                    mm = pe.transpose(h_ps[:, k * P:(k + 1) * P], hid[:, k:DE:KD], c["ident"][:])
                mm.then_inc(S["h_turned"], 1)

            def times_down(b):
                pe.wait_ge(S["hT"], b * 2)
                pe.wait_ge(S["y_out"], b * 2)
                for half in range(2):
                    pe.wait_ge(S["w_lo"], b * 2 + half - 1)
                    cols = slice(half * 512, half * 512 + 512)
                    for k in range(KD):
                        dst = y_ps[:, half, :]
                        pe.matmul(dst, hT_hi[:, k, :], wd_hi[:, k, cols], start=k == 0, stop=False)
                        pe.matmul(dst, hT_hi[:, k, :], wd_lo[:, k, cols], start=False, stop=False)
                        mm = pe.matmul(dst, hT_lo[:, k, :], wd_hi[:, k, cols], start=False, stop=k == KD - 1)
                mm.then_inc(S["down_mm"], 1)

            pe.wait_ge(gathered[0], 16)
            turn_rows(0)
            pe.wait_ge(ld["g"][0], 16)
            pe.wait_ge(S["xT"], 1)
            times_gate(0)
            pe.wait_ge(ld["u"][0], 16)
            times_up(0)
            pe.wait_ge(gathered[1], 16)
            turn_rows(1)
            with pairs(pe, count) as i:
                for b, s in odd_and_even(i):
                    with pe.If(b < count):
                        pe.wait_ge(ld["g"][s], i * 16 + (16 if s else 32))
                        pe.wait_ge(S["xT"], b + 1)
                        pe.wait_ge(S["silu"], b + 1)
                        times_gate(s)
                        turn_hidden(b)
                        pe.wait_ge(ld["u"][s], i * 16 + (16 if s else 32))
                        times_up(s)
                        pe.wait_ge(gathered[1 - s], i * 16 + 32)
                        turn_rows(1 - s)
                        times_down(b)
                    with pe.If(b == count):
                        turn_hidden(b)
                        times_down(b)

        @block.scalar
        def _(act):
            count = act.value_load(rt["count"][0:1, 0:1], min_val=16, max_val=MAXB)
            act.sem_inc(S["silu"], 1)
            act.sem_inc(S["y_out"], 2)
            for s in range(2):
                act.sem_inc(stored[s], 16)

            def rows_out(s):
                act.activation(xT[:, s].rearrange("p k n -> p (k n)"), x_ps[:].rearrange("p a n -> p (a n)"),
                               ACT.Copy).then_inc(S["xT"], 1)

            def split_down(b, s, i):
                act.wait_ge(ld["d"][s], i * 16 + 16)
                act.wait_ge(S["down_mm"], b + 1)
                for half in range(2):
                    cols = slice(half * 512, half * 512 + 512)
                    act.activation(wd_hi[:, :, cols], wd[:, s, :, cols], ACT.Copy).then_inc(S["w_hi"], 1)

            def store(b, s, i):
                act.wait_ge(S["down_mm"], b + 2)
                act.wait_ge(stored[s], i * 16 + 16)
                act.activation(y[:, s, 0:512], y_ps[:, 0, :], ACT.Copy).then_inc(S["y_out"], 1)
                act.wait_ge(S["y_out"], b * 2 + 2)
                act.dma_start(y_blocks[bass.ds(b - 1, 1)].rearrange("o p d -> p (o d)"), y[:, s, :]
                              ).then_inc(stored[s], 16)

            act.wait_ge(S["x_turned"], 1)
            rows_out(0)
            act.wait_ge(S["gate_mm"], 1)
            act.activation(sg[:], g_ps[:], ACT.Silu).then_inc(S["silu"], 1)
            act.wait_ge(S["x_turned"], 2)
            rows_out(1)
            with pairs(act, count) as i:
                for b, s in odd_and_even(i):
                    with act.If(b < count + 1):
                        split_down(b, 1 - s, i)
                    with act.If(b < count):
                        act.wait_ge(S["gate_mm"], b + 1)
                        act.wait_ge(S["hid"], b + 1)
                        act.activation(sg[:], g_ps[:], ACT.Silu).then_inc(S["silu"], 1)
                        act.wait_ge(S["x_turned"], b + 2)
                        rows_out(1 - s)
                    with act.If(b < count + 1):
                        store(b, 1 - s, i)
            act.wait_ge(stored[0], 16 * ((count + 1) // 2) + 16)
            act.wait_ge(stored[1], 16 * (count // 2) + 16)
            act.activation(sg[:, 0:1], c["ones"][:, 0:1], ACT.Copy)

        @block.vector
        def _(dve):
            count = dve.value_load(rt["count"][0:1, 0:1], min_val=16, max_val=MAXB)
            dve.sem_inc(S["hid"], 1)
            dve.wait_ge(S["up_mm"], 3)
            dve.wait_ge(S["silu"], 2)
            dve.tensor_tensor(hid[:], sg[:], u_ps[:], ALU.mult).then_inc(S["hid"], 1)
            with pairs(dve, count) as i:
                for b, s in odd_and_even(i):
                    with dve.If(b < count + 1):
                        dve.wait_ge(S["h_turned"], b)
                        dve.wait_ge(S["down_mm"], b + 1)
                        hi, lo = (x[:].rearrange("p k n -> p (k n)") for x in (hT_hi, hT_lo))
                        dve.tensor_copy(hi, h_ps[:]).then_inc(S["hT"], 1)
                        dve.wait_ge(S["hT"], b * 2 - 1)
                        dve.tensor_tensor(lo, h_ps[:], hi.bitcast(F32), ALU.subtract).then_inc(S["hT"], 1)
                        for half in range(2):
                            cols = slice(half * 512, half * 512 + 512)
                            dve.wait_ge(S["w_hi"], b * 2 + half - 1)
                            dve.tensor_tensor(wd_lo[:, :, cols], wd[:, 1 - s, :, cols],
                                              wd_hi[:, :, cols].bitcast(F32), ALU.subtract).then_inc(S["w_lo"], 1)
                    with dve.If(b < count):
                        dve.wait_ge(S["up_mm"], b + 3)
                        dve.wait_ge(S["silu"], b + 2)
                        dve.tensor_tensor(hid[:], sg[:], u_ps[:], ALU.mult).then_inc(S["hid"], 1)
                    with dve.If(b < count + 1):
                        dve.wait_ge(S["down_mm"], b + 2)
                        dve.wait_ge(stored[1 - s], i * 16 + 16)
                        dve.tensor_copy(y[:, 1 - s, 512:], y_ps[:, 1, :]).then_inc(S["y_out"], 1)


def combine(nc, core, c, a, x1, rt, y_dram, out):
    rows = core.sb("expert_rows", [P, 4, 2, D])
    res = core.sb("result", [P, 2, D])
    sq = core.sb("cb_sq", [P, D])
    nf = core.sb("norm_final_row", [P, D])
    st = core.sb("cb_stats", [P, 4, TT])
    par = core.sem("cb_par")
    got = [[core.sem(f"cb_got{s}{k}") for k in range(2)] for s in range(4)]
    stored = [core.sem(f"cb_stored{s}") for s in range(2)]
    add, sqd, msd, rtd, rsd, res_s = (core.sem("cb_" + n) for n in "add sq ms rt rs res".split())
    out_rows = out.rearrange("b (t p) d -> p (b t) d", p=P)

    with nc.Block() as block:
        @block.gpsimd
        def _(pool):
            for t in range(TT):
                if t >= 4:
                    pool.wait_ge(add, 2 * (t - 3))
                for k in range(2):
                    pool.indirect_dma_start(out=rows[:, t % 4, k, :], out_offset=None, in_=y_dram,
                                            in_offset=bass.IndirectOffsetOnAxis(ap=rt["dest"][:, k, t:t + 1], axis=0)
                                            ).then_inc(got[t % 4][k], 16)

        @block.sync
        def _(sp):
            sp.dma_start(nf[:], a["norm_final"].rearrange("(o n) -> o n", o=1).partition_broadcast(P)
                         ).then_inc(par, 16)
            for t in range(TT):
                sp.wait_ge(res_s, t + 1)
                sp.dma_start(out_rows[:, t, :], res[:, t % 2, :]).then_inc(stored[t % 2], 16)
            for s in range(2):
                sp.wait_ge(stored[s], 16 * TT // 2)

        @block.vector
        def _(dve):
            def norm(t):
                dve.wait_ge(sqd, t + 1)
                dve.tensor_scalar(st[:, 1, t:t + 1], st[:, 0, t:t + 1], 1.0 / D, EPS, ALU.mult, ALU.add
                                  ).then_inc(msd, 1)
                dve.wait_ge(rtd, t + 1)
                dve.reciprocal(st[:, 3, t:t + 1], st[:, 2, t:t + 1]).then_inc(rsd, 1)
                dve.wait_ge(rsd, t + 1)
                if t >= 2:
                    dve.wait_ge(stored[t % 2], 16 * (t // 2))
                dve.scalar_tensor_tensor(out=res[:, t % 2, :], in0=x1[:, t, :], scalar=st[:, 3, t:t + 1],
                                         in1=nf[:], op0=ALU.mult, op1=ALU.mult).then_inc(res_s, 1)

            dve.wait_ge(par, 16)
            for t in range(TT):
                for k in range(2):
                    dve.wait_ge(got[t % 4][k], 16 * (t // 4 + 1))
                    if k:
                        dve.wait_ge(add, 2 * t + 1)
                    dve.scalar_tensor_tensor(out=x1[:, t, :], in0=rows[:, t % 4, k, :],
                                             scalar=rt["gate"][:, k, t:t + 1], in1=x1[:, t, :],
                                             op0=ALU.mult, op1=ALU.add).then_inc(add, 1)
                if t:
                    norm(t - 1)
            norm(TT - 1)

        @block.scalar
        def _(act):
            for t in range(TT):
                act.wait_ge(add, 2 * (t + 1))
                if t:
                    act.wait_ge(sqd, t)
                act.activation(sq[:], x1[:, t, :], ACT.Square, accum_out=st[:, 0, t:t + 1]).then_inc(sqd, 1)
                act.wait_ge(msd, t + 1)
                act.activation(st[:, 2, t:t + 1], st[:, 1, t:t + 1], ACT.Sqrt).then_inc(rtd, 1)


def hybrid_encoder(nc, a, out):
    h_dram = nc.dram_tensor("h_rows", [L, D], F32).ap()
    s5_dram = nc.dram_tensor("s5_factors", [P, COOKED_COLS], F32).ap()
    y_dram = nc.dram_tensor("expert_rows_dram", [(MAXB + 1) * P, D], F32).ap()
    with ExitStack() as whole:
        core = Core(nc, whole)
        c = constants(core)
        filled = core.sem("expert_rows_filled")
        with ExitStack() as late:
            lc = Core(nc, late)
            with ExitStack() as mixers:
                mc = Core(nc, mixers)
                with ExitStack() as pre:
                    pc = Core(nc, pre)
                    cooked_ld = pc.sem("s5_cooked_ld")
                    with ExitStack() as st:
                        dc = Core(nc, st)
                        o = persistent(mc, dc)
                        c["level"] = [dc.sb("level_f", [P, 7, P]), dc.sb("level_b", [P, 7, P])]
                        tb = gate_tables(dc)
                        with ExitStack() as s:
                            in_projection(nc, Core(nc, s), c, a, o, tb, y_dram, filled, s5_dram)
                        o_sum = dc.sb("o_sum", [P, TT, DW])
                        with ExitStack() as s:
                            delta_net(nc, Core(nc, s), c, a, o, tb, o_sum)
                        ydn = o["qT"]
                        x1 = lc.sb("x1", [P, TT, D], side="right")
                        logits = lc.sb("logits", [P, TT, NGRP + NEXP], side="right")
                        cooked = pc.sb("s5_cooked", [P, COOKED_COLS], side="right")
                        with ExitStack() as s:
                            gated_norm(nc, Core(nc, s), c, a, o_sum, o["zs"], ydn, s5_dram, cooked, cooked_ld)
                    ys5 = o["uT"][:].rearrange("p (k g) n -> p k (g n)", k=4)
                    gw = mc.sb("s5_G_or_w_out", [P, 2 * 2 * NP5 * (T5 + 1) * GC])
                    G = gw[:].rearrange("p (i j k q) -> p i j k q", i=2, k=T5 + 1, q=GC)
                    wo = gw[:, 0:KT * D].rearrange("p (k n) -> p k n", k=KT)
                    sq = gw[:, KT * D:]
                    next_ld = {n: mc.sem("next_ld_" + n) for n in "wx"}
                    with ExitStack() as s:
                        s5_mixer(nc, Core(nc, s), c, a, cooked, cooked_ld, o["uT"], ys5, G, x1, wo, next_ld)
                with ExitStack() as s:
                    out_projection(nc, Core(nc, s), c, a, ys5, ydn, x1, wo, sq, next_ld, logits, h_dram, filled)
            rt = router_tables(lc)
            with ExitStack() as moe:
                ec = Core(nc, moe)
                wg, wu = ec.sb("w_gate", [P, 2, KT, DE]), ec.sb("w_up", [P, 2, KT, DE])
                early = ec.sem("expert_0_ld")
                with ExitStack() as s:
                    router(nc, Core(nc, s), c, a, logits, rt, wg, wu, early)
                with ExitStack() as s:
                    experts(nc, Core(nc, s), c, a, rt, h_dram, y_dram, wg, wu, early)
            with ExitStack() as s:
                combine(nc, Core(nc, s), c, a, x1, rt, y_dram, out)


_INS = ["x", "norm_mix", "w_in", "s5_lam_re", "s5_lam_im", "s5_log_dt", "s5_b_re", "s5_b_im", "s5_c_re", "s5_c_im",
        "s5_d", "s5_w_glu", "s5_b_glu", "gdn_conv_w", "gdn_a_log", "gdn_dt_bias", "gdn_norm_w", "w_out", "norm_ffn",
        "router_w_group", "router_b_group", "router_w_expert", "router_b_expert",
        "expert_w_gate", "expert_w_up", "expert_w_down", "norm_final"]


def kernel(**inputs):
    import numpy as np
    import concourse.bacc as bacc
    from concourse.bass_utils import run_bass_kernel_spmd

    nc = bacc.Bacc("TRN2", target_bir_lowering=False, num_devices=1)
    arrays, aps = {}, {}
    for name in _INS:
        arr = np.ascontiguousarray(inputs[name])
        arrays[f"in_{name}"] = arr
        aps[name] = nc.dram_tensor(f"in_{name}", arr.shape, mybir.dt.from_np(arr.dtype), kind="ExternalInput").ap()
    out = nc.dram_tensor("out", (1, L, D), F32, kind="ExternalOutput").ap()
    hybrid_encoder(nc, aps, out)
    r = run_bass_kernel_spmd(nc, [arrays], core_ids=[0])
    return r.results[0]["out"]
```
